# Optimizing a Trainium2 kernel written in Bass

```python
import jax, jax.numpy as jnp
from jax import lax
import numpy as np

D_MODEL = 1024
BATCH = 1
SEQ = 256
DEPTH = 1
DEC_BATCH = 1
DEC_SEQ = 64
PAST_LEN = 512

CHUNK = 64
HEAD_DIM = 64
MIX_DIM = D_MODEL
ATT_DIM = MIX_DIM // 2
N_HEADS = ATT_DIM // HEAD_DIM
N_KV_HEADS = max(1, N_HEADS // 4)
Q_PER_KV = N_HEADS // N_KV_HEADS
KV_DIM = N_KV_HEADS * HEAD_DIM
CONV_DIM = MIX_DIM - ATT_DIM
CONV_W = 3
WINDOW = 128
WIN_CHUNKS = WINDOW // CHUNK
IN_DIM = ATT_DIM + 2 * KV_DIM + 3 * CONV_DIM
SPLITS = (ATT_DIM, ATT_DIM + KV_DIM, ATT_DIM + 2 * KV_DIM,
          ATT_DIM + 2 * KV_DIM + CONV_DIM, ATT_DIM + 2 * KV_DIM + 2 * CONV_DIM)
N_EXPERTS = 32
TOP_K = 4
D_FF = D_MODEL
SWIGLU_LIMIT = 7.0
SWIGLU_ALPHA = 1.702
ROW_BLOCK = 128
EPS = 1e-6
NEG = -1e30

kernel_name = 'hybrid_swa_sink_shortconv_moe_stream_step'

def _rms(x, g):
    xf = x.astype(jnp.float32)
    y = xf * lax.rsqrt(jnp.mean(xf * xf, axis=-1, keepdims=True) + EPS)
    return (y * g.astype(jnp.float32)).astype(x.dtype)

def _project(xn, w_in, q_g, k_g):
    q, k, v, bg, cg, hc = jnp.split(xn @ w_in, SPLITS, axis=-1)
    lead = xn.shape[:-1]
    q = _rms(q.reshape(*lead, N_HEADS, HEAD_DIM), q_g)
    k = _rms(k.reshape(*lead, N_KV_HEADS, HEAD_DIM), k_g)
    v = v.reshape(*lead, N_KV_HEADS, HEAD_DIM)
    return q, k, v, bg, cg * hc

def _sink_attention(q, k, v, key_valid, sinks):
    s = jnp.einsum('...qhgd,...khd->...hgqk', q, k).astype(jnp.float32) * (HEAD_DIM ** -0.5)
    if key_valid is not None:
        s = jnp.where(key_valid[..., None, None, None, :], s, NEG)
    sink = jnp.broadcast_to(sinks.astype(jnp.float32).reshape(N_KV_HEADS, Q_PER_KV, 1, 1),
                            s.shape[:-1] + (1,))
    p = jax.nn.softmax(jnp.concatenate([s, sink], axis=-1), axis=-1)[..., :-1]
    return jnp.einsum('...hgqk,...khd->...qhgd', p.astype(v.dtype), v)

def _window_attention_prompt(q, k, v, sinks):
    b, s = q.shape[0], q.shape[1]
    nc = s // CHUNK
    qb = q.reshape(b, nc, CHUNK, N_KV_HEADS, Q_PER_KV, HEAD_DIM)

    def band(t):
        tc = jnp.pad(t, ((0, 0), (WINDOW, 0), (0, 0), (0, 0))).reshape(
            b, nc + WIN_CHUNKS, CHUNK, N_KV_HEADS, HEAD_DIM)
        return jnp.concatenate([tc[:, i:i + nc] for i in range(WIN_CHUNKS + 1)], axis=2)

    key_pos = (jnp.arange(nc)[:, None] * CHUNK - WINDOW
               + jnp.arange((WIN_CHUNKS + 1) * CHUNK)[None, :])
    o = _sink_attention(qb, band(k), band(v), key_pos >= 0, sinks)
    return o.reshape(b, s, ATT_DIM)

def _window_attention_sample(q, k_ctx, v_ctx, sinks):
    b, s = q.shape[0], q.shape[1]
    qb = q.reshape(b, s, N_KV_HEADS, Q_PER_KV, HEAD_DIM)
    o = _sink_attention(qb, k_ctx, v_ctx, None, sinks)
    return o.reshape(b, s, ATT_DIM)

def _causal_conv(u_ctx, w):
    n = u_ctx.shape[1] - (CONV_W - 1)
    y = u_ctx[:, 0:n] * w[0]
    for j in range(1, CONV_W):
        y = y + u_ctx[:, j:j + n] * w[j]
    return y

def _moe(x2d, w_router, b_router, w_gu, b_gu, w_down, b_down):
    t, d = x2d.shape
    logits = (x2d @ w_router).astype(jnp.float32) + b_router.astype(jnp.float32)
    top_logits, top_idx = lax.top_k(logits, TOP_K)
    gates = jax.nn.softmax(top_logits, axis=-1)
    tk = t * TOP_K
    flat_e = top_idx.reshape(tk)
    order = jnp.argsort(flat_e, stable=True)
    sorted_e = flat_e[order]
    counts = jnp.bincount(flat_e, length=N_EXPERTS)
    padded = (counts + ROW_BLOCK - 1) // ROW_BLOCK * ROW_BLOCK
    pad_ends = jnp.cumsum(padded)
    pad_starts = pad_ends - padded
    starts = jnp.cumsum(counts) - counts
    dest = pad_starts[sorted_e] + (jnp.arange(tk) - starts[sorted_e])
    n_blocks = -(-tk // ROW_BLOCK) + N_EXPERTS
    rows = n_blocks * ROW_BLOCK
    row_token = jnp.zeros((rows,), jnp.int32).at[dest].set((order // TOP_K).astype(jnp.int32))
    row_gate = jnp.zeros((rows,), jnp.float32).at[dest].set(gates.reshape(tk)[order])
    block_e = jnp.minimum(jnp.searchsorted(pad_ends, jnp.arange(n_blocks) * ROW_BLOCK, side='right'),
                          N_EXPERTS - 1)
    xb = x2d[row_token].reshape(n_blocks, ROW_BLOCK, d)

    def expert_block(args):
        xe, e = args
        gu = xe @ w_gu[e] + b_gu[e]
        g, u = gu[:, :D_FF], gu[:, D_FF:]
        g = jnp.minimum(g, SWIGLU_LIMIT)
        u = jnp.clip(u, -SWIGLU_LIMIT, SWIGLU_LIMIT)
        h = (u + 1) * (g * jax.nn.sigmoid(SWIGLU_ALPHA * g))
        return h @ w_down[e] + b_down[e]

    yb = lax.map(expert_block, (xb, block_e))
    yrows = yb.reshape(rows, d) * row_gate[:, None].astype(yb.dtype)
    return jnp.zeros_like(x2d).at[row_token].add(yrows)

def _merge_and_ffn(x, att, conv_out, w_out, norm2_g, w_router, b_router, w_gu, b_gu, w_down, b_down):
    h = x + jnp.concatenate([att, conv_out], axis=-1) @ w_out
    hn = _rms(h, norm2_g)
    ff = _moe(hn.reshape(-1, D_MODEL), w_router, b_router, w_gu, b_gu, w_down, b_down)
    return h + ff.reshape(h.shape)

def setup_inputs(seed: int = 0) -> dict:
    key = jax.random.key(seed)
    ks = jax.random.split(key, 19)
    win_cache = min(WINDOW, PAST_LEN)

    def nrm(k, shape, scale=1.0):
        return jax.random.normal(k, shape, jnp.float32) * scale

    return {
        'x_prompt': nrm(ks[0], (BATCH, SEQ, D_MODEL)),
        'x_sample': nrm(ks[1], (DEC_BATCH, DEC_SEQ, D_MODEL)),
        'cache_k': nrm(ks[2], (DEPTH, DEC_BATCH, win_cache, N_KV_HEADS, HEAD_DIM)),
        'cache_v': nrm(ks[3], (DEPTH, DEC_BATCH, win_cache, N_KV_HEADS, HEAD_DIM)),
        'state_conv': nrm(ks[4], (DEPTH, DEC_BATCH, CONV_W - 1, CONV_DIM)),
        'norm1_g': 1.0 + nrm(ks[5], (DEPTH, D_MODEL), 0.1),
        'w_in': nrm(ks[6], (DEPTH, D_MODEL, IN_DIM), D_MODEL ** -0.5),
        'q_norm_g': 1.0 + nrm(ks[7], (DEPTH, HEAD_DIM), 0.1),
        'k_norm_g': 1.0 + nrm(ks[8], (DEPTH, HEAD_DIM), 0.1),
        'sinks': nrm(ks[9], (DEPTH, N_HEADS), 1.0),
        'conv_w': nrm(ks[10], (DEPTH, CONV_W, CONV_DIM), CONV_W ** -0.5),
        'w_out': nrm(ks[11], (DEPTH, MIX_DIM, D_MODEL), MIX_DIM ** -0.5),
        'norm2_g': 1.0 + nrm(ks[12], (DEPTH, D_MODEL), 0.1),
        'w_router': nrm(ks[13], (DEPTH, D_MODEL, N_EXPERTS), D_MODEL ** -0.5),
        'b_router': nrm(ks[14], (DEPTH, N_EXPERTS), 0.01),
        'w_gu': nrm(ks[15], (DEPTH, N_EXPERTS, D_MODEL, 2 * D_FF), D_MODEL ** -0.5),
        'b_gu': nrm(ks[16], (DEPTH, N_EXPERTS, 2 * D_FF), 0.01),
        'w_down': nrm(ks[17], (DEPTH, N_EXPERTS, D_FF, D_MODEL), D_FF ** -0.5),
        'b_down': nrm(ks[18], (DEPTH, N_EXPERTS, D_MODEL), 0.01),
    }

def reference(x_prompt, x_sample, cache_k, cache_v, state_conv, norm1_g, w_in, q_norm_g, k_norm_g,
              sinks, conv_w, w_out, norm2_g, w_router, b_router, w_gu, b_gu, w_down, b_down):
    win_cache = cache_k.shape[2]
    hp, hs = x_prompt, x_sample
    kp_l, vp_l, cp_l, ks_l, vs_l, cs_l = [], [], [], [], [], []
    for l in range(DEPTH):
        moe_w = (w_router[l], b_router[l], w_gu[l], b_gu[l], w_down[l], b_down[l])
        q, k, v, bg, u = _project(_rms(hp, norm1_g[l]), w_in[l], q_norm_g[l], k_norm_g[l])
        att = _window_attention_prompt(q, k, v, sinks[l])
        cv = _causal_conv(jnp.pad(u, ((0, 0), (CONV_W - 1, 0), (0, 0))), conv_w[l])
        hp = _merge_and_ffn(hp, att, bg * cv, w_out[l], norm2_g[l], *moe_w)
        kp_l.append(k[:, -WINDOW:])
        vp_l.append(v[:, -WINDOW:])
        cp_l.append(u[:, -(CONV_W - 1):])
        q, k, v, bg, u = _project(_rms(hs, norm1_g[l]), w_in[l], q_norm_g[l], k_norm_g[l])
        k_ctx = jnp.concatenate([cache_k[l], k], axis=1)
        v_ctx = jnp.concatenate([cache_v[l], v], axis=1)
        att = _window_attention_sample(q, k_ctx, v_ctx, sinks[l])
        u_ctx = jnp.concatenate([state_conv[l], u], axis=1)
        cv = _causal_conv(u_ctx, conv_w[l])
        hs = _merge_and_ffn(hs, att, bg * cv, w_out[l], norm2_g[l], *moe_w)
        ks_l.append(k_ctx[:, -win_cache:])
        vs_l.append(v_ctx[:, -win_cache:])
        cs_l.append(u_ctx[:, -(CONV_W - 1):])
    return (hp, hs, jnp.stack(kp_l), jnp.stack(vp_l), jnp.stack(cp_l),
            jnp.stack(ks_l), jnp.stack(vs_l), jnp.stack(cs_l))


_drawn_inputs = setup_inputs


def setup_inputs(seed=0):
    import zlib

    import numpy as np

    out = dict(_drawn_inputs(seed))
    spreads = {}
    factors = {'q_norm_g': 2.719, 'sinks': 8.0, 'b_gu': 8.0, 'b_down': 8.0}
    for name, (base, spread) in spreads.items():
        noise = np.random.default_rng([zlib.crc32(name.encode()), seed]).standard_normal(out[name].shape)
        drawn = base * np.exp(spread * noise) if base else spread * noise
        out[name] = __import__('jax').numpy.asarray(drawn.astype(out[name].dtype))
    for name, factor in factors.items():
        out[name] = (out[name] * factor).astype(out[name].dtype)
    return out
```

```python
from contextlib import ExitStack

import concourse.bass as bass
from concourse import mybir

ALU = mybir.AluOpType
ACT = mybir.ActivationFunctionType
AX = mybir.AxisListType
F32 = mybir.dt.float32
I32 = mybir.dt.int32

P = 128
CHUNK = 64
HEAD_DIM = 64
TOP_K = 4
EPS = 1e-6
LIMIT = 7.0
ALPHA = 1.702
CAP = 64
NO_LOGIT = 3.0e38


def hybrid_layer_kernel(nc, x_prompt, x_sample, cache_k, cache_v, state_conv, norm1_g, w_in, q_norm_g,
                        k_norm_g, sinks, conv_w, w_out, norm2_g, w_router, b_router, w_gu, b_gu,
                        w_down, b_down, y_prompt, y_sample, new_k_prompt, new_v_prompt,
                        new_conv_prompt, new_k_sample, new_v_sample, new_conv_sample):
    SEQ, D = x_prompt.shape[1:]
    DEC = x_sample.shape[1]
    IN_DIM = w_in.shape[2]
    NH = sinks.shape[1]
    NKV = cache_k.shape[3]
    KV = NKV * HEAD_DIM
    ATT = NH * HEAD_DIM
    CONV = conv_w.shape[2]
    CW = conv_w.shape[1]
    WIN = cache_k.shape[2]
    NE = w_router.shape[2]
    FF = w_down.shape[2]
    KT = D // P
    FT = FF // P
    CT = CONV // P
    TOK = SEQ + DEC
    NT = 3
    TT = [(0, P), (P, P), (2 * P, DEC)]
    HALF = D // 2
    QT = ATT // P
    NCH = TOK // CHUNK
    SAMPLE = NCH - 1
    MIX = (ATT + CONV) // P
    QKV = ATT + 2 * KV
    PAIRS = NE // 2
    ROUNDS = -(-TOK // CAP)
    ROWS = 2 * CAP
    assert (SEQ, DEC, CHUNK, WIN, KV, NKV, HALF, QT, FT * CAP) == (256, 64, 64, 128, 128, 2, 512, 4, FT * CAP)
    assert FT * CAP <= 512 and KT == FT and 2 * FT * P == 2048

    ctx = ExitStack()
    with ctx:
        def sb(name, shape, dt=F32):
            return ctx.enter_context(nc.sbuf_tensor(name, shape, dt))

        def sem(name):
            return ctx.enter_context(nc.semaphore(name))

        ps = ctx.enter_context(nc.psum_tensor("ps", [P, 8, 512], F32))

        gu_ring = sb("gu_ring", [P, KT, 2 * FF])
        dn_ring = sb("dn_ring", [P, FT // 2, 2, D])
        w_qkv = sb("w_qkv", [P, KT, QKV])
        w_bch = gu_ring[:, 2:KT, :].rearrange("p s f -> p (s f)").rearrange("p (k n) -> p k n", k=KT)
        w_o = dn_ring[:, :, :, :].rearrange("p a b n -> p (a b) n")

        late_used = [0]

        def late(*shape):
            size = 1
            for d in shape:
                size *= d
            at = late_used[0]
            late_used[0] += size
            assert late_used[0] <= KT * QKV
            flat = w_qkv[:, :, :].rearrange("p k n -> p (k n)")[:, at:at + size]
            names = " ".join("abcd"[:len(shape)])
            return flat.rearrange(f"p ({names}) -> p {names}", **dict(zip("abcd", shape))) if len(shape) > 1 else flat

        w_rt = late(KT, NE)
        g2 = late(D)

        ident = sb("ident", [P, P])
        ones = sb("ones", [P, P])
        before = sb("before", [P, P])
        head_ones = sb("head_ones", [P, P])
        row_ids = sb("row_ids", [P, CAP])
        eps = sb("eps", [P, 1])
        V_G1, V_CONV, V_QG, V_KG = 0, KT, KT + CW * CT, KT + CW * CT + 1
        V_STATE = V_KG + 1
        NV = V_STATE + (CW - 1) * CT
        vec_rows = sb("vec_rows", [NV, P])
        vec = sb("vec", [P, NV])
        sink_row = sb("sink_row", [P, NH])
        sink = sb("sink", [P, NH // 2])
        b_rt = sb("b_rt", [P, NE])
        bias_rows = dn_ring[0:NE, 2:4].rearrange("p m a n -> p (m a n)")[:, 0:2 * FF + D]
        b_guT = sb("b_guT", [P, 2 * FT, NE])
        b_dnT = sb("b_dnT", [P, KT, NE])

        x = sb("x", [P, NT, D])
        hn = sb("hn", [P, NT, D])
        xnT = sb("xnT", [P, KT, TOK])
        mixT = sb("mixT", [P, MIX, TOK])
        qk_sq = sb("qk_sq", [P, 1 + QT, TOK])
        kT = sb("kT", [P, TOK])
        qT = sb("qT", [P, NCH, NH // NKV, CHUNK])
        v_nat = sb("v_nat", [P, NT, KV])
        ck_nat = sb("ck_nat", [P, KV])
        ckT = sb("ckT", [P, P])
        cv_nat = sb("cv_nat", [P, KV])
        k_out = sb("k_out", [P, 2, KV])
        UW = SEQ + DEC + 2 * (CW - 1)
        uT = sb("uT", [P, CT, UW])
        c_sb = sb("c_sb", [P, TOK])
        qk_room = qk_sq[:, :, :].rearrange("p a t -> p (a t)")
        cv = qk_room[:, 4 * 256:4 * 256 + UW - (CW - 1)]
        probs = qk_room[:, 0:4 * 256].rearrange("p (b k) -> p b k", b=4)
        probsT = sb("probsT", [P, 2, 512])
        u_out = probsT[0:CW - 1, :, :]
        smx = sb("smx", [P, 8, 4])
        st = sb("st", [P, 4, NT])

        lg = sb("lg", [P, NT, NE])
        top8 = sb("top8", [P, NT, 8])
        top4 = sb("top4", [P, NT, 8])
        left = sb("left", [P, NT, NE])
        sel = sb("sel", [P, NT, NE])
        neg_top = sb("neg_top", [P, NT])
        gates = sb("gates", [P, NT, NE])
        gsum = sb("gsum", [P, NT])
        rank = sb("rank", [P, NT, NE])
        counts = sb("counts", [P, NE], I32)
        most = sb("most", [P, 1])
        most_i = sb("most_i", [P, 1], I32)

        onehot = late(2, NT, CAP)
        gated = late(NT, 2, CAP)
        scat = late(NT * P)
        xe = late(2, KT, CAP)
        ge = late(FT, CAP)
        ue = late(FT, CAP)
        sg = late(FT, CAP)
        he = late(2, FT, CAP)
        yeT = sb("yeT", [P, KT, 2, CAP])
        ye = sb("ye", [P, D])
        hnT = ye[:, :].rearrange("p (k t) -> p k t", k=KT)
        junk = yeT[:, :, :, :].rearrange("p k a c -> p (k a c)")

        x_in = [sem(f"x_in{t}") for t in range(2)]
        wqkv_in, wch_in, wb_in, wo_in = sem("wqkv_in"), sem("wch_in"), sem("wb_in"), sem("wo_in")
        vec_in, bias_in, cache_in, bcast_in, wrt_in = (sem(n) for n in (
            "vec_in", "bias_in", "cache_in", "bcast_in", "wrt_in"))
        gu_in = [sem(f"gu_in{k}") for k in range(KT)]
        dn_in = [sem(f"dn_in{m}") for m in range(FT // 2)]
        kv_stored = sem("kv_stored")
        y_stored = sem("y_stored")
        zeroed, consts, eps_set, heads_set = sem("zeroed"), sem("consts"), sem("eps_set"), sem("heads_set")
        router_set, conv_pad = sem("router_set"), sem("conv_pad")
        x_sumsq, x_std, x_rstd, x_scaled = (sem(n) for n in ("x_sumsq", "x_std", "x_rstd", "x_scaled"))
        vec_turned, vec_ready = sem("vec_turned"), sem("vec_ready")
        bias_turned, bias_ready = sem("bias_turned"), sem("bias_ready")
        x_turned, xnT_ready = sem("x_turned"), sem("xnT_ready")
        qk_done, qk_squared, head_ss, head_std, head_rstd, qk_ready = (sem(n) for n in (
            "qk_done", "qk_squared", "head_ss", "head_std", "head_rstd", "qk_ready"))
        v_done, v_ready = sem("v_done"), sem("v_ready")
        bch_done, c_copied, u_ready, cv_step, conv_mixed = (sem(n) for n in (
            "bch_done", "c_copied", "u_ready", "cv_step", "conv_mixed"))
        sink_set, scores_done, smx_step, smx_neg, exp_done, probs_ready = (sem(n) for n in (
            "sink_set", "scores_done", "smx_step", "smx_neg", "exp_done", "probs_ready"))
        probs_turned, probsT_ready, att_done, att_mixed = (sem(n) for n in (
            "probs_turned", "probsT_ready", "att_done", "att_mixed"))
        k_turned, k_out_ready, u_turned, u_out_ready = (sem(n) for n in (
            "k_turned", "k_out_ready", "u_turned", "u_out_ready"))
        out_done, h_ready, h_sumsq, h_std, h_rstd, hn_ready = (sem(n) for n in (
            "out_done", "h_ready", "h_sumsq", "h_std", "h_rstd", "hn_ready"))
        hn_turned, hnT_ready, logits_done = sem("hn_turned"), sem("hnT_ready"), sem("logits_done")
        route, top_ready, gexp_done, sel_ready, ranked, rank_ready = (sem(n) for n in (
            "route", "top_ready", "gexp_done", "sel_ready", "ranked", "rank_ready"))
        counts_ready = sem("counts_ready")
        onehot_ready, gated_ready, gathered, xe_ready = (sem(n) for n in (
            "onehot_ready", "gated_ready", "gathered", "xe_ready"))
        gu_used, dn_used = sem("gu_used"), sem("dn_used")
        g_biased, g_ready, u_biased, u_clipped, sig_ready, gs_ready, he_ready = (sem(n) for n in (
            "g_biased", "g_ready", "u_biased", "u_clipped", "sig_ready", "gs_ready", "he_ready"))
        yeT_ready, y_turned, ye_ready, scat_turned, scat_ready = (sem(n) for n in (
            "yeT_ready", "y_turned", "ye_ready", "scat_turned", "scat_ready"))
        scattered, added = sem("scattered"), sem("added")
        rows_moved = sem("rows_moved")
        y_ready, second_zero = sem("y_ready"), sem("second_zero")

        B_VEC = 5
        XT_BANK = [(0, 1), (2, 3), (4,)]
        QK_BANK = [3, 4, 5, 0, 1]
        V_BANK = 2
        SS_BANK = [6, 7]
        BCH_BANK = [3, 4, 5]
        SC = ps[:, 6:8, :].rearrange("p a (b k) -> p (a b) k", b=2)
        PT = ps[:, 0:2, :]
        AO = ps[:, 2, 0:256]
        KO = ps[:, 2, 256:512].rearrange("p (a n) -> p a n", a=2)
        OUT_BANK = [(3, 4), (5, 6), (7, 2)]
        LG = ps[:, 3:3 + NT, 0:NE]
        RK = ps[:, 6, 0:(NT + 1) * NE].rearrange("p (t e) -> p t e", t=NT + 1)
        GU = [ps[:, 0:2, 0:FT * CAP], ps[:, 2:4, 0:FT * CAP]]
        YT = ps[:, 4, 0:KT * CAP].rearrange("p (k c) -> p k c", k=KT)
        XE = ps[:, 5, 0:KT * CAP].rearrange("p (k c) -> p k c", k=KT)
        ST = ps[:, 5, 0:NT * P]
        YN = ps[:, 6:8, :].rearrange("p a n -> p (a n)")

        gu_dram = w_gu.rearrange("l e (k p) f -> (l e) k p f", p=P)
        dn_dram = w_down.rearrange("l e (m a p) n -> (l e) m p a n", a=2, p=P)
        in_dram = w_in.rearrange("l (k p) n -> p (l k) n", p=P)
        FIRST_FREE = 2

        def key_window(c):
            if c == SAMPLE:
                return 0, WIN + DEC
            first = max(0, c - WIN // CHUNK)
            return (first % 2) * CHUNK, (c + 1 - first) * CHUNK

        def further_rounds(eng, step, each_round=None):
            eng.wait_ge(counts_ready, 2)
            top = eng.value_load(most_i[0:1, 0:1], min_val=0, max_val=TOK)
            with eng.If(top > CAP):
                n_reg = eng.alloc_register("n_block_" + str(eng.engine).split(".")[-1])
                eng.reg_mov(n_reg, NE)
                with eng.Fori(1, ROUNDS) as q:
                    if each_round:
                        each_round(q)
                    with eng.Fori(0, NE) as e:
                        have = eng.value_load(counts[0:1, bass.ds(e, 1)], min_val=0, max_val=TOK)
                        with eng.If(have > q * CAP):
                            n = eng.snap(n_reg, min_val=NE, max_val=NE * ROUNDS)
                            step(n, e)
                            eng.reg_add(n_reg, n_reg, 1)

        block = ctx.enter_context(nc.Block())

        @block.sync
        def _(sp):
            def load_gu(n, e, k, first=False):
                if not first:
                    sp.wait_ge(gu_used, KT * (n - 1) + k + 1)
                sp.dma_start(gu_ring[:, k, :], gu_dram[e, k]).then_inc(gu_in[k], 16)

            def load_dn(n, e, m, first=False):
                if not first:
                    sp.wait_ge(dn_used, (FT // 2) * (n - 1) + m + 1)
                sp.dma_start(dn_ring[:, m], dn_dram[e, m]).then_inc(dn_in[m], 16)

            sp.dma_start(x[:, 0:2, :], x_prompt.rearrange("b (t p) d -> p (b t) d", p=P)).then_inc(x_in[0], 16)
            sp.dma_start(x[0:DEC, 2, :], x_sample[0]).then_inc(x_in[1], 16)
            sp.dma_start(w_qkv[:, :, :], in_dram[:, :, 0:QKV]).then_inc(wqkv_in, 16)
            sp.dma_start(w_bch[:, :, CONV:3 * CONV], in_dram[:, :, QKV + CONV:IN_DIM]).then_inc(wch_in, 16)
            sp.dma_start(w_bch[:, :, 0:CONV], in_dram[:, :, QKV:QKV + CONV]).then_inc(wb_in, 16)
            sp.wait_ge(bias_turned, 1)
            for g in range(2):
                sp.dma_start(w_o[g * HEAD_DIM:(g + 1) * HEAD_DIM, 0:QT, :],
                             w_out[0, g * ATT // 2:(g + 1) * ATT // 2, :].rearrange("(j p) n -> p j n", p=HEAD_DIM)
                             ).then_inc(wo_in, 16)
            sp.dma_start(w_o[:, QT:MIX, :],
                         w_out[0, ATT:ATT + CONV, :].rearrange("(j p) n -> p j n", p=P)).then_inc(wo_in, 16)
            for k in range(FIRST_FREE):
                load_gu(0, 0, k, first=True)
            sp.wait_ge(bch_done, 3 * CT)
            for k in range(FIRST_FREE, KT):
                load_gu(0, 0, k, first=True)
            for k in range(KT):
                load_gu(1, 1, k)
            sp.wait_ge(out_done, 2 * NT)
            for m in range(FT // 2):
                load_dn(0, 0, m, first=True)
            with sp.Fori(2, NE) as e:
                for k in range(KT):
                    load_gu(e, e, k)
                for m in range(FT // 2):
                    load_dn(e - 1, e - 1, m)
            for m in range(FT // 2):
                load_dn(NE - 1, NE - 1, m)

            def again(n, e):
                for k in range(KT):
                    load_gu(n, e, k)
                for m in range(FT // 2):
                    load_dn(n, e, m)

            further_rounds(sp, again)

            sp.wait_ge(y_ready, 1)
            sp.dma_start(y_prompt.rearrange("b (t p) d -> p (b t) d", p=P), x[:, 0:2, :]).then_inc(y_stored, 16)
            sp.dma_start(y_sample[0], x[0:DEC, 2, :]).then_inc(y_stored, 16)
            sp.wait_ge(y_stored, 32)
            sp.wait_ge(kv_stored, 8 * 16)

        @block.gpsimd
        def _(pool):
            rows = vec_rows
            pool.dma_start(rows[V_G1:V_G1 + KT, :], norm1_g.rearrange("l (k p) -> (l k) p", p=P)).then_inc(vec_in, 16)
            pool.dma_start(rows[V_CONV:V_CONV + CW * CT, :],
                           conv_w.rearrange("l w (c p) -> (l w c) p", p=P)).then_inc(vec_in, 16)
            for g in range(2):
                half = slice(g * HEAD_DIM, (g + 1) * HEAD_DIM)
                pool.dma_start(rows[V_QG:V_QG + 1, half], q_norm_g).then_inc(vec_in, 16)
                pool.dma_start(rows[V_KG:V_KG + 1, half], k_norm_g).then_inc(vec_in, 16)
            pool.dma_start(rows[V_STATE:NV, :],
                           state_conv.rearrange("l b r (c p) -> (l b r c) p", p=P)).then_inc(vec_in, 16)
            pool.dma_start(ck_nat[:, :], cache_k[0, 0].rearrange("t h d -> t (h d)")).then_inc(cache_in, 16)
            pool.memset(ident[:, :], 0.0).then_inc(zeroed, 1)
            pool.memset(ones[:, :], 1.0).then_inc(zeroed, 1)
            pool.wait_ge(zeroed, 2)
            pool.affine_select(out=ident[:, :], in_=ident[:, :], compare_op=ALU.not_equal, fill=1.0,
                               base=0, pattern=[[-1, P]], channel_multiplier=1).then_inc(consts, 1)
            pool.affine_select(out=before[:, :], in_=ones[:, :], compare_op=ALU.is_gt, fill=0.0,
                               base=0, pattern=[[1, P]], channel_multiplier=-1).then_inc(consts, 1)
            pool.iota(row_ids[:, :], pattern=[[1, CAP]], base=0, channel_multiplier=0,
                      allow_small_or_imprecise_dtypes=True).then_inc(consts, 1)
            pool.dma_start(bias_rows[:, 0:2 * FF], b_gu[0]).then_inc(bias_in, 16)
            pool.dma_start(bias_rows[:, 2 * FF:], b_down[0]).then_inc(bias_in, 16)
            pool.dma_start(sink_row[:, :], sinks.to_broadcast([P, NH])).then_inc(bcast_in, 16)
            pool.dma_start(cv_nat[:, :], cache_v[0, 0].rearrange("t h d -> t (h d)")).then_inc(cache_in, 16)
            pool.wait_ge(v_done, 1)
            pool.dma_start(g2[:, :], norm2_g.to_broadcast([P, D])).then_inc(bcast_in, 16)
            pool.dma_start(b_rt[:, :], b_router.to_broadcast([P, NE])).then_inc(bcast_in, 16)
            pool.dma_start(w_rt[:, :, :], w_router.rearrange("l (k p) e -> p (l k) e", p=P)).then_inc(wrt_in, 16)

            roll = WIN - DEC
            rows_of = lambda a: a[0, 0].rearrange("t h d -> t (h d)")
            pool.wait_ge(cache_in, 32)
            pool.dma_start(rows_of(new_k_sample)[0:roll, :], ck_nat[DEC:WIN, :]).then_inc(kv_stored, 16)
            pool.dma_start(rows_of(new_v_sample)[0:roll, :], cv_nat[DEC:WIN, :]).then_inc(kv_stored, 16)
            pool.wait_ge(v_ready, 2)
            pool.dma_start(rows_of(new_v_prompt), v_nat[:, 1, :]).then_inc(kv_stored, 16)
            pool.dma_start(rows_of(new_v_sample)[roll:WIN, :], v_nat[0:DEC, 2, :]).then_inc(kv_stored, 16)
            pool.wait_ge(k_out_ready, 2)
            pool.dma_start(rows_of(new_k_prompt), k_out[:, 0, :]).then_inc(kv_stored, 16)
            pool.dma_start(rows_of(new_k_sample)[roll:WIN, :], k_out[0:DEC, 1, :]).then_inc(kv_stored, 16)
            pool.wait_ge(u_out_ready, 2)
            pool.dma_start(new_conv_prompt[0, 0], u_out[:, 0, :]).then_inc(kv_stored, 16)
            pool.dma_start(new_conv_sample[0, 0], u_out[:, 1, :]).then_inc(kv_stored, 16)

        @block.tensor
        def _(pe):
            mm = nc.tensor.matmul

            pe.wait_ge(consts, 3)
            pe.wait_ge(vec_in, 16 * 7)
            nc.tensor.transpose(ps[:, B_VEC, 0:NV], vec_rows[:, :], ident[0:NV, 0:NV]).then_inc(vec_turned, 1)
            pe.wait_ge(cache_in, 32)
            nc.tensor.transpose(ps[:, B_VEC, P:2 * P], ck_nat[:, :], ident[:, :]).then_inc(vec_turned, 1)

            for t, (_, n) in enumerate(TT):
                pe.wait_ge(x_scaled, t + 1)
                per = KT // len(XT_BANK[t])
                for k in range(KT):
                    out = ps[:, XT_BANK[t][k // per], (k % per) * n:(k % per + 1) * n]
                    last = nc.tensor.transpose(out, hn[0:n, t, k * P:(k + 1) * P], ident[0:n, 0:n])
                last.then_inc(x_turned, 1)

            pe.wait_ge(bias_in, 32)
            for f in range(2 * FT + KT):
                bank, at = (6, f) if f < 2 * FT else (7, f - 2 * FT)
                last = nc.tensor.transpose(ps[:, bank, at * NE:(at + 1) * NE], bias_rows[:, f * P:(f + 1) * P],
                                           ident[0:NE, 0:NE])
            last.then_inc(bias_turned, 1)

            pe.wait_ge(xnT_ready, len(TT) + 2)
            pe.wait_ge(wqkv_in, 16)

            def sum_squares(i):
                pe.wait_ge(qk_squared, i + 1)
                if i == 0:
                    pe.wait_ge(heads_set, 3)
                if i < 2:
                    pe.wait_ge(bias_ready, 2)
                else:
                    pe.wait_ge(head_std, i - 1)
                mm(ps[:, SS_BANK[i % 2], 0:TOK], head_ones[:, :], qk_sq[:, i, :], start=True, stop=True
                   ).then_inc(head_ss, 1)

            for i in range(1 + QT):
                if i == 2:
                    pe.wait_ge(vec_ready, 2)
                for k in range(KT):
                    cols = w_qkv[:, k, ATT:ATT + KV] if i == 0 else w_qkv[:, k, (i - 1) * P:i * P]
                    last = mm(ps[:, QK_BANK[i], 0:TOK], cols, xnT[:, k, :], start=(k == 0), stop=(k == KT - 1))
                last.then_inc(qk_done, 1)
                if i >= 1:
                    sum_squares(i - 1)
            for t, (t0, n) in enumerate(TT):
                for k in range(KT):
                    last = mm(ps[0:n, V_BANK, t * P:t * P + KV], xnT[:, k, t0:t0 + n], w_qkv[:, k, ATT + KV:QKV],
                              start=(k == 0), stop=(k == KT - 1))
            last.then_inc(v_done, 1)
            sum_squares(QT)

            def scores(c):
                if c == 0:
                    pe.wait_ge(qk_ready, 1 + QT)
                    pe.wait_ge(head_std, 1 + QT)
                else:
                    pe.wait_ge(exp_done, 5 * c)
                off, n = key_window(c)
                for b in range(4):
                    g, jp = b // 2, b % 2
                    half = slice(g * HEAD_DIM, (g + 1) * HEAD_DIM)
                    qs = qT[half, c, 2 * jp:2 * jp + 2, :].rearrange("p a t -> p (a t)")
                    if c == SAMPLE:
                        mm(SC[:, b, 0:WIN], qs, ckT[half, :], start=True, stop=True)
                        last = mm(SC[:, b, WIN:WIN + DEC], qs, kT[half, SEQ:TOK], start=True, stop=True)
                    else:
                        last = mm(SC[:, b, off:off + n], qs, kT[half, (c + 1) * CHUNK - n:(c + 1) * CHUNK],
                                  start=True, stop=True)
                last.then_inc(scores_done, 1)

            def key_tiles(c):
                off, n = key_window(c)
                parts = [(0, off, min(P, off + n))]
                if off + n > P:
                    parts.append((1, 0, off + n - P))
                return parts

            def turn_probs(c):
                pe.wait_ge(probs_ready, c + 1)
                if c >= 1:
                    pe.wait_ge(probsT_ready, c)
                if c == 0:
                    pe.wait_ge(qk_ready, 1 + QT)
                for b in range(4):
                    for tile, _, k1 in key_tiles(c):
                        last = nc.tensor.transpose(PT[0:k1, tile, b * P:(b + 1) * P],
                                                   probs[:, b, tile * P:tile * P + k1], ident[:, :])
                last.then_inc(probs_turned, 1)

            def attend(c):
                pe.wait_ge(probsT_ready, c + 1)
                pe.wait_ge(v_ready, 2)
                if c >= 1:
                    pe.wait_ge(att_mixed, c)
                parts = key_tiles(c)
                for b in range(4):
                    g, jp = b // 2, b % 2
                    cols = slice(g * HEAD_DIM, (g + 1) * HEAD_DIM)
                    for i, (tile, k0, k1) in enumerate(parts):
                        if c == SAMPLE:
                            vals = cv_nat[:, cols] if tile == 0 else v_nat[0:k1, 2, cols]
                        else:
                            vals = v_nat[k0:k1, tile, cols]
                        last = mm(AO[cols, jp * P:(jp + 1) * P], vals, probsT[k0:k1, tile, b * P:(b + 1) * P],
                                  start=(i == 0), stop=(i == len(parts) - 1))
                last.then_inc(att_done, 1)

            def turn_keys():
                pe.wait_ge(v_ready, 2)
                nc.tensor.transpose(KO[:, 0, :], kT[:, SEQ - WIN:SEQ], ident[:, :])
                nc.tensor.transpose(KO[0:DEC, 1, :], kT[:, SEQ:TOK], ident[:, :]).then_inc(k_turned, 1)

            for n in range(3 * CT):
                j, part = n // 3, n % 3
                if n == 0:
                    pe.wait_ge(wch_in, 16)
                if n == 2:
                    pe.wait_ge(wb_in, 16)
                if n < 3:
                    pe.wait_ge(qk_ready, n + 1)
                elif part == 0:
                    pe.wait_ge(c_copied, j)
                elif part == 1:
                    pe.wait_ge(u_ready, j)
                else:
                    pe.wait_ge(conv_mixed, j)
                col = (CONV, 2 * CONV, 0)[part] + j * P
                for k in range(KT):
                    last = mm(ps[:, BCH_BANK[part], 0:TOK], w_bch[:, k, col:col + P], xnT[:, k, :],
                              start=(k == 0), stop=(k == KT - 1))
                last.then_inc(bch_done, 1)
                if n % 2 == 0:
                    if n // 2 >= 1:
                        turn_probs(n // 2 - 1)
                    if n // 2 < NCH:
                        scores(n // 2)
                elif n >= 3:
                    attend((n - 3) // 2)
                else:
                    turn_keys()
            pe.wait_ge(u_ready, CT)
            pe.wait_ge(probsT_ready, NCH)
            for s, at in enumerate((SEQ, UW - (CW - 1))):
                for j in range(CT):
                    last = nc.tensor.transpose(ps[0:CW - 1, s, j * P:(j + 1) * P], uT[:, j, at:at + CW - 1],
                                               ident[:, :])
            last.then_inc(u_turned, 1)

            pe.wait_ge(wo_in, 48)

            def project_out(t):
                t0, n = TT[t]
                if t == 0:
                    pe.wait_ge(att_mixed, NCH)
                    pe.wait_ge(conv_mixed, CT)
                for half in range(2):
                    for j in range(MIX):
                        last = mm(ps[0:n, OUT_BANK[t][half], :], mixT[:, j, t0:t0 + n],
                                  w_o[:, j, half * HALF:(half + 1) * HALF], start=(j == 0), stop=(j == MIX - 1))
                    last.then_inc(out_done, 1)

            def logits(t):
                _, n = TT[t]
                pe.wait_ge(hn_ready, t + 1)
                if t == 0:
                    pe.wait_ge(u_out_ready, 2)
                    pe.wait_ge(wrt_in, 16)
                else:
                    pe.wait_ge(hnT_ready, t)
                for k in range(KT):
                    out = ps[:, k // 4, (k % 4) * P:(k % 4) * P + n]
                    last = nc.tensor.transpose(out, hn[0:n, t, k * P:(k + 1) * P], ident[0:n, 0:n])
                last.then_inc(hn_turned, 1)
                pe.wait_ge(hnT_ready, t + 1)
                for k in range(KT):
                    last = mm(LG[0:n, t, :], hnT[:, k, 0:n], w_rt[:, k, :], start=(k == 0), stop=(k == KT - 1))
                last.then_inc(logits_done, 1)

            project_out(0)
            project_out(1)
            logits(0)
            project_out(2)
            logits(1)
            logits(2)

            pe.wait_ge(sel_ready, 1)
            for t in range(NT + 1):
                for s in range(min(t, NT - 1) + 1):
                    last = mm(RK[:, t, :], before[:, :] if s == t else ones[:, :], sel[:, s, :],
                              start=(s == 0), stop=(s == min(t, NT - 1)))
            last.then_inc(ranked, 1)

            def gather(n, slot):
                pe.wait_ge(onehot_ready, n + 1)
                for k in range(KT):
                    for t, (_, m) in enumerate(TT):
                        last = mm(XE[:, k, :], hn[0:m, t, k * P:(k + 1) * P], onehot[0:m, slot, t, :],
                                  start=(t == 0), stop=(t == NT - 1))
                last.then_inc(gathered, 1)

            def gate_up(n, slot):
                pe.wait_ge(xe_ready, n + 1)
                for k in range(KT):
                    pe.wait_ge(gu_in[k], 16 * (n + 1))
                    for f in range(2 * FT):
                        last = mm(GU[slot][:, f // FT, (f % FT) * CAP:(f % FT + 1) * CAP],
                                  gu_ring[:, k, f * P:(f + 1) * P], xe[:, slot, k, :],
                                  start=(k == 0 and f % FT == 0), stop=(k == KT - 1), skip_group_check=True)
                    last.then_inc(gu_used, 1)

            def down(n, slot):
                pe.wait_ge(he_ready, n + 1)
                for m in range(FT // 2):
                    pe.wait_ge(dn_in[m], 16 * (n + 1))
                    for a in range(2):
                        for d in range(KT):
                            last = mm(YT[:, d, :], dn_ring[:, m, a, d * P:(d + 1) * P], he[:, slot, 2 * m + a, :],
                                      start=(m == 0 and a == 0 and d == 0), stop=(m == FT // 2 - 1 and a == 1),
                                      skip_group_check=True)
                    last.then_inc(dn_used, 1)

            def turn_gates(i):
                pe.wait_ge(gated_ready, i + 1)
                for t, (_, m) in enumerate(TT):
                    last = nc.tensor.transpose(ST[0:ROWS, t * P:t * P + m],
                                               gated[0:m, t, :, :].rearrange("p a c -> p (a c)")[:, 0:ROWS],
                                               ident[0:m, 0:m])
                last.then_inc(scat_turned, 1)

            def turn_rows(i):
                for k in range(KT):
                    last = nc.tensor.transpose(YN[0:ROWS, k * P:(k + 1) * P],
                                               yeT[:, k, :, :].rearrange("p a c -> p (a c)")[:, 0:ROWS],
                                               ident[:, :])
                last.then_inc(y_turned, 1)

            def scatter(i):
                pe.wait_ge(ye_ready, i + 1)
                pe.wait_ge(scat_ready, i + 1)
                for u in range(2 * NT):
                    t, half = u // 2, u % 2
                    if u >= 2:
                        pe.wait_ge(added, 2 * NT * i + u - 1)
                    _, m = TT[t]
                    mm(ps[0:m, 6 + half, :], scat[0:ROWS, t * P:t * P + m], ye[0:ROWS, half * HALF:(half + 1) * HALF],
                       start=True, stop=True).then_inc(scattered, 1)

            def even(i, first=False):
                e = 2 * i
                pe.wait_ge(xe_ready, e + 1)
                gather(e + 1, 1)
                if not first:
                    pe.wait_ge(u_biased, e - 1)
                gate_up(e, 0)
                if not first:
                    pe.wait_ge(xe_ready, e + 2)
                    turn_gates(i - 1)
                    pe.wait_ge(yeT_ready, e - 1)
                    down(e - 1, 1)

            def odd(i, first=False, last=False):
                e = 2 * i + 1
                if not last:
                    if not first:
                        pe.wait_ge(scat_ready, i)
                    gather(e + 1, 0)
                if not first:
                    pe.wait_ge(yeT_ready, e - 1)
                    pe.wait_ge(added, 2 * NT * (i - 1))
                    turn_rows(i - 1)
                    pe.wait_ge(u_biased, e - 1)
                gate_up(e, 1)
                if not first:
                    scatter(i - 1)
                    pe.wait_ge(yeT_ready, e - 1)
                down(e - 1, 0)

            pe.wait_ge(rank_ready, 1)
            gather(0, 0)
            even(0, first=True)
            odd(0, first=True)
            with pe.Fori(1, PAIRS - 1) as i:
                even(i)
                odd(i)
            even(PAIRS - 1)
            odd(PAIRS - 1, last=True)
            turn_gates(PAIRS - 1)
            pe.wait_ge(yeT_ready, NE - 1)
            down(NE - 1, 1)
            pe.wait_ge(yeT_ready, NE)
            pe.wait_ge(added, 2 * NT * (PAIRS - 1))
            turn_rows(PAIRS - 1)
            scatter(PAIRS - 1)

            def again(n, e):
                i = n - NE + PAIRS
                pe.wait_ge(added, 2 * NT * i)
                pe.wait_ge(second_zero, 1)
                gather(n, 0)
                gate_up(n, 0)
                turn_gates(i)
                down(n, 0)
                pe.wait_ge(yeT_ready, n + 1)
                turn_rows(i)
                scatter(i)

            further_rounds(pe, again)

        @block.scalar
        def _(act):
            A = nc.scalar.activation
            act.wait_ge(eps_set, 1)
            for t, (_, n) in enumerate(TT):
                act.wait_ge(x_in[t // 2], 16)
                if t:
                    act.wait_ge(x_sumsq, t)
                A(junk[0:n, :], x[0:n, t, :], ACT.Square, accum_out=st[0:n, 0, t:t + 1]).then_inc(x_sumsq, 1)
                act.wait_ge(x_sumsq, t + 1)
                A(st[0:n, 1, t:t + 1], st[0:n, 0, t:t + 1], ACT.Sqrt, bias=eps[0:n, :], scale=1.0 / D
                  ).then_inc(x_std, 1)

            act.wait_ge(bias_turned, 1)
            nc.scalar.copy(b_guT[:, :, :].rearrange("p f e -> p (f e)"), ps[:, 6, :]).then_inc(bias_ready, 1)
            nc.scalar.copy(b_dnT[:, :, :].rearrange("p f e -> p (f e)"), ps[:, 7, 0:KT * NE]).then_inc(bias_ready, 1)

            def square_head(i):
                act.wait_ge(qk_done, i + 1)
                A(qk_sq[:, i, :], ps[:, QK_BANK[i], 0:TOK], ACT.Square).then_inc(qk_squared, 1)

            def root_head(i):
                act.wait_ge(head_ss, i + 1)
                A(qk_sq[:, i, :], ps[:, SS_BANK[i % 2], 0:TOK], ACT.Sqrt, bias=eps[:, :], scale=1.0 / HEAD_DIM
                  ).then_inc(head_std, 1)

            for i in range(1 + QT):
                square_head(i)
                if i:
                    root_head(i - 1)
            act.wait_ge(v_done, 1)
            nc.scalar.copy(v_nat[:, 0:2, :].rearrange("p t n -> p (t n)"), ps[:, V_BANK, 0:2 * P]).then_inc(v_ready, 1)
            nc.scalar.copy(v_nat[0:DEC, 2, :], ps[0:DEC, V_BANK, 2 * P:3 * P]).then_inc(v_ready, 1)
            root_head(QT)

            def exps(c):
                off, n = key_window(c)
                act.wait_ge(smx_neg, 2 * (c + 1))
                for b in range(4):
                    A(probs[:, b, off:off + n], SC[:, b, off:off + n], ACT.Exp, bias=smx[:, 2, b:b + 1],
                      scale=HEAD_DIM ** -0.5, accum_out=smx[:, 4, b:b + 1]).then_inc(exp_done, 1)
                A(smx[:, 5, :], smx[:, 3, :], ACT.Exp).then_inc(exp_done, 1)

            def copy_probsT(c):
                off, n = key_window(c)
                act.wait_ge(probs_turned, c + 1)
                if c >= 1:
                    act.wait_ge(att_done, c)
                lo = min(P, off + n)
                last = nc.scalar.copy(probsT[0:lo, 0, :], PT[0:lo, 0, :])
                if off + n > P:
                    last = nc.scalar.copy(probsT[0:off + n - P, 1, :], PT[0:off + n - P, 1, :])
                last.then_inc(probsT_ready, 1)

            for n in range(3 * CT):
                if n % 3 == 0:
                    act.wait_ge(bch_done, n + 1)
                    if n:
                        act.wait_ge(u_ready, n // 3)
                    nc.scalar.copy(c_sb[:, :], ps[:, BCH_BANK[0], 0:TOK]).then_inc(c_copied, 1)
                if n % 2 == 0:
                    if n // 2 >= 1:
                        copy_probsT(n // 2 - 1)
                    if n // 2 < NCH:
                        exps(n // 2)
                elif n == 1:
                    act.wait_ge(k_turned, 1)
                    nc.scalar.copy(k_out[:, 0, :], KO[:, 0, :]).then_inc(k_out_ready, 1)
                    nc.scalar.copy(k_out[0:DEC, 1, :], KO[0:DEC, 1, :]).then_inc(k_out_ready, 1)
            act.wait_ge(u_turned, 1)
            for s in range(2):
                nc.scalar.copy(u_out[:, s, :], ps[0:CW - 1, s, :]).then_inc(u_out_ready, 1)

            def rms_h(t):
                _, n = TT[t]
                act.wait_ge(h_ready, 2 * (t + 1))
                if t:
                    act.wait_ge(h_sumsq, t)
                A(junk[0:n, :], x[0:n, t, :], ACT.Square, accum_out=st[0:n, 0, t:t + 1]).then_inc(h_sumsq, 1)
                act.wait_ge(h_sumsq, t + 1)
                A(st[0:n, 1, t:t + 1], st[0:n, 0, t:t + 1], ACT.Sqrt, bias=eps[0:n, :], scale=1.0 / D
                  ).then_inc(h_std, 1)

            def copy_hnT(t):
                _, n = TT[t]
                act.wait_ge(hn_turned, t + 1)
                if t:
                    act.wait_ge(logits_done, t)
                nc.scalar.copy(hnT[:, :, 0:n], ps[:, 0:2, :].rearrange("p a (k t) -> p (a k) t", t=P)[:, :, 0:n]
                               ).then_inc(hnT_ready, 1)

            rms_h(0)
            rms_h(1)
            copy_hnT(0)
            rms_h(2)
            copy_hnT(1)
            copy_hnT(2)
            act.wait_ge(top_ready, 1)
            for t in range(NT):
                A(gates[:, t, :], lg[:, t, :], ACT.Exp, bias=neg_top[:, t:t + 1]).then_inc(gexp_done, 1)

            def copy_xe(n, slot):
                act.wait_ge(gathered, n + 1)
                nc.scalar.copy(xe[:, slot, :, :], XE).then_inc(xe_ready, 1)

            def sigmoid(n):
                act.wait_ge(g_ready, n + 1)
                A(sg[:, :, :], ge[:, :, :], ACT.Sigmoid, scale=ALPHA).then_inc(sig_ready, 1)

            def copy_scat(i):
                act.wait_ge(scat_turned, i + 1)
                nc.scalar.copy(scat[0:ROWS, 0:2 * P + DEC], ST[0:ROWS, 0:2 * P + DEC]).then_inc(scat_ready, 1)

            def copy_rows(i):
                act.wait_ge(y_turned, i + 1)
                nc.scalar.copy(ye[0:ROWS, :], YN[0:ROWS, :]).then_inc(ye_ready, 1)

            def even(i, first=False):
                e = 2 * i
                if not first:
                    act.wait_ge(gu_used, KT * e)
                copy_xe(e + 1, 1)
                sigmoid(e)
                if not first:
                    copy_scat(i - 1)

            def odd(i, first=False, last=False):
                e = 2 * i + 1
                if not last:
                    act.wait_ge(gu_used, KT * e)
                    copy_xe(e + 1, 0)
                if not first:
                    copy_rows(i - 1)
                sigmoid(e)

            copy_xe(0, 0)
            even(0, first=True)
            odd(0, first=True)
            with act.Fori(1, PAIRS - 1) as i:
                even(i)
                odd(i)
            even(PAIRS - 1)
            odd(PAIRS - 1, last=True)
            act.wait_ge(scattered, 2 * NT * (PAIRS - 1))
            copy_scat(PAIRS - 1)
            copy_rows(PAIRS - 1)

            def again(n, e):
                i = n - NE + PAIRS
                copy_xe(n, 0)
                sigmoid(n)
                copy_scat(i)
                copy_rows(i)

            further_rounds(act, again)

        @block.vector
        def _(dve):
            V = nc.vector
            V.memset(eps[:, :], EPS).then_inc(eps_set, 1)
            V.memset(head_ones[:, :], 0.0).then_inc(heads_set, 1)
            dve.wait_ge(heads_set, 1)
            for g in range(2):
                half = slice(g * HEAD_DIM, (g + 1) * HEAD_DIM)
                V.memset(head_ones[half, half], 1.0).then_inc(heads_set, 1)
            V.memset(lg[:, :, :], 0.0).then_inc(router_set, 1)
            V.memset(top4[:, :, :], NO_LOGIT).then_inc(router_set, 1)
            V.memset(uT[:, :, 0:CW - 1], 0.0).then_inc(conv_pad, 1)
            for t, (_, n) in enumerate(TT):
                dve.wait_ge(x_std, t + 1)
                V.reciprocal(st[0:n, 2, t:t + 1], st[0:n, 1, t:t + 1]).then_inc(x_rstd, 1)
                dve.wait_ge(x_rstd, t + 1)
                V.tensor_scalar(hn[0:n, t, :], x[0:n, t, :], st[0:n, 2, t:t + 1], None, ALU.mult
                                ).then_inc(x_scaled, 1)
            dve.wait_ge(vec_turned, 2)
            V.tensor_copy(vec[:, :], ps[:, B_VEC, 0:NV]).then_inc(vec_ready, 1)
            V.tensor_copy(ckT[:, :], ps[:, B_VEC, P:2 * P]).then_inc(vec_ready, 1)
            dve.wait_ge(vec_ready, 1)
            for t, (t0, n) in enumerate(TT):
                dve.wait_ge(x_turned, t + 1)
                per = KT // len(XT_BANK[t])
                for i, bank in enumerate(XT_BANK[t]):
                    g = vec[:, V_G1 + i * per:V_G1 + (i + 1) * per].unsqueeze(2).to_broadcast([P, per, n])
                    V.tensor_tensor(xnT[:, i * per:(i + 1) * per, t0:t0 + n],
                                    ps[:, bank, 0:per * n].rearrange("p (k t) -> p k t", t=n), g, ALU.mult
                                    ).then_inc(xnT_ready, 1)
            V.tensor_copy(uT[:, :, SEQ + CW - 1:SEQ + 2 * (CW - 1)],
                          vec[:, V_STATE:NV].rearrange("p (r c) -> p c r", r=CW - 1)).then_inc(conv_pad, 1)
            dve.wait_ge(bcast_in, 48)
            for a in range(2):
                half = slice(a * CHUNK, (a + 1) * CHUNK)
                V.tensor_copy(sink[half, :], sink_row[half, :].rearrange("p (b a) -> p a b", a=2)[:, a, :]
                              ).then_inc(sink_set, 1)

            for i in range(1 + QT):
                dve.wait_ge(head_std, i + 1)
                V.reciprocal(qk_sq[:, i, :], qk_sq[:, i, :]).then_inc(head_rstd, 1)
                dve.wait_ge(head_rstd, i + 1)
                if i == 0:
                    V.scalar_tensor_tensor(out=kT[:, :], in0=ps[:, QK_BANK[i], 0:TOK], scalar=vec[:, V_KG:V_KG + 1],
                                           in1=qk_sq[:, i, :], op0=ALU.mult, op1=ALU.mult).then_inc(qk_ready, 1)
                    continue
                for a in range(2):
                    head = 2 * (i - 1) + a
                    g, j = head // (NH // NKV), head % (NH // NKV)
                    src = slice(a * HEAD_DIM, (a + 1) * HEAD_DIM)
                    by_chunk = lambda ap: ap.rearrange("p (c t) -> p c t", t=CHUNK)
                    last = V.scalar_tensor_tensor(
                        out=qT[g * HEAD_DIM:(g + 1) * HEAD_DIM, :, j, :], in0=by_chunk(ps[src, QK_BANK[i], 0:TOK]),
                        scalar=vec[src, V_QG:V_QG + 1], in1=by_chunk(qk_sq[src, i, :]), op0=ALU.mult, op1=ALU.mult)
                last.then_inc(qk_ready, 1)

            def softmax(c):
                off, n = key_window(c)
                S = 4 * c
                dve.wait_ge(scores_done, c + 1)
                if c == 0:
                    dve.wait_ge(sink_set, 2)
                V.tensor_reduce(smx[:, 0, :], SC[:, :, off:off + n], AX.X, ALU.max).then_inc(smx_step, 1)
                dve.wait_ge(smx_step, S + 1)
                V.scalar_tensor_tensor(out=smx[:, 1, :], in0=smx[:, 0, :], scalar=HEAD_DIM ** -0.5, in1=sink[:, :],
                                       op0=ALU.mult, op1=ALU.max).then_inc(smx_step, 1)
                dve.wait_ge(smx_step, S + 2)
                V.tensor_scalar(smx[:, 2, :], smx[:, 1, :], -1.0, None, ALU.mult).then_inc(smx_neg, 1)
                V.tensor_tensor(smx[:, 3, :], sink[:, :], smx[:, 1, :], ALU.subtract).then_inc(smx_neg, 1)
                dve.wait_ge(exp_done, 5 * (c + 1))
                V.tensor_tensor(smx[:, 6, :], smx[:, 4, :], smx[:, 5, :], ALU.add).then_inc(smx_step, 1)
                dve.wait_ge(smx_step, S + 3)
                V.reciprocal(smx[:, 7, :], smx[:, 6, :]).then_inc(smx_step, 1)
                dve.wait_ge(smx_step, S + 4)
                V.tensor_tensor(probs[:, :, off:off + n], probs[:, :, off:off + n],
                                smx[:, 7, :].unsqueeze(2).to_broadcast([P, 4, n]), ALU.mult).then_inc(probs_ready, 1)

            def convolve(j):
                dve.wait_ge(c_copied, j + 1)
                dve.wait_ge(bch_done, 3 * j + 2)
                hc = ps[:, BCH_BANK[1], 0:TOK]
                V.tensor_tensor(uT[:, j, CW - 1:CW - 1 + SEQ], c_sb[:, 0:SEQ], hc[:, 0:SEQ], ALU.mult
                                ).then_inc(cv_step, 1)
                V.tensor_tensor(uT[:, j, UW - DEC:UW], c_sb[:, SEQ:TOK], hc[:, SEQ:TOK], ALU.mult
                                ).then_inc(u_ready, 1)
                dve.wait_ge(cv_step, 3 * j + 1)
                dve.wait_ge(u_ready, j + 1)
                if j == 0:
                    dve.wait_ge(conv_pad, 2)
                else:
                    dve.wait_ge(conv_mixed, j)
                W = UW - (CW - 1)
                tap = lambda w: vec[:, V_CONV + w * CT + j:V_CONV + w * CT + j + 1]
                V.tensor_scalar(cv[:, :], uT[:, j, 0:W], tap(0), None, ALU.mult).then_inc(cv_step, 1)
                dve.wait_ge(cv_step, 3 * j + 2)
                V.scalar_tensor_tensor(out=cv[:, :], in0=uT[:, j, 1:1 + W], scalar=tap(1), in1=cv[:, :],
                                       op0=ALU.mult, op1=ALU.add).then_inc(cv_step, 1)
                dve.wait_ge(cv_step, 3 * j + 3)
                V.scalar_tensor_tensor(out=cv[:, :], in0=uT[:, j, 2:2 + W], scalar=tap(2), in1=cv[:, :],
                                       op0=ALU.mult, op1=ALU.add).then_inc(rows_moved, 1)

            def gate_conv(j):
                dve.wait_ge(bch_done, 3 * j + 3)
                dve.wait_ge(rows_moved, j + 1)
                B = ps[:, BCH_BANK[2], 0:TOK]
                V.tensor_tensor(mixT[:, QT + j, 0:SEQ], B[:, 0:SEQ], cv[:, 0:SEQ], ALU.mult)
                V.tensor_tensor(mixT[:, QT + j, SEQ:TOK], B[:, SEQ:TOK], cv[:, SEQ + CW - 1:], ALU.mult
                                ).then_inc(conv_mixed, 1)

            for n in range(3 * CT):
                if n % 3 == 1:
                    convolve(n // 3)
                if n % 3 == 2:
                    gate_conv(n // 3)
                if n % 2 == 0 and n // 2 < NCH:
                    softmax(n // 2)
                if n % 2 == 1 and n >= 3:
                    c = (n - 3) // 2
                    dve.wait_ge(att_done, c + 1)
                    V.tensor_copy(mixT[:, 0:QT, c * CHUNK:(c + 1) * CHUNK],
                                  AO.rearrange("p (j t) -> p j t", t=CHUNK)).then_inc(att_mixed, 1)

            for t, (_, n) in enumerate(TT):
                for half in range(2):
                    cols = slice(half * HALF, (half + 1) * HALF)
                    dve.wait_ge(out_done, 2 * t + half + 1)
                    V.tensor_tensor(x[0:n, t, cols], ps[0:n, OUT_BANK[t][half], :], x[0:n, t, cols], ALU.add
                                    ).then_inc(h_ready, 1)
                dve.wait_ge(h_std, t + 1)
                V.reciprocal(st[0:n, 2, t:t + 1], st[0:n, 1, t:t + 1]).then_inc(h_rstd, 1)
                dve.wait_ge(h_rstd, t + 1)
                V.scalar_tensor_tensor(out=hn[0:n, t, :], in0=x[0:n, t, :], scalar=st[0:n, 2, t:t + 1],
                                       in1=g2[0:n, :], op0=ALU.mult, op1=ALU.mult).then_inc(hn_ready, 1)

            n_route = [0]

            def then(ins):
                n_route[0] += 1
                ins.then_inc(route, 1)
                dve.wait_ge(route, n_route[0])

            dve.wait_ge(router_set, 2)
            for t, (_, n) in enumerate(TT):
                dve.wait_ge(logits_done, t + 1)
                then(V.tensor_tensor(lg[0:n, t, :], LG[0:n, t, :], b_rt[0:n, :], ALU.add))
                then(V.max(top8[:, t, :], lg[:, t, :]))
            then(V.tensor_copy(top4[:, :, 0:TOP_K], top8[:, :, 0:TOP_K]))
            V.tensor_scalar(neg_top[:, :], top8[:, :, 0], -1.0, None, ALU.mult).then_inc(top_ready, 1)
            for t in range(NT):
                then(V.match_replace(left[:, t, :], top4[:, t, :], lg[:, t, :], -NO_LOGIT))
            then(V.tensor_tensor(sel[:, :, :], left[:, :, :], lg[:, :, :], ALU.not_equal))
            V.memset(sel[DEC:P, 2, :], 0.0).then_inc(sel_ready, 1)
            dve.wait_ge(sel_ready, 1)
            dve.wait_ge(gexp_done, NT)
            then(V.tensor_tensor(gates[:, :, :], gates[:, :, :], sel[:, :, :], ALU.mult))
            then(V.tensor_reduce(gsum[:, :], gates[:, :, :], AX.X, ALU.add))
            then(V.memset(gsum[DEC:P, 2:3], 1.0))
            then(V.reciprocal(gsum[:, :], gsum[:, :]))
            then(V.tensor_tensor(gates[:, :, :], gates[:, :, :],
                                 gsum[:, :].unsqueeze(2).to_broadcast([P, NT, NE]), ALU.mult))
            dve.wait_ge(ranked, 1)
            then(V.scalar_tensor_tensor(out=rank[:, :, :], in0=RK[:, 0:NT, :], scalar=1.0, in1=sel[:, :, :],
                                        op0=ALU.add, op1=ALU.mult))
            then(V.tensor_scalar(rank[:, :, :], rank[:, :, :], -1.0, None, ALU.add))
            V.tensor_copy(counts[:, :], RK[:, NT, :]).then_inc(counts_ready, 1)
            then(V.tensor_reduce(most[:, :], RK[:, NT, :], AX.X, ALU.max))
            V.tensor_copy(most_i[:, :], most[:, :]).then_inc(counts_ready, 1)
            dve.wait_ge(counts_ready, 2)
            V.memset(smx[:, 0, 0:1], 0.0).then_inc(rank_ready, 1)

            def mark_rows(n, e, slot):
                V.tensor_tensor(onehot[:, slot, :, :], row_ids[:, :].unsqueeze(1).to_broadcast([P, NT, CAP]),
                                rank[:, :, bass.ds(e, 1)].to_broadcast([P, NT, CAP]), ALU.is_equal
                                ).then_inc(onehot_ready, 1)

            def mark_gates(n, e, slot, s):
                dve.wait_ge(onehot_ready, n + 1)
                return V.tensor_tensor(gated[:, :, s, :], onehot[:, slot, :, :],
                                       gates[:, :, bass.ds(e, 1)].to_broadcast([P, NT, CAP]), ALU.mult)

            def swiglu(n, e, slot):
                bias = lambda f0: b_guT[:, f0:f0 + FT, bass.ds(e, 1)].to_broadcast([P, FT, CAP])
                tiles = lambda a: GU[slot][:, a, :].rearrange("p (f c) -> p f c", f=FT)
                dve.wait_ge(gu_used, KT * (n + 1))
                V.tensor_tensor(ge[:, :, :], tiles(0), bias(0), ALU.add).then_inc(g_biased, 1)
                dve.wait_ge(g_biased, n + 1)
                V.tensor_scalar(ge[:, :, :], ge[:, :, :], LIMIT, None, ALU.min).then_inc(g_ready, 1)
                V.tensor_tensor(ue[:, :, :], tiles(1), bias(FT), ALU.add).then_inc(u_biased, 1)
                dve.wait_ge(u_biased, n + 1)
                V.tensor_scalar(ue[:, :, :], ue[:, :, :], LIMIT, -LIMIT, ALU.min, ALU.max).then_inc(u_clipped, 1)
                dve.wait_ge(sig_ready, n + 1)
                V.tensor_tensor(ge[:, :, :], ge[:, :, :], sg[:, :, :], ALU.mult).then_inc(gs_ready, 1)
                dve.wait_ge(u_clipped, n + 1)
                dve.wait_ge(gs_ready, n + 1)
                V.scalar_tensor_tensor(out=he[:, slot, :, :], in0=ue[:, :, :], scalar=1.0, in1=ge[:, :, :],
                                       op0=ALU.add, op1=ALU.mult).then_inc(he_ready, 1)

            def take_y(n, e, s):
                dve.wait_ge(dn_used, (FT // 2) * (n + 1))
                V.tensor_tensor(yeT[:, :, s, :], YT, b_dnT[:, :, bass.ds(e, 1)].to_broadcast([P, KT, CAP]), ALU.add
                                ).then_inc(yeT_ready, 1)

            def add_rows(i):
                for u in range(2 * NT):
                    t, half = u // 2, u % 2
                    _, m = TT[t]
                    cols = slice(half * HALF, (half + 1) * HALF)
                    dve.wait_ge(scattered, 2 * NT * i + u + 1)
                    V.tensor_tensor(x[0:m, t, cols], ps[0:m, 6 + half, :], x[0:m, t, cols], ALU.add
                                    ).then_inc(added, 1)

            def even(i, first=False):
                e = 2 * i
                if not first:
                    pass
                dve.wait_ge(gathered, e + 1)
                swiglu(e, e, 0)
                if not first:
                    dve.wait_ge(scat_turned, i)
                mark_gates(e, e, 0, 0)
                dve.wait_ge(gathered, e + 2)
                mark_gates(e + 1, e + 1, 1, 1).then_inc(gated_ready, 1)
                if not first:
                    take_y(e - 1, e - 1, 1)

            def odd(i, first=False, last=False):
                e = 2 * i + 1
                if not last:
                    dve.wait_ge(gated_ready, i + 1)
                    mark_rows(e + 1, e + 1, 0)
                swiglu(e, e, 1)
                if not last:
                    mark_rows(e + 2, e + 2, 1)
                if not first:
                    add_rows(i - 1)
                    dve.wait_ge(y_turned, i)
                take_y(e - 1, e - 1, 0)

            mark_rows(0, 0, 0)
            mark_rows(1, 1, 1)
            even(0, first=True)
            odd(0, first=True)
            with dve.Fori(1, PAIRS - 1) as i:
                even(i)
                odd(i)
            even(PAIRS - 1)
            odd(PAIRS - 1, last=True)
            take_y(NE - 1, NE - 1, 1)
            add_rows(PAIRS - 1)

            def next_round(q):
                V.tensor_scalar(row_ids[:, :], row_ids[:, :], float(CAP), None, ALU.add).then_inc(rows_moved, 1)
                dve.wait_ge(rows_moved, q + CT)
                V.memset(gated[:, :, 1, :], 0.0)
                V.memset(yeT[:, :, 1, :], 0.0).then_inc(second_zero, 1)

            def again(n, e):
                i = n - NE + PAIRS
                dve.wait_ge(added, 2 * NT * i)
                mark_rows(n, e, 0)
                mark_gates(n, e, 0, 0).then_inc(gated_ready, 1)
                swiglu(n, e, 0)
                take_y(n, e, 0)
                add_rows(i)

            further_rounds(dve, again, next_round)
            V.memset(smx[:, 0, 1:2], 0.0).then_inc(y_ready, 1)


_INS = ['x_prompt', 'x_sample', 'cache_k', 'cache_v', 'state_conv', 'norm1_g', 'w_in', 'q_norm_g', 'k_norm_g',
        'sinks', 'conv_w', 'w_out', 'norm2_g', 'w_router', 'b_router', 'w_gu', 'b_gu', 'w_down', 'b_down']
_OUTS = [(1, 256, 1024), (1, 64, 1024), (1, 1, 128, 2, 64), (1, 1, 128, 2, 64), (1, 1, 2, 512),
         (1, 1, 128, 2, 64), (1, 1, 128, 2, 64), (1, 1, 2, 512)]


def kernel(**inputs):
    import numpy as _np
    import concourse.bacc as _bacc
    from concourse import mybir as _mybir
    from concourse.bass_utils import run_bass_kernel_spmd as _run

    nc = _bacc.Bacc("TRN2", target_bir_lowering=False, num_devices=1)
    arrays, args = {}, []
    for name in _INS:
        a = _np.ascontiguousarray(inputs[name])
        arrays[f"in_{name}_dram"] = a
        args.append(nc.dram_tensor(f"in_{name}_dram", a.shape, _mybir.dt.from_np(a.dtype), kind="ExternalInput").ap())
    for i, shape in enumerate(_OUTS):
        dt = _mybir.dt.from_np(_np.dtype("float32"))
        args.append(nc.dram_tensor(f"out_{i}_dram", shape, dt, kind="ExternalOutput").ap())
    hybrid_layer_kernel(nc, *args)
    r = _run(nc, [arrays], core_ids=[0])
    return tuple(r.results[0][f"out_{i}_dram"] for i in range(len(_OUTS)))
```

```python
from contextlib import ExitStack

import concourse.bass as bass
from concourse import mybir

ALU = mybir.AluOpType
ACT = mybir.ActivationFunctionType
AX = mybir.AxisListType
F32 = mybir.dt.float32
F32R = mybir.dt.float32r
I32 = mybir.dt.int32

P = 128
CHUNK = 64
HEAD_DIM = 64
TOP_K = 4
EPS = 1e-6
LIMIT = 7.0
ALPHA = 1.702
CAP = 64
NO_LOGIT = 3.0e38


def hybrid_layer_kernel(nc, x_prompt, x_sample, cache_k, cache_v, state_conv, norm1_g, w_in, q_norm_g,
                        k_norm_g, sinks, conv_w, w_out, norm2_g, w_router, b_router, w_gu, b_gu,
                        w_down, b_down, y_prompt, y_sample, new_k_prompt, new_v_prompt,
                        new_conv_prompt, new_k_sample, new_v_sample, new_conv_sample):
    SEQ, D = x_prompt.shape[1:]
    DEC = x_sample.shape[1]
    IN_DIM = w_in.shape[2]
    NH = sinks.shape[1]
    NKV = cache_k.shape[3]
    KV = NKV * HEAD_DIM
    ATT = NH * HEAD_DIM
    CONV = conv_w.shape[2]
    CW = conv_w.shape[1]
    WIN = cache_k.shape[2]
    NE = w_router.shape[2]
    FF = w_down.shape[2]
    KT = D // P
    FT = FF // P
    CT = CONV // P
    TOK = SEQ + DEC
    NT = 3
    TT = [(0, P), (P, P), (2 * P, DEC)]
    HALF = D // 2
    QT = ATT // P
    NCH = TOK // CHUNK
    SAMPLE = NCH - 1
    MIX = (ATT + CONV) // P
    QKV = ATT + 2 * KV
    PAIRS = NE // 2
    ROUNDS = -(-TOK // CAP)
    FLAT = 2 * FF
    GUC, DNC = KT, FT * D // FLAT
    CH = GUC + DNC
    FPC = FLAT // D
    RAW, SPLIT = 8, 3
    assert (2 * CH) % RAW == 0 and CH % SPLIT == 0 and (RAW, CH, GUC) == (8, 12, 8)
    assert (SEQ, DEC, CHUNK, WIN, KV, NKV, HALF, QT, FT * CAP) == (256, 64, 64, 128, 128, 2, 512, 4, FT * CAP)
    assert FT * CAP <= 512 and KT == FT and 2 * FT * P == 2048

    ctx = ExitStack()
    with ctx:
        def sb(name, shape, dt=F32):
            return ctx.enter_context(nc.sbuf_tensor(name, shape, dt))

        class Region:

            def __init__(self, name, size):
                sb(name, [P, size // 4])
                self.base = nc.sbuf_base - size
                self.size, self.name = size, name
                self.at = 0

            def put(self, name, *shape, dt=F32, at=None, rows=P):
                size = 4
                for d in shape:
                    size *= d
                at = self.at if at is None else at
                assert at % 32 == 0 and at + size <= self.size, (self.name, name, at + size)
                self.at = at + -(-size // 32) * 32
                return nc.alloc_sbuf_tensor_at(name, [rows, *shape], dt, offset=self.base + at)

        def sem(name):
            return ctx.enter_context(nc.semaphore(name))

        ps = ctx.enter_context(nc.psum_tensor("ps", [P, 8, 512], F32))

        raw_region = Region("raw_region", RAW * FLAT * 4)
        raw = raw_region.put("raw", RAW, FLAT)
        w_bch = raw_region.put("w_bch", KT, 3 * CONV, at=2 * FLAT * 4)
        split_region = Region("split_region", 2 * SPLIT * FLAT * 4)
        w_hi = split_region.put("w_hi", SPLIT, FLAT, dt=F32R)
        w_lo = split_region.put("w_lo", SPLIT, FLAT, dt=F32R)
        w_qkv = split_region.put("w_qkv", KT, QKV, at=0)
        xnT = split_region.put("xnT", KT, TOK)
        qk_sq = split_region.put("qk_sq", 1 + QT, TOK)
        qT = split_region.put("qT", NCH, NH // NKV, CHUNK)
        kT = split_region.put("kT", TOK)
        hnT = split_region.put("hnT", KT, P, at=0)
        g2 = split_region.put("g2", D)
        w_rt = split_region.put("w_rt", KT, NE)
        probsT = split_region.put("probsT", 2, 512)
        k_out = split_region.put("k_out", 2, KV)
        c_sb = split_region.put("c_sb", TOK)
        junk_h = split_region.put("junk_h", D)
        v_nat = split_region.put("v_nat", NT, KV)
        assert split_region.at <= KT * QKV * 4
        work_region = Region("work_region", 49152)
        xhl = work_region.put("xhl", 2, KT, 2 * CAP, dt=F32R)
        he = work_region.put("he", FT, 2 * CAP, dt=F32R)
        y_hi = work_region.put("y_hi", 2, D, dt=F32R)
        y_lo = work_region.put("y_lo", 2, D, dt=F32R)
        ohT = work_region.put("ohT", 2, NT * P, dt=F32R)
        gu_sb = work_region.put("gu_sb", FLAT)
        ge = work_region.put("ge", FT, CAP)
        ue = work_region.put("ue", FT, CAP)
        sg = work_region.put("sg", FT, CAP)
        oh = work_region.put("oh", NT, 2, 2, CAP)
        w_o = work_region.put("w_o", MIX, D, at=0)
        bias_rows = work_region.put("bias_rows", 2 * FF, rows=NE)
        UW = SEQ + DEC + 2 * (CW - 1)
        uT = work_region.put("uT", CT, UW)

        ident = sb("ident", [P, P])
        ones = sb("ones", [P, P])
        before = sb("before", [P, P])
        head_ones = sb("head_ones", [P, P])
        fold = sb("fold", [2 * CAP, CAP])
        row_ids = sb("row_ids", [P, CAP])
        eps = sb("eps", [P, 1])
        V_G1, V_CONV, V_QG, V_KG = 0, KT, KT + CW * CT, KT + CW * CT + 1
        V_STATE = V_KG + 1
        NV = V_STATE + (CW - 1) * CT
        vec_rows = sb("vec_rows", [NV, P])
        vec = sb("vec", [P, NV])
        sink_row = sb("sink_row", [P, NH])
        sink = sb("sink", [P, NH // 2])
        b_rt = sb("b_rt", [P, NE])
        b_dn = sb("b_dn", [NE, D])
        b_guT = sb("b_guT", [P, 2 * FT, NE])

        x = sb("x", [P, NT, D])
        hn = sb("hn", [P, NT, D])
        mixT = sb("mixT", [P, MIX, TOK])
        junk = mixT[:, :, :].rearrange("p m t -> p (m t)")[:, 0:D]
        ck_nat = sb("ck_nat", [P, KV])
        ckT = sb("ckT", [P, P])
        cv_nat = sb("cv_nat", [P, KV])
        qk_room = qk_sq[:, :, :].rearrange("p a t -> p (a t)")
        probs = qk_room[:, 0:4 * 256].rearrange("p (b k) -> p b k", b=4)
        cv = qk_room[:, 4 * 256:4 * 256 + UW - (CW - 1)]
        u_out = probsT[0:CW - 1, :, :]
        smx = sb("smx", [P, 8, 4])
        st = sb("st", [P, 4, NT])

        lg = sb("lg", [P, NT, NE])
        top8 = sb("top8", [P, NT, 8])
        top4 = sb("top4", [P, NT, 8])
        left = sb("left", [P, NT, NE])
        sel = sb("sel", [P, NT, NE])
        neg_top = sb("neg_top", [P, NT])
        gates = sb("gates", [P, NT, NE])
        gatesT = mixT[0:NE, :, :].rearrange("p m t -> p (m t)")[:, 0:NT * P]
        gsum = sb("gsum", [P, NT])
        rank = sb("rank", [P, NT, NE])
        counts = sb("counts", [P, NE], I32)
        most = sb("most", [P, 1])
        most_i = sb("most_i", [P, 1], I32)
        gate_col = sb("gate_col", [P, NT, 2])
        gate_row = sb("gate_row", [P, 2])

        x_in = [sem(f"x_in{t}") for t in range(2)]
        wqkv_in, wch_in, wb_in, wo_in = sem("wqkv_in"), sem("wch_in"), sem("wb_in"), sem("wo_in")
        vec_in, bias_in, cache_in, bcast_in, wrt_in = (sem(n) for n in (
            "vec_in", "bias_in", "cache_in", "bcast_in", "wrt_in"))
        raw_in = [sem(f"raw_in{q}") for q in range(RAW)]
        hi_done, split_done, chunk_used = sem("hi_done"), sem("split_done"), sem("chunk_used")
        kv_stored = sem("kv_stored")
        y_stored = sem("y_stored")
        zeroed, consts, eps_set, heads_set = sem("zeroed"), sem("consts"), sem("eps_set"), sem("heads_set")
        router_set, conv_pad = sem("router_set"), sem("conv_pad")
        x_sumsq, x_std, x_rstd, x_scaled = (sem(n) for n in ("x_sumsq", "x_std", "x_rstd", "x_scaled"))
        vec_turned, vec_ready = sem("vec_turned"), sem("vec_ready")
        bias_turned, bias_ready = sem("bias_turned"), sem("bias_ready")
        x_turned, xnT_ready = sem("x_turned"), sem("xnT_ready")
        qk_done, qk_squared, head_ss, head_std, head_rstd, qk_ready = (sem(n) for n in (
            "qk_done", "qk_squared", "head_ss", "head_std", "head_rstd", "qk_ready"))
        v_done, v_ready = sem("v_done"), sem("v_ready")
        bch_done, c_copied, u_ready, cv_step, conv_mixed = (sem(n) for n in (
            "bch_done", "c_copied", "u_ready", "cv_step", "conv_mixed"))
        sink_set, scores_done, smx_step, smx_neg, exp_done, probs_ready = (sem(n) for n in (
            "sink_set", "scores_done", "smx_step", "smx_neg", "exp_done", "probs_ready"))
        probs_turned, probsT_ready, att_done, att_mixed = (sem(n) for n in (
            "probs_turned", "probsT_ready", "att_done", "att_mixed"))
        k_turned, k_out_ready, u_turned, u_out_ready = (sem(n) for n in (
            "k_turned", "k_out_ready", "u_turned", "u_out_ready"))
        out_done, h_ready, h_sumsq, h_std, h_rstd, hn_ready = (sem(n) for n in (
            "out_done", "h_ready", "h_sumsq", "h_std", "h_rstd", "hn_ready"))
        hn_turned, hnT_ready, logits_done = sem("hn_turned"), sem("hnT_ready"), sem("logits_done")
        route, top_ready, gexp_done, sel_ready, ranked, rank_ready = (sem(n) for n in (
            "route", "top_ready", "gexp_done", "sel_ready", "ranked", "rank_ready"))
        counts_ready = sem("counts_ready")
        oh_ready, oh_turned, ohT_ready = sem("oh_ready"), sem("oh_turned"), sem("ohT_ready")
        gathered, xh_ready, xl_ready = sem("gathered"), sem("xh_ready"), sem("xl_ready")
        gates_turned, gatesT_ready, b_spread, b_added = (sem(n) for n in (
            "gates_turned", "gatesT_ready", "b_spread", "b_added"))
        gu_copied, folded = sem("gu_copied"), sem("folded")
        g_biased, g_ready, u_biased, u_clipped, sig_ready, gs_ready, h_ready2, hh_ready, he_ready = (
            sem(n) for n in ("g_biased", "g_ready", "u_biased", "u_clipped", "sig_ready", "gs_ready",
                             "hidden_ready", "hh_ready", "he_ready"))
        yh_ready, yl_ready = sem("yh_ready"), sem("yl_ready")
        scattered, added = sem("scattered"), sem("added")
        rows_moved, round_set = sem("rows_moved"), sem("round_set")
        y_ready = sem("y_ready")

        B_VEC = 5
        XT_BANK = [(0, 1), (2, 3), (4,)]
        QK_BANK = [3, 4, 5, 0, 1]
        V_BANK = 2
        SS_BANK = [6, 7]
        BCH_BANK = [3, 4, 5]
        SC = ps[:, 6:8, :].rearrange("p a (b k) -> p (a b) k", b=2)
        PT = ps[:, 0:2, :]
        AO = ps[:, 2, 0:256]
        KO = ps[:, 2, 256:512].rearrange("p (a n) -> p a n", a=2)
        OUT_BANK = [(3, 4), (5, 6), (7, 2)]
        LG = ps[:, 3:3 + NT, 0:NE]
        RK = ps[:, 6, 0:(NT + 1) * NE].rearrange("p (t e) -> p t e", t=NT + 1)
        GU = ps[:, 0:4, :]
        XE = ps[:, 0:2, :].rearrange("p a (k c) -> p (a k) c", c=2 * CAP)
        TU = ps[:, 4:6, :].rearrange("p a (f c) -> p a f c", c=CAP)
        OT = ps[:, 4:6, :]
        Y = ps[:, 6:8, :].rearrange("p a n -> p (a n)")

        gu_dram = w_gu.rearrange("l e (k p) f -> (l e) k p f", p=P)
        dn_dram = w_down.rearrange("l e (m a p) n -> (l e) m p a n", a=FPC, p=P)

        LAST = CH * NE + DNC

        class Chunk:
            def __init__(self, e, c):
                self.e, self.c = e, c
                if isinstance(e, int):
                    even, par = e - e % 2, e % 2
                    place = CH * e + c + (DNC if e == 0 else 0) - (GUC if e == NE else 0)
                    assert DNC <= place < LAST
                    self.raw, self.split = place % RAW, place % SPLIT
                    turn = place // RAW
                    self.nth = place - DNC
                else:
                    i, par = e
                    self.e = 2 * i + par
                    self.raw, self.split = (CH * par + c) % RAW, (CH * par + c) % SPLIT
                    turn = i * (2 * CH // RAW) + (CH * par + c) // RAW
                    self.nth = i * (2 * CH) + (CH * par + c - DNC)
                self.arrivals = turn + 1 - (1 if self.raw < DNC else 0)
                self.reload = isinstance(e, tuple) or self.nth >= RAW
                self.resplit = isinstance(e, tuple) or self.nth >= SPLIT
                self.free_raw = self.nth - RAW + 1
                self.free_split = self.nth - SPLIT + 1

        class LateChunk:

            def __init__(self, n, e, c):
                self.e, self.raw, self.split = e, c % RAW, c % SPLIT
                self.nth = CH * n + c
                self.reload = self.resplit = True
                full = CH * NE // RAW
                self.arrivals = (n - NE) * 2 + full + c // RAW + 1 if self.raw < CH - RAW else n - NE + full + 1
                self.free_raw = self.nth - RAW + 1 if c >= RAW else CH * n
                self.free_split = self.nth - SPLIT + 1
                self.c = c

        def slot(ring, q):
            return ring[:, (q - DNC) % RAW, :]

        in_dram = w_in.rearrange("l (k p) n -> p (l k) n", p=P)

        def key_window(c):
            if c == SAMPLE:
                return 0, WIN + DEC
            first = max(0, c - WIN // CHUNK)
            return (first % 2) * CHUNK, (c + 1 - first) * CHUNK

        def further_rounds(eng, step, each_round=None):
            eng.wait_ge(counts_ready, 2)
            top = eng.value_load(most_i[0:1, 0:1], min_val=0, max_val=TOK)
            with eng.If(top > CAP):
                n_reg = eng.alloc_register("n_block_" + str(eng.engine).split(".")[-1])
                eng.reg_mov(n_reg, NE)
                with eng.Fori(1, ROUNDS) as q:
                    if each_round:
                        each_round(q)
                    with eng.Fori(0, NE) as e:
                        have = eng.value_load(counts[0:1, bass.ds(e, 1)], min_val=0, max_val=TOK)
                        with eng.If(have > q * CAP):
                            n = eng.snap(n_reg, min_val=NE, max_val=NE * ROUNDS)
                            step(n, e)
                            eng.reg_add(n_reg, n_reg, 1)

        block = ctx.enter_context(nc.Block())

        @block.sync
        def _(sp):
            def load(ch):
                if ch.reload:
                    sp.wait_ge(split_done, ch.free_raw)
                if ch.c < GUC:
                    src, dst = gu_dram[ch.e, ch.c], slot(raw, ch.raw)
                else:
                    src = dn_dram[ch.e, ch.c - GUC]
                    dst = slot(raw, ch.raw).rearrange("p (a n) -> p a n", a=FPC)
                sp.dma_start(dst, src).then_inc(raw_in[ch.raw], 16)

            def step_loads(e, which=range(CH)):
                for c in which:
                    ch = Chunk(e, c)
                    if c >= GUC:
                        ch.e = ch.e - 1
                    load(ch)

            sp.dma_start(x[:, 0:2, :], x_prompt.rearrange("b (t p) d -> p (b t) d", p=P)).then_inc(x_in[0], 16)
            sp.dma_start(x[0:DEC, 2, :], x_sample[0]).then_inc(x_in[1], 16)
            sp.dma_start(w_qkv[:, :, :], in_dram[:, :, 0:QKV]).then_inc(wqkv_in, 16)
            sp.dma_start(w_bch[:, :, CONV:3 * CONV], in_dram[:, :, QKV + CONV:IN_DIM]).then_inc(wch_in, 16)
            sp.dma_start(w_bch[:, :, 0:CONV], in_dram[:, :, QKV:QKV + CONV]).then_inc(wb_in, 16)
            sp.wait_ge(bias_turned, 1)
            for g in range(2):
                sp.dma_start(w_o[g * HEAD_DIM:(g + 1) * HEAD_DIM, 0:QT, :],
                             w_out[0, g * ATT // 2:(g + 1) * ATT // 2, :].rearrange("(j p) n -> p j n", p=HEAD_DIM)
                             ).then_inc(wo_in, 16)
            sp.dma_start(w_o[:, QT:MIX, :],
                         w_out[0, ATT:ATT + CONV, :].rearrange("(j p) n -> p j n", p=P)).then_inc(wo_in, 16)
            step_loads(0, range(2))
            sp.wait_ge(bch_done, 3 * CT)
            step_loads(0, range(2, GUC))
            step_loads(1)
            with sp.Fori(1, PAIRS) as i:
                step_loads((i, 0))
                step_loads((i, 1))
            step_loads(NE, range(GUC, CH))

            def again(n, e):
                for c in range(CH):
                    load(LateChunk(n, e, c))

            further_rounds(sp, again)

            sp.wait_ge(y_ready, 1)
            sp.dma_start(y_prompt.rearrange("b (t p) d -> p (b t) d", p=P), x[:, 0:2, :]).then_inc(y_stored, 16)
            sp.dma_start(y_sample[0], x[0:DEC, 2, :]).then_inc(y_stored, 16)
            sp.wait_ge(y_stored, 32)
            sp.wait_ge(kv_stored, 8 * 16)

        @block.gpsimd
        def _(pool):
            rows = vec_rows
            pool.dma_start(rows[V_G1:V_G1 + KT, :], norm1_g.rearrange("l (k p) -> (l k) p", p=P)).then_inc(vec_in, 16)
            pool.dma_start(rows[V_CONV:V_CONV + CW * CT, :],
                           conv_w.rearrange("l w (c p) -> (l w c) p", p=P)).then_inc(vec_in, 16)
            for g in range(2):
                half = slice(g * HEAD_DIM, (g + 1) * HEAD_DIM)
                pool.dma_start(rows[V_QG:V_QG + 1, half], q_norm_g).then_inc(vec_in, 16)
                pool.dma_start(rows[V_KG:V_KG + 1, half], k_norm_g).then_inc(vec_in, 16)
            pool.dma_start(rows[V_STATE:NV, :],
                           state_conv.rearrange("l b r (c p) -> (l b r c) p", p=P)).then_inc(vec_in, 16)
            pool.dma_start(ck_nat[:, :], cache_k[0, 0].rearrange("t h d -> t (h d)")).then_inc(cache_in, 16)
            pool.memset(ident[:, :], 0.0).then_inc(zeroed, 1)
            pool.memset(ones[:, :], 1.0).then_inc(zeroed, 1)
            pool.wait_ge(zeroed, 2)
            pool.affine_select(out=ident[:, :], in_=ident[:, :], compare_op=ALU.not_equal, fill=1.0,
                               base=0, pattern=[[-1, P]], channel_multiplier=1).then_inc(consts, 1)
            pool.affine_select(out=before[:, :], in_=ones[:, :], compare_op=ALU.is_gt, fill=0.0,
                               base=0, pattern=[[1, P]], channel_multiplier=-1).then_inc(consts, 1)
            pool.iota(row_ids[:, :], pattern=[[1, CAP]], base=0, channel_multiplier=0,
                      allow_small_or_imprecise_dtypes=True).then_inc(consts, 1)
            pool.dma_start(bias_rows[:, :], b_gu[0]).then_inc(bias_in, 16)
            pool.dma_start(b_dn[:, :], b_down[0]).then_inc(bias_in, 16)
            pool.dma_start(sink_row[:, :], sinks.to_broadcast([P, NH])).then_inc(bcast_in, 16)
            pool.dma_start(cv_nat[:, :], cache_v[0, 0].rearrange("t h d -> t (h d)")).then_inc(cache_in, 16)
            pool.wait_ge(v_done, 1)
            pool.dma_start(g2[:, :], norm2_g.to_broadcast([P, D])).then_inc(bcast_in, 16)
            pool.dma_start(b_rt[:, :], b_router.to_broadcast([P, NE])).then_inc(bcast_in, 16)
            pool.dma_start(w_rt[:, :, :], w_router.rearrange("l (k p) e -> p (l k) e", p=P)).then_inc(wrt_in, 16)

            roll = WIN - DEC
            rows_of = lambda a: a[0, 0].rearrange("t h d -> t (h d)")
            pool.wait_ge(cache_in, 32)
            pool.dma_start(rows_of(new_k_sample)[0:roll, :], ck_nat[DEC:WIN, :]).then_inc(kv_stored, 16)
            pool.dma_start(rows_of(new_v_sample)[0:roll, :], cv_nat[DEC:WIN, :]).then_inc(kv_stored, 16)
            pool.wait_ge(v_ready, 2)
            pool.dma_start(rows_of(new_v_prompt), v_nat[:, 1, :]).then_inc(kv_stored, 16)
            pool.dma_start(rows_of(new_v_sample)[roll:WIN, :], v_nat[0:DEC, 2, :]).then_inc(kv_stored, 16)
            pool.wait_ge(k_out_ready, 2)
            pool.dma_start(rows_of(new_k_prompt), k_out[:, 0, :]).then_inc(kv_stored, 16)
            pool.dma_start(rows_of(new_k_sample)[roll:WIN, :], k_out[0:DEC, 1, :]).then_inc(kv_stored, 16)
            pool.wait_ge(u_out_ready, 2)
            pool.dma_start(new_conv_prompt[0, 0], u_out[:, 0, :]).then_inc(kv_stored, 16)
            pool.dma_start(new_conv_sample[0, 0], u_out[:, 1, :]).then_inc(kv_stored, 16)

        @block.tensor
        def _(pe):
            mm = nc.tensor.matmul

            pe.wait_ge(consts, 3)
            pe.wait_ge(vec_in, 16 * 7)
            nc.tensor.transpose(ps[:, B_VEC, 0:NV], vec_rows[:, :], ident[0:NV, 0:NV]).then_inc(vec_turned, 1)
            pe.wait_ge(cache_in, 32)
            nc.tensor.transpose(ps[:, B_VEC, P:2 * P], ck_nat[:, :], ident[:, :]).then_inc(vec_turned, 1)

            for t, (_, n) in enumerate(TT):
                pe.wait_ge(x_scaled, t + 1)
                per = KT // len(XT_BANK[t])
                for k in range(KT):
                    out = ps[:, XT_BANK[t][k // per], (k % per) * n:(k % per + 1) * n]
                    last = nc.tensor.transpose(out, hn[0:n, t, k * P:(k + 1) * P], ident[0:n, 0:n])
                last.then_inc(x_turned, 1)

            pe.wait_ge(bias_in, 32)
            for f in range(2 * FT):
                last = nc.tensor.transpose(ps[:, 6, f * NE:(f + 1) * NE], bias_rows[:, f * P:(f + 1) * P],
                                           ident[0:NE, 0:NE])
            last.then_inc(bias_turned, 1)

            pe.wait_ge(xnT_ready, len(TT) + 2)
            pe.wait_ge(wqkv_in, 16)

            def sum_squares(i):
                pe.wait_ge(qk_squared, i + 1)
                if i == 0:
                    pe.wait_ge(heads_set, 5)
                if i < 2:
                    pe.wait_ge(bias_ready, 1)
                else:
                    pe.wait_ge(head_std, i - 1)
                mm(ps[:, SS_BANK[i % 2], 0:TOK], head_ones[:, :], qk_sq[:, i, :], start=True, stop=True
                   ).then_inc(head_ss, 1)

            for i in range(1 + QT):
                if i == 2:
                    pe.wait_ge(vec_ready, 2)
                for k in range(KT):
                    cols = w_qkv[:, k, ATT:ATT + KV] if i == 0 else w_qkv[:, k, (i - 1) * P:i * P]
                    last = mm(ps[:, QK_BANK[i], 0:TOK], cols, xnT[:, k, :], start=(k == 0), stop=(k == KT - 1))
                last.then_inc(qk_done, 1)
                if i >= 1:
                    sum_squares(i - 1)
            for t, (t0, n) in enumerate(TT):
                for k in range(KT):
                    last = mm(ps[0:n, V_BANK, t * P:t * P + KV], xnT[:, k, t0:t0 + n], w_qkv[:, k, ATT + KV:QKV],
                              start=(k == 0), stop=(k == KT - 1))
            last.then_inc(v_done, 1)
            sum_squares(QT)

            def scores(c):
                if c == 0:
                    pe.wait_ge(qk_ready, 1 + QT)
                    pe.wait_ge(head_std, 1 + QT)
                else:
                    pe.wait_ge(exp_done, 5 * c)
                off, n = key_window(c)
                for b in range(4):
                    g, jp = b // 2, b % 2
                    half = slice(g * HEAD_DIM, (g + 1) * HEAD_DIM)
                    qs = qT[half, c, 2 * jp:2 * jp + 2, :].rearrange("p a t -> p (a t)")
                    if c == SAMPLE:
                        mm(SC[:, b, 0:WIN], qs, ckT[half, :], start=True, stop=True)
                        last = mm(SC[:, b, WIN:WIN + DEC], qs, kT[half, SEQ:TOK], start=True, stop=True)
                    else:
                        last = mm(SC[:, b, off:off + n], qs, kT[half, (c + 1) * CHUNK - n:(c + 1) * CHUNK],
                                  start=True, stop=True)
                last.then_inc(scores_done, 1)

            def key_tiles(c):
                off, n = key_window(c)
                parts = [(0, off, min(P, off + n))]
                if off + n > P:
                    parts.append((1, 0, off + n - P))
                return parts

            def turn_probs(c):
                pe.wait_ge(probs_ready, c + 1)
                if c >= 1:
                    pe.wait_ge(probsT_ready, c)
                if c == 0:
                    pe.wait_ge(qk_ready, 1 + QT)
                for b in range(4):
                    for tile, _, k1 in key_tiles(c):
                        last = nc.tensor.transpose(PT[0:k1, tile, b * P:(b + 1) * P],
                                                   probs[:, b, tile * P:tile * P + k1], ident[:, :])
                last.then_inc(probs_turned, 1)

            def attend(c):
                pe.wait_ge(probsT_ready, c + 1)
                pe.wait_ge(v_ready, 2)
                if c >= 1:
                    pe.wait_ge(att_mixed, c)
                parts = key_tiles(c)
                for b in range(4):
                    g, jp = b // 2, b % 2
                    cols = slice(g * HEAD_DIM, (g + 1) * HEAD_DIM)
                    for i, (tile, k0, k1) in enumerate(parts):
                        if c == SAMPLE:
                            vals = cv_nat[:, cols] if tile == 0 else v_nat[0:k1, 2, cols]
                        else:
                            vals = v_nat[k0:k1, tile, cols]
                        last = mm(AO[cols, jp * P:(jp + 1) * P], vals, probsT[k0:k1, tile, b * P:(b + 1) * P],
                                  start=(i == 0), stop=(i == len(parts) - 1))
                last.then_inc(att_done, 1)

            def turn_keys():
                pe.wait_ge(v_ready, 2)
                nc.tensor.transpose(KO[:, 0, :], kT[:, SEQ - WIN:SEQ], ident[:, :])
                nc.tensor.transpose(KO[0:DEC, 1, :], kT[:, SEQ:TOK], ident[:, :]).then_inc(k_turned, 1)

            for n in range(3 * CT):
                j, part = n // 3, n % 3
                if n == 0:
                    pe.wait_ge(wch_in, 16)
                if n == 2:
                    pe.wait_ge(wb_in, 16)
                if n < 3:
                    pe.wait_ge(qk_ready, n + 1)
                elif part == 0:
                    pe.wait_ge(c_copied, j)
                elif part == 1:
                    pe.wait_ge(u_ready, j)
                else:
                    pe.wait_ge(conv_mixed, j)
                col = (CONV, 2 * CONV, 0)[part] + j * P
                for k in range(KT):
                    last = mm(ps[:, BCH_BANK[part], 0:TOK], w_bch[:, k, col:col + P], xnT[:, k, :],
                              start=(k == 0), stop=(k == KT - 1))
                last.then_inc(bch_done, 1)
                if n % 2 == 0:
                    if n // 2 >= 1:
                        turn_probs(n // 2 - 1)
                    if n // 2 < NCH:
                        scores(n // 2)
                elif n >= 3:
                    attend((n - 3) // 2)
                else:
                    turn_keys()
            pe.wait_ge(u_ready, CT)
            pe.wait_ge(probsT_ready, NCH)
            for s, at in enumerate((SEQ, UW - (CW - 1))):
                for j in range(CT):
                    last = nc.tensor.transpose(ps[0:CW - 1, s, j * P:(j + 1) * P], uT[:, j, at:at + CW - 1],
                                               ident[:, :])
            last.then_inc(u_turned, 1)

            pe.wait_ge(wo_in, 48)

            def project_out(t):
                t0, n = TT[t]
                if t == 0:
                    pe.wait_ge(att_mixed, NCH)
                    pe.wait_ge(conv_mixed, CT)
                for half in range(2):
                    for j in range(MIX):
                        last = mm(ps[0:n, OUT_BANK[t][half], :], mixT[:, j, t0:t0 + n],
                                  w_o[:, j, half * HALF:(half + 1) * HALF], start=(j == 0), stop=(j == MIX - 1))
                    last.then_inc(out_done, 1)

            def logits(t):
                _, n = TT[t]
                pe.wait_ge(hn_ready, t + 1)
                if t == 0:
                    pe.wait_ge(u_out_ready, 2)
                    pe.wait_ge(wrt_in, 16)
                else:
                    pe.wait_ge(hnT_ready, t)
                for k in range(KT):
                    out = ps[:, k // 4, (k % 4) * P:(k % 4) * P + n]
                    last = nc.tensor.transpose(out, hn[0:n, t, k * P:(k + 1) * P], ident[0:n, 0:n])
                last.then_inc(hn_turned, 1)
                pe.wait_ge(hnT_ready, t + 1)
                for k in range(KT):
                    last = mm(LG[0:n, t, :], hnT[:, k, 0:n], w_rt[:, k, :], start=(k == 0), stop=(k == KT - 1))
                last.then_inc(logits_done, 1)

            project_out(0)
            project_out(1)
            logits(0)
            project_out(2)
            logits(1)
            logits(2)

            pe.wait_ge(sel_ready, 1)
            for t in range(NT + 1):
                for s in range(min(t, NT - 1) + 1):
                    last = mm(RK[:, t, :], before[:, :] if s == t else ones[:, :], sel[:, s, :],
                              start=(s == 0), stop=(s == min(t, NT - 1)))
            last.then_inc(ranked, 1)

            def gather(i):
                pe.wait_ge(oh_ready, i + 1)
                for k in range(KT):
                    for t, (_, m) in enumerate(TT):
                        last = mm(XE[:, k, :], hn[0:m, t, k * P:(k + 1) * P], oh[0:m, t, :, 0, :],
                                  start=(t == 0), stop=(t == NT - 1))
                last.then_inc(gathered, 1)

            def gate_up(chunks, s):
                for k, ch in enumerate(chunks):
                    pe.wait_ge(split_done, ch.nth + 1)
                    for w in (w_hi, w_lo):
                        for n in range(FLAT // 512):
                            last = mm(GU[:, n, :], xhl[:, s, k, :], w[:, ch.split, n * 512:(n + 1) * 512],
                                      start=(k == 0 and w is w_hi), stop=(k == KT - 1 and w is w_lo),
                                      skip_group_check=True)
                    last.then_inc(chunk_used, 1)

            def down(n, chunks):
                pe.wait_ge(he_ready, n + 1)
                for m, ch in enumerate(chunks):
                    pe.wait_ge(split_done, ch.nth + 1)
                    for a in range(FPC):
                        for w in (w_hi, w_lo):
                            for half in range(2):
                                at = a * D + half * HALF
                                last = mm(Y[:, half * HALF:(half + 1) * HALF], he[:, FPC * m + a, :],
                                          w[:, ch.split, at:at + HALF], start=(m == 0 and a == 0 and w is w_hi),
                                          stop=(m == DNC - 1 and a == FPC - 1 and w is w_lo),
                                          skip_group_check=True)
                    last.then_inc(chunk_used, 1)

            def fold_gu(n):
                pe.wait_ge(gu_copied, n + 1)
                for f in range(2 * FT):
                    last = mm(TU[:, f // FT, f % FT, :], gu_sb[:, f * P:(f + 1) * P], fold[:, :],
                              start=True, stop=True)
                last.then_inc(folded, 1)

            def turn_oh(i, experts=(0, 1)):
                pe.wait_ge(oh_ready, i + 1)
                for s in experts:
                    for t in range(NT):
                        nc.tensor.transpose(OT[:, s, t * P:(t + 1) * P],
                                            oh[:, t, s, :, :].rearrange("p a c -> p (a c)"), ident[:, :])
                    for t in range(NT):
                        last = mm(OT[:, s, NT * P:NT * P + 1], oh[:, t, s, :, :].rearrange("p a c -> p (a c)"),
                                  gate_col[:, t, s:s + 1], start=(t == 0), stop=(t == NT - 1))
                last.then_inc(oh_turned, 1)

            def scatter(i, experts=(0, 1)):
                pe.wait_ge(ohT_ready, i + 1)
                for u in range(2 * NT):
                    t, half = u // 2, u % 2
                    if u >= 2:
                        pe.wait_ge(added, 2 * NT * i + u - 1)
                    for s in experts:
                        for y in (y_hi, y_lo):
                            last = mm(ps[:, 6 + half, :], ohT[:, s, t * P:(t + 1) * P],
                                      y[:, s, half * HALF:(half + 1) * HALF],
                                      start=(s == 0 and y is y_hi), stop=(s == experts[-1] and y is y_lo))
                    last.then_inc(scattered, 1)

            def chunks_of(e, which):
                return [Chunk(e, c) for c in which]

            def even(i, e, step):
                if not isinstance(i, int) or i > 0:
                    pe.wait_ge(gu_copied, e)
                pe.wait_ge(xl_ready, i + 1)
                gate_up(chunks_of(step, range(GUC)), 0)
                if not isinstance(i, int) or i > 0:
                    pe.wait_ge(yl_ready, e - 1)
                    down(e - 1, chunks_of(step, range(GUC, CH)))
                    pe.wait_ge(u_biased, e)
                    fold_gu(e)
                    pe.wait_ge(yl_ready, e)
                    scatter(i - 1)

            def odd(i, e, step, last=False):
                pe.wait_ge(gu_copied, e)
                gate_up(chunks_of(step, range(GUC)), 1)
                pe.wait_ge(u_biased, e)
                turn_oh(i)
                if not isinstance(i, int) or i > 0:
                    pe.wait_ge(added, 2 * NT * i)
                else:
                    pe.wait_ge(b_added, 2 * NT)
                down(e - 1, chunks_of(step, range(GUC, CH)))
                if not last:
                    pe.wait_ge(gu_copied, e + 1)
                    gather(i + 1)
                pe.wait_ge(ohT_ready, i + 1)
                fold_gu(e)

            def spread_b_down():
                pe.wait_ge(gatesT_ready, 1)
                for u in range(2 * NT):
                    t, half = u // 2, u % 2
                    t0, m = t * P, TT[t][1]
                    if u >= 2:
                        pe.wait_ge(b_added, u - 1)
                    mm(ps[0:m, 6 + half, :], gatesT[:, t0:t0 + m], b_dn[:, half * HALF:(half + 1) * HALF],
                       start=True, stop=True).then_inc(b_spread, 1)

            pe.wait_ge(rank_ready, 1)
            gather(0)
            for t in range(NT):
                last = nc.tensor.transpose(ps[0:NE, 7, t * P:(t + 1) * P], gates[:, t, :], ident[:, :])
            last.then_inc(gates_turned, 1)
            even(0, 0, 0)
            spread_b_down()
            fold_gu(0)
            odd(0, 1, 1)
            with pe.Fori(1, PAIRS - 1) as i:
                even(i, 2 * i, (i, 0))
                odd(i, 2 * i + 1, (i, 1))
            even(PAIRS - 1, NE - 2, NE - 2)
            odd(PAIRS - 1, NE - 1, NE - 1, last=True)
            pe.wait_ge(yl_ready, NE - 1)
            down(NE - 1, chunks_of(NE, range(GUC, CH)))
            pe.wait_ge(yl_ready, NE)
            scatter(PAIRS - 1)

            def again(n, e):
                i = n - NE + PAIRS
                pe.wait_ge(added, 2 * NT * i)
                gather(i)
                turn_oh(i, (0,))
                pe.wait_ge(xl_ready, i + 1)
                gate_up([LateChunk(n, e, c) for c in range(GUC)], 0)
                pe.wait_ge(ohT_ready, i + 1)
                fold_gu(n)
                down(n, [LateChunk(n, e, c) for c in range(GUC, CH)])
                pe.wait_ge(yl_ready, n + 1)
                scatter(i, (0,))

            further_rounds(pe, again)

        @block.scalar
        def _(act):
            A = nc.scalar.activation
            act.wait_ge(eps_set, 1)
            for t, (_, n) in enumerate(TT):
                act.wait_ge(x_in[t // 2], 16)
                if t:
                    act.wait_ge(x_sumsq, t)
                A(junk[0:n, :], x[0:n, t, :], ACT.Square, accum_out=st[0:n, 0, t:t + 1]).then_inc(x_sumsq, 1)
                act.wait_ge(x_sumsq, t + 1)
                A(st[0:n, 1, t:t + 1], st[0:n, 0, t:t + 1], ACT.Sqrt, bias=eps[0:n, :], scale=1.0 / D
                  ).then_inc(x_std, 1)

            act.wait_ge(bias_turned, 1)
            nc.scalar.copy(b_guT[:, :, :].rearrange("p f e -> p (f e)"), ps[:, 6, :]).then_inc(bias_ready, 1)

            def square_head(i):
                act.wait_ge(qk_done, i + 1)
                A(qk_sq[:, i, :], ps[:, QK_BANK[i], 0:TOK], ACT.Square).then_inc(qk_squared, 1)

            def root_head(i):
                act.wait_ge(head_ss, i + 1)
                A(qk_sq[:, i, :], ps[:, SS_BANK[i % 2], 0:TOK], ACT.Sqrt, bias=eps[:, :], scale=1.0 / HEAD_DIM
                  ).then_inc(head_std, 1)

            for i in range(1 + QT):
                square_head(i)
                if i:
                    root_head(i - 1)
            act.wait_ge(v_done, 1)
            nc.scalar.copy(v_nat[:, 0:2, :].rearrange("p t n -> p (t n)"), ps[:, V_BANK, 0:2 * P]).then_inc(v_ready, 1)
            nc.scalar.copy(v_nat[0:DEC, 2, :], ps[0:DEC, V_BANK, 2 * P:3 * P]).then_inc(v_ready, 1)
            root_head(QT)

            def exps(c):
                off, n = key_window(c)
                act.wait_ge(smx_neg, 2 * (c + 1))
                for b in range(4):
                    A(probs[:, b, off:off + n], SC[:, b, off:off + n], ACT.Exp, bias=smx[:, 2, b:b + 1],
                      scale=HEAD_DIM ** -0.5, accum_out=smx[:, 4, b:b + 1]).then_inc(exp_done, 1)
                A(smx[:, 5, :], smx[:, 3, :], ACT.Exp).then_inc(exp_done, 1)

            def copy_probsT(c):
                off, n = key_window(c)
                act.wait_ge(probs_turned, c + 1)
                if c >= 1:
                    act.wait_ge(att_done, c)
                lo = min(P, off + n)
                last = nc.scalar.copy(probsT[0:lo, 0, :], PT[0:lo, 0, :])
                if off + n > P:
                    last = nc.scalar.copy(probsT[0:off + n - P, 1, :], PT[0:off + n - P, 1, :])
                last.then_inc(probsT_ready, 1)

            for n in range(3 * CT):
                if n % 3 == 0:
                    act.wait_ge(bch_done, n + 1)
                    if n:
                        act.wait_ge(u_ready, n // 3)
                    nc.scalar.copy(c_sb[:, :], ps[:, BCH_BANK[0], 0:TOK]).then_inc(c_copied, 1)
                if n % 2 == 0:
                    if n // 2 >= 1:
                        copy_probsT(n // 2 - 1)
                    if n // 2 < NCH:
                        exps(n // 2)
                elif n == 1:
                    act.wait_ge(k_turned, 1)
                    nc.scalar.copy(k_out[:, 0, :], KO[:, 0, :]).then_inc(k_out_ready, 1)
                    nc.scalar.copy(k_out[0:DEC, 1, :], KO[0:DEC, 1, :]).then_inc(k_out_ready, 1)
            act.wait_ge(u_turned, 1)
            for s in range(2):
                nc.scalar.copy(u_out[:, s, :], ps[0:CW - 1, s, :]).then_inc(u_out_ready, 1)

            def rms_h(t):
                _, n = TT[t]
                act.wait_ge(h_ready, 2 * (t + 1))
                if t:
                    act.wait_ge(h_sumsq, t)
                A(junk_h[0:n, :], x[0:n, t, :], ACT.Square, accum_out=st[0:n, 0, t:t + 1]).then_inc(h_sumsq, 1)
                act.wait_ge(h_sumsq, t + 1)
                A(st[0:n, 1, t:t + 1], st[0:n, 0, t:t + 1], ACT.Sqrt, bias=eps[0:n, :], scale=1.0 / D
                  ).then_inc(h_std, 1)

            def copy_hnT(t):
                _, n = TT[t]
                act.wait_ge(hn_turned, t + 1)
                if t:
                    act.wait_ge(logits_done, t)
                nc.scalar.copy(hnT[:, :, 0:n], ps[:, 0:2, :].rearrange("p a (k t) -> p (a k) t", t=P)[:, :, 0:n]
                               ).then_inc(hnT_ready, 1)

            rms_h(0)
            rms_h(1)
            copy_hnT(0)
            rms_h(2)
            copy_hnT(1)
            copy_hnT(2)
            act.wait_ge(top_ready, 1)
            for t in range(NT):
                A(gates[:, t, :], lg[:, t, :], ACT.Exp, bias=neg_top[:, t:t + 1]).then_inc(gexp_done, 1)

            def split_hi(ch):
                act.wait_ge(raw_in[ch.raw], 16 * ch.arrivals)
                if ch.resplit:
                    act.wait_ge(chunk_used, ch.free_split)
                nc.scalar.copy(w_hi[:, ch.split, :], slot(raw, ch.raw)).then_inc(hi_done, 1)

            def split_xh(i, experts=(0, 1)):
                act.wait_ge(gathered, i + 1)
                for s in experts:
                    last = nc.scalar.copy(xhl[:, s, :, 0:CAP], XE[:, :, s * CAP:(s + 1) * CAP])
                last.then_inc(xh_ready, 1)

            def copy_gu(n, last_chunk):
                act.wait_ge(chunk_used, last_chunk.nth + 1)
                nc.scalar.copy(gu_sb[:, :], GU.rearrange("p a n -> p (a n)")).then_inc(gu_copied, 1)

            def sigmoid(n):
                act.wait_ge(g_ready, n + 1)
                A(sg[:, :, :], ge[:, :, :], ACT.Sigmoid, scale=ALPHA).then_inc(sig_ready, 1)

            def split_hh(n):
                act.wait_ge(h_ready2, n + 1)
                nc.scalar.copy(he[:, :, 0:CAP], ue[:, :, :]).then_inc(hh_ready, 1)

            def copy_ohT(i, experts=(0, 1)):
                act.wait_ge(oh_turned, i + 1)
                for s in experts:
                    nc.scalar.copy(ohT[:, s, :], OT[:, s, 0:NT * P])
                nc.scalar.copy(gate_row[:, 0:len(experts)], OT[:, 0:len(experts), NT * P]).then_inc(ohT_ready, 1)

            def split_yh(n, s, last_chunk):
                act.wait_ge(chunk_used, last_chunk.nth + 1)
                A(y_hi[:, s, :], Y, ACT.Copy, scale=gate_row[:, s:s + 1]).then_inc(yh_ready, 1)

            def step(e, at, par, nxt, n_first=2, i=None):
                first = isinstance(e, int) and e == 0
                for c in range(n_first, CH if not first else GUC):
                    split_hi(Chunk(at, c))
                    if not first and c == 3:
                        sigmoid(e - 1)
                    if not first and c == 4:
                        split_hh(e - 1)
                    if c == 9 or (first and c == GUC - 1):
                        copy_gu(e, Chunk(at, GUC - 1))
                        if par:
                            copy_ohT(i)
                for c in range(*((0, 2) if nxt != NE else (GUC, GUC + 2))):
                    split_hi(Chunk(nxt, c))
                if not first:
                    split_yh(e - 1, 1 - par, Chunk(at, CH - 1))
                else:
                    act.wait_ge(gates_turned, 1)

            act.wait_ge(rank_ready, 1)
            act.wait_ge(kv_stored, 8 * 16)
            split_hi(Chunk(0, 0))
            split_hi(Chunk(0, 1))
            split_xh(0)
            act.wait_ge(gates_turned, 1)
            nc.scalar.copy(gatesT[:, :], ps[0:NE, 7, 0:NT * P]).then_inc(gatesT_ready, 1)
            step(0, 0, 0, 1)
            step(1, 1, 1, 2, i=0)
            split_xh(1)
            with act.Fori(1, PAIRS - 1) as i:
                step(2 * i, (i, 0), 0, (i, 1))
                step(2 * i + 1, (i, 1), 1, (i + 1, 0), i=i)
                split_xh(i + 1)
            step(NE - 2, NE - 2, 0, NE - 1)
            step(NE - 1, NE - 1, 1, NE, i=PAIRS - 1)
            sigmoid(NE - 1)
            split_hh(NE - 1)
            split_hi(Chunk(NE, GUC + 2))
            split_hi(Chunk(NE, GUC + 3))
            split_yh(NE - 1, 1, Chunk(NE, CH - 1))

            def again(n, e):
                i = n - NE + PAIRS
                act.wait_ge(scattered, 2 * NT * i)
                split_xh(i, (0,))
                copy_ohT(i, (0,))
                for c in range(CH):
                    if c == GUC:
                        copy_gu(n, LateChunk(n, e, GUC - 1))
                        sigmoid(n)
                        split_hh(n)
                    split_hi(LateChunk(n, e, c))
                split_yh(n, 0, LateChunk(n, e, CH - 1))

            further_rounds(act, again)

        @block.vector
        def _(dve):
            V = nc.vector
            V.memset(eps[:, :], EPS).then_inc(eps_set, 1)
            dve.wait_ge(consts, 3)
            for g in range(2):
                half = slice(g * CAP, (g + 1) * CAP)
                V.tensor_copy(fold[half, :], ident[half, half]).then_inc(heads_set, 1)
            V.memset(head_ones[:, :], 0.0).then_inc(heads_set, 1)
            dve.wait_ge(heads_set, 3)
            for g in range(2):
                half = slice(g * HEAD_DIM, (g + 1) * HEAD_DIM)
                V.memset(head_ones[half, half], 1.0).then_inc(heads_set, 1)
            V.memset(lg[:, :, :], 0.0).then_inc(router_set, 1)
            V.memset(top4[:, :, :], NO_LOGIT).then_inc(router_set, 1)
            V.memset(uT[:, :, 0:CW - 1], 0.0).then_inc(conv_pad, 1)
            for t, (_, n) in enumerate(TT):
                dve.wait_ge(x_std, t + 1)
                V.reciprocal(st[0:n, 2, t:t + 1], st[0:n, 1, t:t + 1]).then_inc(x_rstd, 1)
                dve.wait_ge(x_rstd, t + 1)
                V.tensor_scalar(hn[0:n, t, :], x[0:n, t, :], st[0:n, 2, t:t + 1], None, ALU.mult
                                ).then_inc(x_scaled, 1)
            dve.wait_ge(vec_turned, 2)
            V.tensor_copy(vec[:, :], ps[:, B_VEC, 0:NV]).then_inc(vec_ready, 1)
            V.tensor_copy(ckT[:, :], ps[:, B_VEC, P:2 * P]).then_inc(vec_ready, 1)
            dve.wait_ge(vec_ready, 1)
            for t, (t0, n) in enumerate(TT):
                dve.wait_ge(x_turned, t + 1)
                per = KT // len(XT_BANK[t])
                for i, bank in enumerate(XT_BANK[t]):
                    g = vec[:, V_G1 + i * per:V_G1 + (i + 1) * per].unsqueeze(2).to_broadcast([P, per, n])
                    V.tensor_tensor(xnT[:, i * per:(i + 1) * per, t0:t0 + n],
                                    ps[:, bank, 0:per * n].rearrange("p (k t) -> p k t", t=n), g, ALU.mult
                                    ).then_inc(xnT_ready, 1)
            V.tensor_copy(uT[:, :, SEQ + CW - 1:SEQ + 2 * (CW - 1)],
                          vec[:, V_STATE:NV].rearrange("p (r c) -> p c r", r=CW - 1)).then_inc(conv_pad, 1)
            dve.wait_ge(bcast_in, 48)
            for a in range(2):
                half = slice(a * CHUNK, (a + 1) * CHUNK)
                V.tensor_copy(sink[half, :], sink_row[half, :].rearrange("p (b a) -> p a b", a=2)[:, a, :]
                              ).then_inc(sink_set, 1)

            for i in range(1 + QT):
                dve.wait_ge(head_std, i + 1)
                V.reciprocal(qk_sq[:, i, :], qk_sq[:, i, :]).then_inc(head_rstd, 1)
                dve.wait_ge(head_rstd, i + 1)
                if i == 0:
                    V.scalar_tensor_tensor(out=kT[:, :], in0=ps[:, QK_BANK[i], 0:TOK], scalar=vec[:, V_KG:V_KG + 1],
                                           in1=qk_sq[:, i, :], op0=ALU.mult, op1=ALU.mult).then_inc(qk_ready, 1)
                    continue
                for a in range(2):
                    head = 2 * (i - 1) + a
                    g, j = head // (NH // NKV), head % (NH // NKV)
                    src = slice(a * HEAD_DIM, (a + 1) * HEAD_DIM)
                    by_chunk = lambda ap: ap.rearrange("p (c t) -> p c t", t=CHUNK)
                    last = V.scalar_tensor_tensor(
                        out=qT[g * HEAD_DIM:(g + 1) * HEAD_DIM, :, j, :], in0=by_chunk(ps[src, QK_BANK[i], 0:TOK]),
                        scalar=vec[src, V_QG:V_QG + 1], in1=by_chunk(qk_sq[src, i, :]), op0=ALU.mult, op1=ALU.mult)
                last.then_inc(qk_ready, 1)

            def softmax(c):
                off, n = key_window(c)
                S = 4 * c
                dve.wait_ge(scores_done, c + 1)
                if c == 0:
                    dve.wait_ge(sink_set, 2)
                V.tensor_reduce(smx[:, 0, :], SC[:, :, off:off + n], AX.X, ALU.max).then_inc(smx_step, 1)
                dve.wait_ge(smx_step, S + 1)
                V.scalar_tensor_tensor(out=smx[:, 1, :], in0=smx[:, 0, :], scalar=HEAD_DIM ** -0.5, in1=sink[:, :],
                                       op0=ALU.mult, op1=ALU.max).then_inc(smx_step, 1)
                dve.wait_ge(smx_step, S + 2)
                V.tensor_scalar(smx[:, 2, :], smx[:, 1, :], -1.0, None, ALU.mult).then_inc(smx_neg, 1)
                V.tensor_tensor(smx[:, 3, :], sink[:, :], smx[:, 1, :], ALU.subtract).then_inc(smx_neg, 1)
                dve.wait_ge(exp_done, 5 * (c + 1))
                V.tensor_tensor(smx[:, 6, :], smx[:, 4, :], smx[:, 5, :], ALU.add).then_inc(smx_step, 1)
                dve.wait_ge(smx_step, S + 3)
                V.reciprocal(smx[:, 7, :], smx[:, 6, :]).then_inc(smx_step, 1)
                dve.wait_ge(smx_step, S + 4)
                V.tensor_tensor(probs[:, :, off:off + n], probs[:, :, off:off + n],
                                smx[:, 7, :].unsqueeze(2).to_broadcast([P, 4, n]), ALU.mult).then_inc(probs_ready, 1)

            def convolve(j):
                dve.wait_ge(c_copied, j + 1)
                dve.wait_ge(bch_done, 3 * j + 2)
                hc = ps[:, BCH_BANK[1], 0:TOK]
                V.tensor_tensor(uT[:, j, CW - 1:CW - 1 + SEQ], c_sb[:, 0:SEQ], hc[:, 0:SEQ], ALU.mult
                                ).then_inc(cv_step, 1)
                V.tensor_tensor(uT[:, j, UW - DEC:UW], c_sb[:, SEQ:TOK], hc[:, SEQ:TOK], ALU.mult
                                ).then_inc(u_ready, 1)
                dve.wait_ge(cv_step, 3 * j + 1)
                dve.wait_ge(u_ready, j + 1)
                if j == 0:
                    dve.wait_ge(conv_pad, 2)
                else:
                    dve.wait_ge(conv_mixed, j)
                W = UW - (CW - 1)
                tap = lambda w: vec[:, V_CONV + w * CT + j:V_CONV + w * CT + j + 1]
                V.tensor_scalar(cv[:, :], uT[:, j, 0:W], tap(0), None, ALU.mult).then_inc(cv_step, 1)
                dve.wait_ge(cv_step, 3 * j + 2)
                V.scalar_tensor_tensor(out=cv[:, :], in0=uT[:, j, 1:1 + W], scalar=tap(1), in1=cv[:, :],
                                       op0=ALU.mult, op1=ALU.add).then_inc(cv_step, 1)
                dve.wait_ge(cv_step, 3 * j + 3)
                V.scalar_tensor_tensor(out=cv[:, :], in0=uT[:, j, 2:2 + W], scalar=tap(2), in1=cv[:, :],
                                       op0=ALU.mult, op1=ALU.add).then_inc(rows_moved, 1)

            def gate_conv(j):
                dve.wait_ge(bch_done, 3 * j + 3)
                dve.wait_ge(rows_moved, j + 1)
                B = ps[:, BCH_BANK[2], 0:TOK]
                V.tensor_tensor(mixT[:, QT + j, 0:SEQ], B[:, 0:SEQ], cv[:, 0:SEQ], ALU.mult)
                V.tensor_tensor(mixT[:, QT + j, SEQ:TOK], B[:, SEQ:TOK], cv[:, SEQ + CW - 1:], ALU.mult
                                ).then_inc(conv_mixed, 1)

            for n in range(3 * CT):
                if n % 3 == 1:
                    convolve(n // 3)
                if n % 3 == 2:
                    gate_conv(n // 3)
                if n % 2 == 0 and n // 2 < NCH:
                    softmax(n // 2)
                if n % 2 == 1 and n >= 3:
                    c = (n - 3) // 2
                    dve.wait_ge(att_done, c + 1)
                    V.tensor_copy(mixT[:, 0:QT, c * CHUNK:(c + 1) * CHUNK],
                                  AO.rearrange("p (j t) -> p j t", t=CHUNK)).then_inc(att_mixed, 1)

            for t, (_, n) in enumerate(TT):
                for half in range(2):
                    cols = slice(half * HALF, (half + 1) * HALF)
                    dve.wait_ge(out_done, 2 * t + half + 1)
                    V.tensor_tensor(x[0:n, t, cols], ps[0:n, OUT_BANK[t][half], :], x[0:n, t, cols], ALU.add
                                    ).then_inc(h_ready, 1)
                dve.wait_ge(h_std, t + 1)
                V.reciprocal(st[0:n, 2, t:t + 1], st[0:n, 1, t:t + 1]).then_inc(h_rstd, 1)
                dve.wait_ge(h_rstd, t + 1)
                V.scalar_tensor_tensor(out=hn[0:n, t, :], in0=x[0:n, t, :], scalar=st[0:n, 2, t:t + 1],
                                       in1=g2[0:n, :], op0=ALU.mult, op1=ALU.mult).then_inc(hn_ready, 1)

            n_route = [0]

            def then(ins):
                n_route[0] += 1
                ins.then_inc(route, 1)
                dve.wait_ge(route, n_route[0])

            dve.wait_ge(router_set, 2)
            for t, (_, n) in enumerate(TT):
                dve.wait_ge(logits_done, t + 1)
                then(V.tensor_tensor(lg[0:n, t, :], LG[0:n, t, :], b_rt[0:n, :], ALU.add))
                then(V.max(top8[:, t, :], lg[:, t, :]))
            then(V.tensor_copy(top4[:, :, 0:TOP_K], top8[:, :, 0:TOP_K]))
            V.tensor_scalar(neg_top[:, :], top8[:, :, 0], -1.0, None, ALU.mult).then_inc(top_ready, 1)
            for t in range(NT):
                then(V.match_replace(left[:, t, :], top4[:, t, :], lg[:, t, :], -NO_LOGIT))
            then(V.tensor_tensor(sel[:, :, :], left[:, :, :], lg[:, :, :], ALU.not_equal))
            V.memset(sel[DEC:P, 2, :], 0.0).then_inc(sel_ready, 1)
            dve.wait_ge(sel_ready, 1)
            dve.wait_ge(gexp_done, NT)
            then(V.tensor_tensor(gates[:, :, :], gates[:, :, :], sel[:, :, :], ALU.mult))
            then(V.tensor_reduce(gsum[:, :], gates[:, :, :], AX.X, ALU.add))
            then(V.memset(gsum[DEC:P, 2:3], 1.0))
            then(V.reciprocal(gsum[:, :], gsum[:, :]))
            then(V.tensor_tensor(gates[:, :, :], gates[:, :, :],
                                 gsum[:, :].unsqueeze(2).to_broadcast([P, NT, NE]), ALU.mult))
            dve.wait_ge(ranked, 1)
            then(V.scalar_tensor_tensor(out=rank[:, :, :], in0=RK[:, 0:NT, :], scalar=1.0, in1=sel[:, :, :],
                                        op0=ALU.add, op1=ALU.mult))
            then(V.tensor_scalar(rank[:, :, :], rank[:, :, :], -1.0, None, ALU.add))
            V.tensor_copy(counts[:, :], RK[:, NT, :]).then_inc(counts_ready, 1)
            then(V.tensor_reduce(most[:, :], RK[:, NT, :], AX.X, ALU.max))
            V.tensor_copy(most_i[:, :], most[:, :]).then_inc(counts_ready, 1)
            dve.wait_ge(counts_ready, 2)
            V.memset(smx[:, 0, 0:1], 0.0).then_inc(rank_ready, 1)

            def split_lo(ch):
                dve.wait_ge(hi_done, ch.nth + 1)
                V.tensor_tensor(w_lo[:, ch.split, :], slot(raw, ch.raw), w_hi[:, ch.split, :], ALU.subtract
                                ).then_inc(split_done, 1)

            def mark_rows(i, e, experts=(0, 1)):
                for s in experts:
                    V.tensor_tensor(oh[:, :, s, :, :], row_ids[:, :].unsqueeze(1).unsqueeze(1).to_broadcast([P, NT, 2, CAP]),
                                    rank[:, :, bass.ds(e + s, 1)].unsqueeze(3).to_broadcast([P, NT, 2, CAP]),
                                    ALU.is_equal)
                V.tensor_copy(gate_col[:, :, 0:len(experts)], gates[:, :, bass.ds(e, len(experts))]).then_inc(oh_ready, 1)

            def split_xl(i, experts=(0, 1)):
                dve.wait_ge(xh_ready, i + 1)
                for s in experts:
                    last = V.tensor_tensor(xhl[:, s, :, CAP:], XE[:, :, s * CAP:(s + 1) * CAP], xhl[:, s, :, 0:CAP],
                                           ALU.subtract)
                last.then_inc(xl_ready, 1)

            def gate_and_up(n, e):
                bias = lambda f0: b_guT[:, f0:f0 + FT, bass.ds(e, 1)].to_broadcast([P, FT, CAP])
                dve.wait_ge(folded, n + 1)
                V.tensor_tensor(ge[:, :, :], TU[:, 0], bias(0), ALU.add).then_inc(g_biased, 1)
                V.tensor_tensor(ue[:, :, :], TU[:, 1], bias(FT), ALU.add).then_inc(u_biased, 1)
                dve.wait_ge(g_biased, n + 1)
                V.tensor_scalar(ge[:, :, :], ge[:, :, :], LIMIT, None, ALU.min).then_inc(g_ready, 1)
                dve.wait_ge(u_biased, n + 1)
                V.tensor_scalar(ue[:, :, :], ue[:, :, :], LIMIT, -LIMIT, ALU.min, ALU.max).then_inc(u_clipped, 1)

            def hidden(n):
                dve.wait_ge(sig_ready, n + 1)
                V.tensor_tensor(ge[:, :, :], ge[:, :, :], sg[:, :, :], ALU.mult).then_inc(gs_ready, 1)
                dve.wait_ge(u_clipped, n + 1)
                dve.wait_ge(gs_ready, n + 1)
                V.scalar_tensor_tensor(out=ue[:, :, :], in0=ue[:, :, :], scalar=1.0, in1=ge[:, :, :],
                                       op0=ALU.add, op1=ALU.mult).then_inc(h_ready2, 1)

            def split_hl(n):
                dve.wait_ge(hh_ready, n + 1)
                V.tensor_tensor(he[:, :, CAP:], ue[:, :, :], he[:, :, 0:CAP], ALU.subtract).then_inc(he_ready, 1)

            def split_yl(n, s):
                dve.wait_ge(yh_ready, n + 1)
                V.scalar_tensor_tensor(out=y_lo[:, s, :], in0=Y, scalar=gate_row[:, s:s + 1], in1=y_hi[:, s, :],
                                       op0=ALU.mult, op1=ALU.subtract).then_inc(yl_ready, 1)

            def add_rows(done, told, base):
                for u in range(2 * NT):
                    t, half = u // 2, u % 2
                    _, m = TT[t]
                    cols = slice(half * HALF, (half + 1) * HALF)
                    dve.wait_ge(done, base + u + 1)
                    V.tensor_tensor(x[0:m, t, cols], ps[0:m, 6 + half, :], x[0:m, t, cols], ALU.add
                                    ).then_inc(told, 1)

            def step(e, at, par, nxt, i=None, last=False):
                first = isinstance(e, int) and e == 0
                if par and not (isinstance(e, int) and e == 1):
                    add_rows(scattered, added, 2 * NT * (i - 1))
                for c in range(2, CH if not first else GUC):
                    split_lo(Chunk(at, c))
                    if not first and c == 2:
                        gate_and_up(e - 1, e - 1)
                    if not first and c == 3:
                        hidden(e - 1)
                    if not first and c == 4:
                        split_hl(e - 1)
                    if par and not last and c == 9:
                        dve.wait_ge(oh_turned, i + 1)
                        mark_rows(i + 1, 2 * i + 2)
                if first:
                    add_rows(b_spread, b_added, 0)
                for c in range(*((0, 2) if nxt != NE else (GUC, GUC + 2))):
                    split_lo(Chunk(nxt, c))
                if not first:
                    split_yl(e - 1, 1 - par)

            mark_rows(0, 0)
            split_lo(Chunk(0, 0))
            split_lo(Chunk(0, 1))
            split_xl(0)
            step(0, 0, 0, 1)
            step(1, 1, 1, 2, i=0)
            split_xl(1)
            with dve.Fori(1, PAIRS - 1) as i:
                step(2 * i, (i, 0), 0, (i, 1))
                step(2 * i + 1, (i, 1), 1, (i + 1, 0), i=i)
                split_xl(i + 1)
            step(NE - 2, NE - 2, 0, NE - 1)
            step(NE - 1, NE - 1, 1, NE, i=PAIRS - 1, last=True)
            gate_and_up(NE - 1, NE - 1)
            hidden(NE - 1)
            split_hl(NE - 1)
            split_lo(Chunk(NE, GUC + 2))
            split_lo(Chunk(NE, GUC + 3))
            split_yl(NE - 1, 1)
            add_rows(scattered, added, 2 * NT * (PAIRS - 1))

            def next_round(q):
                V.tensor_scalar(row_ids[:, :], row_ids[:, :], float(CAP), None, ALU.add).then_inc(round_set, 1)
                dve.wait_ge(round_set, q)
                V.memset(smx[:, 0, 2:3], 0.0)

            def again(n, e):
                i = n - NE + PAIRS
                dve.wait_ge(added, 2 * NT * i)
                mark_rows(i, e, (0,))
                split_xl(i, (0,))
                for c in range(CH):
                    if c == GUC:
                        gate_and_up(n, e)
                        hidden(n)
                        split_hl(n)
                    split_lo(LateChunk(n, e, c))
                split_yl(n, 0)
                add_rows(scattered, added, 2 * NT * i)

            further_rounds(dve, again, next_round)
            V.memset(smx[:, 0, 1:2], 0.0).then_inc(y_ready, 1)


_INS = ['x_prompt', 'x_sample', 'cache_k', 'cache_v', 'state_conv', 'norm1_g', 'w_in', 'q_norm_g', 'k_norm_g',
        'sinks', 'conv_w', 'w_out', 'norm2_g', 'w_router', 'b_router', 'w_gu', 'b_gu', 'w_down', 'b_down']
_OUTS = [(1, 256, 1024), (1, 64, 1024), (1, 1, 128, 2, 64), (1, 1, 128, 2, 64), (1, 1, 2, 512),
         (1, 1, 128, 2, 64), (1, 1, 128, 2, 64), (1, 1, 2, 512)]


def kernel(**inputs):
    import numpy as _np
    import concourse.bacc as _bacc
    from concourse import mybir as _mybir
    from concourse.bass_utils import run_bass_kernel_spmd as _run

    nc = _bacc.Bacc("TRN2", target_bir_lowering=False, num_devices=1)
    arrays, args = {}, []
    for name in _INS:
        a = _np.ascontiguousarray(inputs[name])
        arrays[f"in_{name}_dram"] = a
        args.append(nc.dram_tensor(f"in_{name}_dram", a.shape, _mybir.dt.from_np(a.dtype), kind="ExternalInput").ap())
    for i, shape in enumerate(_OUTS):
        dt = _mybir.dt.from_np(_np.dtype("float32"))
        args.append(nc.dram_tensor(f"out_{i}_dram", shape, dt, kind="ExternalOutput").ap())
    hybrid_layer_kernel(nc, *args)
    r = _run(nc, [arrays], core_ids=[0])
    return tuple(r.results[0][f"out_{i}_dram"] for i in range(len(_OUTS)))
```

```python
from contextlib import ExitStack

import concourse.bass as bass
from concourse import mybir

ALU = mybir.AluOpType
ACT = mybir.ActivationFunctionType
AX = mybir.AxisListType
F32 = mybir.dt.float32
F32R = mybir.dt.float32r
I32 = mybir.dt.int32

P = 128
CHUNK = 64
HEAD_DIM = 64
TOP_K = 4
EPS = 1e-6
LIMIT = 7.0
ALPHA = 1.702
CAP = 64
NO_LOGIT = 3.0e38


def hybrid_layer_kernel(nc, x_prompt, x_sample, cache_k, cache_v, state_conv, norm1_g, w_in, q_norm_g,
                        k_norm_g, sinks, conv_w, w_out, norm2_g, w_router, b_router, w_gu, b_gu,
                        w_down, b_down, y_prompt, y_sample, new_k_prompt, new_v_prompt,
                        new_conv_prompt, new_k_sample, new_v_sample, new_conv_sample):
    SEQ, D = x_prompt.shape[1:]
    DEC = x_sample.shape[1]
    IN_DIM = w_in.shape[2]
    NH = sinks.shape[1]
    NKV = cache_k.shape[3]
    KV = NKV * HEAD_DIM
    ATT = NH * HEAD_DIM
    CONV = conv_w.shape[2]
    CW = conv_w.shape[1]
    WIN = cache_k.shape[2]
    NE = w_router.shape[2]
    FF = w_down.shape[2]
    KT = D // P
    FT = FF // P
    CT = CONV // P
    TOK = SEQ + DEC
    NT = 3
    TT = [(0, P), (P, P), (2 * P, DEC)]
    HALF = D // 2
    QT = ATT // P
    NCH = TOK // CHUNK
    SAMPLE = NCH - 1
    MIX = (ATT + CONV) // P
    QKV = ATT + 2 * KV
    PAIRS = NE // 2
    ROUNDS = -(-TOK // CAP)
    FLAT = 2 * FF
    GUC, DNC = KT, FT * D // FLAT
    CH = GUC + DNC
    FPC = FLAT // D
    RAW, SPLIT = 8, 4
    assert (2 * CH) % RAW == 0 and CH % SPLIT == 0 and (RAW, CH, GUC) == (8, 12, 8)
    assert (SEQ, DEC, CHUNK, WIN, KV, NKV, HALF, QT) == (256, 64, 64, 128, 128, 2, 512, 4)
    assert FT * CAP <= 512 and KT == FT and 2 * FT * P == 2048

    ctx = ExitStack()
    with ctx:
        def sb(name, shape, dt=F32):
            return ctx.enter_context(nc.sbuf_tensor(name, shape, dt))

        class Region:

            def __init__(self, name, size):
                sb(name, [P, size // 4])
                self.base = nc.sbuf_base - size
                self.size, self.name = size, name
                self.at = 0

            def put(self, name, *shape, dt=F32, at=None, rows=P):
                size = 4
                for d in shape:
                    size *= d
                at = self.at if at is None else at
                assert at % 32 == 0 and at + size <= self.size, (self.name, name, at + size)
                self.at = at + -(-size // 32) * 32
                return nc.alloc_sbuf_tensor_at(name, [rows, *shape], dt, offset=self.base + at)

        def sem(name):
            return ctx.enter_context(nc.semaphore(name))

        ps = ctx.enter_context(nc.psum_tensor("ps", [P, 8, 512], F32))

        V_G1, V_CONV, V_QG, V_KG = 0, KT, KT + CW * CT, KT + CW * CT + 1
        V_STATE = V_KG + 1
        NV = V_STATE + (CW - 1) * CT

        raw_region = Region("raw_region", (RAW - 1) * FLAT * 4 + (ATT + CONV) // P * TOK * 4)
        raw = raw_region.put("raw", RAW, FLAT)
        gatesT = raw_region.put("gatesT", NT * P, rows=NE)
        w_chc = raw_region.put("w_chc", KT, 2 * CONV, at=3 * FLAT * 4)
        mixT = raw_region.put("mixT", MIX, TOK)
        split_region = Region("split_region", 2 * SPLIT * FLAT * 4)
        w_hi = split_region.put("w_hi", SPLIT, FLAT, dt=F32R)
        w_lo = split_region.put("w_lo", SPLIT, FLAT, dt=F32R)
        w_qkv = split_region.put("w_qkv", KT, QKV, at=0)
        xnT = split_region.put("xnT", KT, TOK)
        qk_sq = split_region.put("qk_sq", 1 + QT, TOK)
        qT = split_region.put("qT", NCH, NH // NKV, CHUNK)
        kT = split_region.put("kT", TOK)
        w_b = split_region.put("w_b", KT, CONV)
        ck_nat = split_region.put("ck_nat", KV)
        cv_nat = split_region.put("cv_nat", KV)
        vec_rows = split_region.put("vec_rows", P, rows=NV)
        probsT = split_region.put("probsT", 2, 512, at=0)
        k_out = split_region.put("k_out", 2, KV)
        c_sb = split_region.put("c_sb", TOK)
        v_nat = split_region.put("v_nat", NT, KV)
        assert split_region.at <= KT * QKV * 4
        hnT = split_region.put("hnT", KT, P, at=(SPLIT - 1) * FLAT * 4)
        g2 = split_region.put("g2", D)
        w_rt = split_region.put("w_rt", KT, NE, at=(2 * SPLIT - 1) * FLAT * 4)
        junk_h = split_region.put("junk_h", D)
        sel_sum = split_region.put("sel_sum", NT + 1, NE)
        work_region = Region("work_region", 46144)
        xhl = work_region.put("xhl", 2, KT, 2 * CAP, dt=F32R)
        he = work_region.put("he", FT, 2 * CAP, dt=F32R)
        ge = work_region.put("ge", FT, CAP, at=work_region.at - FT * 2 * CAP * 4)
        sg = work_region.put("sg", FT, CAP)
        y_hi = work_region.put("y_hi", 2, D, dt=F32R)
        b_dn = work_region.put("b_dn", D, rows=NE)
        y_lo = work_region.put("y_lo", 2, D, dt=F32R, at=work_region.at - D * 4)
        ohT = work_region.put("ohT", 2, NT * P, dt=F32R)
        gu_sb = work_region.put("gu_sb", FLAT)
        ue = work_region.put("ue", FT, CAP)
        oh = work_region.put("oh", NT, 2, 2, CAP)
        ge_last = work_region.put("ge_last", FT, CAP, at=0)
        sg_last = work_region.put("sg_last", FT, CAP)
        he_last = work_region.put("he_last", FT, 2 * CAP, dt=F32R)
        w_o = work_region.put("w_o", MIX, D, at=0)
        bias_rows = work_region.put("bias_rows", 2 * FF, rows=NE)
        UW = SEQ + DEC + 2 * (CW - 1)
        uT = work_region.put("uT", CT, UW)

        ident = sb("ident", [P, P])
        ones = sb("ones", [P, P])
        before = sb("before", [P, P])
        head_ones = sb("head_ones", [P, P])
        fold = sb("fold", [2 * CAP, CAP])
        row_ids = sb("row_ids", [P, CAP])
        eps = sb("eps", [P, 1])
        vec = sb("vec", [P, NV])
        sink_row = sb("sink_row", [P, NH])
        sink = sb("sink", [P, NH // 2])
        b_rt = sb("b_rt", [P, NE])
        b_guT = sb("b_guT", [P, 2 * FT, NE])

        x = sb("x", [P, NT, D])
        hn = sb("hn", [P, NT, D])
        junk = mixT[:, :, :].rearrange("p m t -> p (m t)")[:, 0:D]
        ckT = sb("ckT", [P, P])
        qk_room = qk_sq[:, :, :].rearrange("p a t -> p (a t)")
        probs = qk_room[:, 0:4 * 256].rearrange("p (b k) -> p b k", b=4)
        cv = qk_room[:, 4 * 256:4 * 256 + UW - (CW - 1)]
        u_out = probsT[0:CW - 1, :, :]
        smx = sb("smx", [P, 8, 4])
        st = sb("st", [P, 4, NT])

        lg = sb("lg", [P, NT, NE])
        top8 = sb("top8", [P, NT, 8])
        top4 = sb("top4", [P, NT, 8])
        left = sb("left", [P, NT, NE])
        sel = sb("sel", [P, NT, NE])
        neg_top = sb("neg_top", [P, NT])
        gates = sb("gates", [P, NT, NE])
        gsum = sb("gsum", [P, NT])
        rank = sb("rank", [P, NT, NE])
        counts = sb("counts", [P, NE], I32)
        most = sb("most", [P, 1])
        most_i = sb("most_i", [P, 1], I32)
        gate_col = sb("gate_col", [P, NT, 2])
        gate_row = sb("gate_row", [P, 2])

        x_in = [sem(f"x_in{t}") for t in range(2)]
        wqkv_in, wch_in, wb_in, wo_in = sem("wqkv_in"), sem("wch_in"), sem("wb_in"), sem("wo_in")
        first_marked = sem("first_marked")
        b_down_in, sink_in, router_in = sem("b_down_in"), sem("sink_in"), sem("router_in")
        vec_in, bias_in, ck_in, cv_in = (sem(n) for n in ("vec_in", "bias_in", "ck_in", "cv_in"))
        raw_in = [sem(f"raw_in{q}") for q in range(RAW)]
        hi_done, split_done, chunk_used = sem("hi_done"), sem("split_done"), sem("chunk_used")
        kv_stored = sem("kv_stored")
        y_stored = sem("y_stored")
        zeroed, consts, eps_set, heads_set = sem("zeroed"), sem("consts"), sem("eps_set"), sem("heads_set")
        router_set, conv_pad = sem("router_set"), sem("conv_pad")
        x_sumsq, x_std, x_rstd, x_scaled = (sem(n) for n in ("x_sumsq", "x_std", "x_rstd", "x_scaled"))
        vec_turned, vec_ready = sem("vec_turned"), sem("vec_ready")
        bias_turned, bias_ready = sem("bias_turned"), sem("bias_ready")
        x_turned, xnT_ready = sem("x_turned"), sem("xnT_ready")
        qk_done, qk_squared, head_ss, head_std, head_rstd, qk_ready = (sem(n) for n in (
            "qk_done", "qk_squared", "head_ss", "head_std", "head_rstd", "qk_ready"))
        v_done, v_ready = sem("v_done"), sem("v_ready")
        bch_done, c_copied, u_ready, cv_step, conv_mixed = (sem(n) for n in (
            "bch_done", "c_copied", "u_ready", "cv_step", "conv_mixed"))
        sink_set, scores_done, smx_step, smx_neg, exp_done, probs_ready = (sem(n) for n in (
            "sink_set", "scores_done", "smx_step", "smx_neg", "exp_done", "probs_ready"))
        probs_turned, probsT_ready, att_done, att_mixed = (sem(n) for n in (
            "probs_turned", "probsT_ready", "att_done", "att_mixed"))
        k_turned, k_out_ready, u_turned, u_out_ready = (sem(n) for n in (
            "k_turned", "k_out_ready", "u_turned", "u_out_ready"))
        out_done, h_ready, h_sumsq, h_std, h_rstd, hn_ready = (sem(n) for n in (
            "out_done", "h_ready", "h_sumsq", "h_std", "h_rstd", "hn_ready"))
        hn_turned, hnT_ready, logits_done = sem("hn_turned"), sem("hnT_ready"), sem("logits_done")
        route, top_ready, gexp_done, sel_ready, ranked, rank_ready = (sem(n) for n in (
            "route", "top_ready", "gexp_done", "sel_ready", "ranked", "rank_ready"))
        counts_ready = sem("counts_ready")
        oh_ready, oh_turned, ohT_ready = sem("oh_ready"), sem("oh_turned"), sem("ohT_ready")
        gathered, xh_ready, xl_ready = sem("gathered"), sem("xh_ready"), sem("xl_ready")
        gates_turned, gatesT_ready, b_spread, b_added = (sem(n) for n in (
            "gates_turned", "gatesT_ready", "b_spread", "b_added"))
        gu_copied, folded = sem("gu_copied"), sem("folded")
        g_biased, g_ready, u_biased, u_clipped, sig_ready, gs_ready, hidden_ready, hh_ready, he_ready = (
            sem(n) for n in ("g_biased", "g_ready", "u_biased", "u_clipped", "sig_ready", "gs_ready",
                             "hidden_ready", "hh_ready", "he_ready"))
        yh_ready, yl_ready = sem("yh_ready"), sem("yl_ready")
        scattered, added = sem("scattered"), sem("added")
        rows_moved, round_set = sem("rows_moved"), sem("round_set")
        y_ready = sem("y_ready")

        B_VEC = 5
        XT_BANK = [(0, 1), (2, 3), (4,)]
        QK_BANK = [3, 4, 5, 0, 1]
        V_BANK = 2
        SS_BANK = [6, 7]
        BCH_BANK = [3, 4, 5]
        SC = ps[:, 6:8, :].rearrange("p a (b k) -> p (a b) k", b=2)
        PT = ps[:, 0:2, :]
        AO = ps[:, 2, 0:256]
        KO = ps[:, 2, 256:512].rearrange("p (a n) -> p a n", a=2)
        OUT_BANK = [(3, 4), (5, 6), (7, 2)]
        LG = ps[:, 3:3 + NT, 0:NE]
        RK = ps[:, 6, 0:2 * NE].rearrange("p (t e) -> p t e", t=2)
        RK_LAST = ps[:, 4, 0:2 * NE].rearrange("p (t e) -> p t e", t=2)

        def turned_h(t):
            n = TT[t][1]
            if t < 2:
                return ps[:, 0:2, :].rearrange("p a (k t) -> p (a k) t", t=n)
            return ps[:, 3, :].rearrange("p (k t) -> p k t", t=n)

        GU = ps[:, 0:4, :]
        XE = ps[:, 0:2, :].rearrange("p a (k c) -> p (a k) c", c=2 * CAP)
        TU = ps[:, 4:6, :].rearrange("p a (f c) -> p a f c", c=CAP)
        OT = ps[:, 4:6, :]
        Y = ps[:, 6:8, :].rearrange("p a n -> p (a n)")
        LAST_BANK = [2, 3, 4, 5, 6, 7]
        Y_LAST = ps[:, 0:2, :].rearrange("p a n -> p (a n)")

        gu_dram = w_gu.rearrange("l e (k p) f -> (l e) k p f", p=P)
        dn_dram = w_down.rearrange("l e (m a p) n -> (l e) m p a n", a=FPC, p=P)

        LAST = CH * NE + DNC

        class Chunk:
            def __init__(self, e, c):
                self.e, self.c = e, c
                if isinstance(e, int):
                    even, par = e - e % 2, e % 2
                    place = CH * e + c + (DNC if e == 0 else 0) - (GUC if e == NE else 0)
                    assert DNC <= place < LAST
                    self.raw, self.split = place % RAW, place % SPLIT
                    turn = place // RAW
                    self.nth = place - DNC
                else:
                    i, par = e
                    self.e = 2 * i + par
                    self.raw, self.split = (CH * par + c) % RAW, (CH * par + c) % SPLIT
                    turn = i * (2 * CH // RAW) + (CH * par + c) // RAW
                    self.nth = i * (2 * CH) + (CH * par + c - DNC)
                self.arrivals = turn + 1 - (1 if self.raw < DNC else 0)
                self.reload = isinstance(e, tuple) or self.nth >= RAW
                self.resplit = isinstance(e, tuple) or self.nth >= SPLIT
                self.free_raw = self.nth - RAW + 1
                self.free_split = self.nth - SPLIT + 1

        AHEAD = [SPLIT - 1, SPLIT]
        EARLY = SPLIT - 1

        def ahead(par, nxt):
            return range(AHEAD[par]) if nxt != NE else range(GUC, GUC + AHEAD[par])

        class LateChunk:

            def __init__(self, n, e, c):
                self.e, self.raw, self.split = e, c % RAW, c % SPLIT
                self.nth = CH * n + c
                self.reload = self.resplit = True
                full = CH * NE // RAW
                self.arrivals = (n - NE) * 2 + full + c // RAW + 1 if self.raw < CH - RAW else n - NE + full + 1
                self.free_raw = self.nth - RAW + 1 if c >= RAW else CH * n
                self.free_split = self.nth - SPLIT + 1
                self.c = c

        def slot(ring, q):
            return ring[:, (q - DNC) % RAW, :]

        in_dram = w_in.rearrange("l (k p) n -> p (l k) n", p=P)

        def key_window(c):
            if c == SAMPLE:
                return 0, WIN + DEC
            first = max(0, c - WIN // CHUNK)
            return (first % 2) * CHUNK, (c + 1 - first) * CHUNK

        def further_rounds(eng, step, each_round=None, at_start=None, at_end=None):
            eng.wait_ge(counts_ready, 2)
            top = eng.value_load(most_i[0:1, 0:1], min_val=0, max_val=TOK)
            with eng.If(top > CAP):
                n_reg = eng.alloc_register("n_block_" + str(eng.engine).split(".")[-1])
                eng.reg_mov(n_reg, NE)
                if at_start:
                    at_start()
                with eng.Fori(1, ROUNDS) as q:
                    if each_round:
                        each_round(q)
                    with eng.Fori(0, NE) as e:
                        have = eng.value_load(counts[0:1, bass.ds(e, 1)], min_val=0, max_val=TOK)
                        with eng.If(have > q * CAP):
                            n = eng.snap(n_reg, min_val=NE, max_val=NE * ROUNDS)
                            step(n, e)
                            eng.reg_add(n_reg, n_reg, 1)
                if at_end:
                    at_end()

        block = ctx.enter_context(nc.Block())

        @block.sync
        def _(sp):
            def load(ch):
                if ch.reload:
                    sp.wait_ge(split_done, ch.free_raw)
                if ch.c < GUC:
                    src, dst = gu_dram[ch.e, ch.c], slot(raw, ch.raw)
                else:
                    src = dn_dram[ch.e, ch.c - GUC]
                    dst = slot(raw, ch.raw).rearrange("p (a n) -> p a n", a=FPC)
                sp.dma_start(dst, src).then_inc(raw_in[ch.raw], 16)

            def step_loads(e, which=range(CH)):
                for c in which:
                    ch = Chunk(e, c)
                    if c >= GUC:
                        ch.e = ch.e - 1
                    load(ch)

            sp.dma_start(x[:, 0:2, :], x_prompt.rearrange("b (t p) d -> p (b t) d", p=P)).then_inc(x_in[0], 16)
            sp.dma_start(x[0:DEC, 2, :], x_sample[0]).then_inc(x_in[1], 16)
            sp.dma_start(w_qkv[:, :, :], in_dram[:, :, 0:QKV]).then_inc(wqkv_in, 16)
            sp.wait_ge(bias_in, 16)
            sp.wait_ge(sink_in, 16)
            sp.dma_start(w_chc[:, :, :], in_dram[:, :, QKV + CONV:IN_DIM]).then_inc(wch_in, 16)
            sp.dma_start(w_b[:, :, :], in_dram[:, :, QKV:QKV + CONV]).then_inc(wb_in, 16)
            for g in range(2):
                sp.dma_start(w_o[g * HEAD_DIM:(g + 1) * HEAD_DIM, 0:QT, :],
                             w_out[0, g * ATT // 2:(g + 1) * ATT // 2, :].rearrange("(j p) n -> p j n", p=HEAD_DIM)
                             ).then_inc(wo_in, 16)
            sp.dma_start(w_o[:, QT:MIX, :],
                         w_out[0, ATT:ATT + CONV, :].rearrange("(j p) n -> p j n", p=P)).then_inc(wo_in, 16)
            step_loads(0, range(3))
            sp.wait_ge(bch_done, 3 * CT)
            step_loads(0, range(3, RAW - 1))
            sp.wait_ge(out_done, 2 * NT)
            step_loads(0, range(RAW - 1, GUC))
            step_loads(1)
            with sp.Fori(1, PAIRS) as i:
                step_loads((i, 0))
                step_loads((i, 1))
            step_loads(NE, range(GUC, CH))

            def store_y(told, base, times):
                for t, (_, n) in enumerate(TT):
                    sp.wait_ge(told, base + 2 * (t + 1))
                    dst = y_prompt[0, t * P:(t + 1) * P, :] if t < 2 else y_sample[0]
                    sp.dma_start(dst, x[0:n, t, :]).then_inc(y_stored, 16)
                sp.wait_ge(y_stored, 16 * NT * times)

            store_y(added, 2 * NT * (PAIRS - 1), 1)

            def again(n, e):
                for c in range(CH):
                    load(LateChunk(n, e, c))

            further_rounds(sp, again, at_end=lambda: store_y(y_ready, 0, 2))
            sp.wait_ge(kv_stored, 8 * 16)

        @block.gpsimd
        def _(pool):
            pool.memset(ident[:, :], 0.0).then_inc(zeroed, 1)
            pool.memset(ones[:, :], 1.0).then_inc(zeroed, 1)
            pool.wait_ge(zeroed, 2)
            pool.affine_select(out=ident[:, :], in_=ident[:, :], compare_op=ALU.not_equal, fill=1.0,
                               base=0, pattern=[[-1, P]], channel_multiplier=1).then_inc(consts, 1)
            pool.affine_select(out=before[:, :], in_=ones[:, :], compare_op=ALU.is_gt, fill=0.0,
                               base=0, pattern=[[1, P]], channel_multiplier=-1).then_inc(consts, 1)
            pool.iota(row_ids[:, :], pattern=[[1, CAP]], base=0, channel_multiplier=0,
                      allow_small_or_imprecise_dtypes=True).then_inc(consts, 1)
            pool.dma_start(bias_rows[:, :], b_gu[0]).then_inc(bias_in, 16)

            roll = WIN - DEC
            rows_of = lambda a: a[0, 0].rearrange("t h d -> t (h d)")
            pool.wait_ge(ck_in, 16)
            pool.dma_start(rows_of(new_k_sample)[0:roll, :], ck_nat[DEC:WIN, :]).then_inc(kv_stored, 16)
            pool.wait_ge(cv_in, 16)
            pool.dma_start(rows_of(new_v_sample)[0:roll, :], cv_nat[DEC:WIN, :]).then_inc(kv_stored, 16)
            pool.wait_ge(v_ready, 2)
            pool.dma_start(rows_of(new_v_prompt), v_nat[:, 1, :]).then_inc(kv_stored, 16)
            pool.dma_start(rows_of(new_v_sample)[roll:WIN, :], v_nat[0:DEC, 2, :]).then_inc(kv_stored, 16)
            pool.wait_ge(k_out_ready, 2)
            pool.dma_start(rows_of(new_k_prompt), k_out[:, 0, :]).then_inc(kv_stored, 16)
            pool.dma_start(rows_of(new_k_sample)[roll:WIN, :], k_out[0:DEC, 1, :]).then_inc(kv_stored, 16)
            pool.wait_ge(bch_done, 3 * CT)
            pool.dma_start(g2[:, :], norm2_g.to_broadcast([P, D])).then_inc(router_in, 16)
            pool.dma_start(b_rt[:, :], b_router.to_broadcast([P, NE])).then_inc(router_in, 16)
            pool.dma_start(w_rt[:, :, :], w_router.rearrange("l (k p) e -> p (l k) e", p=P)).then_inc(router_in, 16)
            pool.wait_ge(u_out_ready, 2)
            pool.dma_start(new_conv_prompt[0, 0], u_out[:, 0, :]).then_inc(kv_stored, 16)
            pool.dma_start(new_conv_sample[0, 0], u_out[:, 1, :]).then_inc(kv_stored, 16)
            pool.wait_ge(out_done, 2 * NT)
            pool.dma_start(b_dn[:, :], b_down[0]).then_inc(b_down_in, 16)

        @block.tensor
        def _(pe):
            mm = nc.tensor.matmul

            pe.wait_ge(consts, 3)
            for t, (_, n) in enumerate(TT):
                pe.wait_ge(x_scaled, t + 1)
                per = KT // len(XT_BANK[t])
                for k in range(KT):
                    out = ps[:, XT_BANK[t][k // per], (k % per) * n:(k % per + 1) * n]
                    last = nc.tensor.transpose(out, hn[0:n, t, k * P:(k + 1) * P], ident[0:n, 0:n])
                last.then_inc(x_turned, 1)
                if t == 0:
                    pe.wait_ge(vec_in, 16 * 7)
                    nc.tensor.transpose(ps[:, B_VEC, 0:NV], vec_rows[:, :], ident[0:NV, 0:NV]).then_inc(vec_turned, 1)
                    pe.wait_ge(ck_in, 16)
                    nc.tensor.transpose(ps[:, B_VEC, P:2 * P], ck_nat[:, :], ident[:, :]).then_inc(vec_turned, 1)

            def turn_biases():
                pe.wait_ge(bias_in, 16)
                for f in range(2 * FT):
                    last = nc.tensor.transpose(ps[:, 6, f * NE:(f + 1) * NE], bias_rows[:, f * P:(f + 1) * P],
                                               ident[0:NE, 0:NE])
                last.then_inc(bias_turned, 1)

            pe.wait_ge(xnT_ready, len(TT) + 2)
            pe.wait_ge(wqkv_in, 16)

            def sum_squares(i):
                pe.wait_ge(qk_squared, i + 1)
                if i == 0:
                    pe.wait_ge(heads_set, 5)
                if i < 2:
                    pe.wait_ge(bias_ready, 1)
                else:
                    pe.wait_ge(head_std, i - 1)
                mm(ps[:, SS_BANK[i % 2], 0:TOK], head_ones[:, :], qk_sq[:, i, :], start=True, stop=True
                   ).then_inc(head_ss, 1)

            for i in range(1 + QT):
                if i == 2:
                    pe.wait_ge(vec_ready, 2)
                for k in range(KT):
                    cols = w_qkv[:, k, ATT:ATT + KV] if i == 0 else w_qkv[:, k, (i - 1) * P:i * P]
                    last = mm(ps[:, QK_BANK[i], 0:TOK], cols, xnT[:, k, :], start=(k == 0), stop=(k == KT - 1))
                last.then_inc(qk_done, 1)
                if i == 0:
                    turn_biases()
                if i >= 1:
                    sum_squares(i - 1)
            for t, (t0, n) in enumerate(TT):
                for k in range(KT):
                    last = mm(ps[0:n, V_BANK, t * P:t * P + KV], xnT[:, k, t0:t0 + n], w_qkv[:, k, ATT + KV:QKV],
                              start=(k == 0), stop=(k == KT - 1))
            last.then_inc(v_done, 1)
            sum_squares(QT)

            def scores(c):
                if c == 0:
                    pe.wait_ge(qk_ready, 1 + QT)
                    pe.wait_ge(head_std, 1 + QT)
                else:
                    pe.wait_ge(exp_done, 5 * c)
                off, n = key_window(c)
                for b in range(4):
                    g, jp = b // 2, b % 2
                    half = slice(g * HEAD_DIM, (g + 1) * HEAD_DIM)
                    qs = qT[half, c, 2 * jp:2 * jp + 2, :].rearrange("p a t -> p (a t)")
                    if c == SAMPLE:
                        mm(SC[:, b, 0:WIN], qs, ckT[half, :], start=True, stop=True)
                        last = mm(SC[:, b, WIN:WIN + DEC], qs, kT[half, SEQ:TOK], start=True, stop=True)
                    else:
                        last = mm(SC[:, b, off:off + n], qs, kT[half, (c + 1) * CHUNK - n:(c + 1) * CHUNK],
                                  start=True, stop=True)
                last.then_inc(scores_done, 1)

            def key_tiles(c):
                off, n = key_window(c)
                parts = [(0, off, min(P, off + n))]
                if off + n > P:
                    parts.append((1, 0, off + n - P))
                return parts

            def turn_probs(c):
                pe.wait_ge(probs_ready, c + 1)
                if c >= 1:
                    pe.wait_ge(probsT_ready, c)
                if c == 0:
                    pe.wait_ge(qk_ready, 1 + QT)
                for b in range(4):
                    for tile, _, k1 in key_tiles(c):
                        last = nc.tensor.transpose(PT[0:k1, tile, b * P:(b + 1) * P],
                                                   probs[:, b, tile * P:tile * P + k1], ident[:, :])
                last.then_inc(probs_turned, 1)

            def attend(c):
                pe.wait_ge(probsT_ready, c + 1)
                pe.wait_ge(v_ready, 2)
                if c == SAMPLE:
                    pe.wait_ge(cv_in, 16)
                if c >= 1:
                    pe.wait_ge(att_mixed, c)
                parts = key_tiles(c)
                for b in range(4):
                    g, jp = b // 2, b % 2
                    cols = slice(g * HEAD_DIM, (g + 1) * HEAD_DIM)
                    for i, (tile, k0, k1) in enumerate(parts):
                        if c == SAMPLE:
                            vals = cv_nat[:, cols] if tile == 0 else v_nat[0:k1, 2, cols]
                        else:
                            vals = v_nat[k0:k1, tile, cols]
                        last = mm(AO[cols, jp * P:(jp + 1) * P], vals, probsT[k0:k1, tile, b * P:(b + 1) * P],
                                  start=(i == 0), stop=(i == len(parts) - 1))
                last.then_inc(att_done, 1)

            def turn_keys():
                pe.wait_ge(v_ready, 2)
                nc.tensor.transpose(KO[:, 0, :], kT[:, SEQ - WIN:SEQ], ident[:, :])
                nc.tensor.transpose(KO[0:DEC, 1, :], kT[:, SEQ:TOK], ident[:, :]).then_inc(k_turned, 1)

            for n in range(3 * CT):
                j, part = n // 3, n % 3
                if n == 0:
                    pe.wait_ge(wch_in, 16)
                if n == 2:
                    pe.wait_ge(wb_in, 16)
                if n < 3:
                    pe.wait_ge(qk_ready, n + 1)
                elif part == 0:
                    pe.wait_ge(c_copied, j)
                elif part == 1:
                    pe.wait_ge(u_ready, j)
                else:
                    pe.wait_ge(conv_mixed, j)
                w, col = ((w_chc, 0), (w_chc, CONV), (w_b, 0))[part]
                col += j * P
                for k in range(KT):
                    last = mm(ps[:, BCH_BANK[part], 0:TOK], w[:, k, col:col + P], xnT[:, k, :],
                              start=(k == 0), stop=(k == KT - 1))
                last.then_inc(bch_done, 1)
                if n % 2 == 0:
                    if n // 2 >= 1:
                        turn_probs(n // 2 - 1)
                    if n // 2 < NCH:
                        scores(n // 2)
                elif n >= 3:
                    attend((n - 3) // 2)
                else:
                    turn_keys()
            pe.wait_ge(u_ready, CT)
            pe.wait_ge(probsT_ready, NCH)
            for s, at in enumerate((SEQ, UW - (CW - 1))):
                for j in range(CT):
                    last = nc.tensor.transpose(ps[0:CW - 1, s, j * P:(j + 1) * P], uT[:, j, at:at + CW - 1],
                                               ident[:, :])
            last.then_inc(u_turned, 1)

            pe.wait_ge(wo_in, 48)

            def project_out(t, halves=(0, 1), tiles=range(MIX)):
                t0, n = TT[t]
                if t == 0:
                    pe.wait_ge(att_mixed, NCH)
                    pe.wait_ge(conv_mixed, CT)
                for half in halves:
                    for j in tiles:
                        last = mm(ps[0:n, OUT_BANK[t][half], :], mixT[:, j, t0:t0 + n],
                                  w_o[:, j, half * HALF:(half + 1) * HALF], start=(j == 0), stop=(j == MIX - 1))
                    if j == MIX - 1:
                        last.then_inc(out_done, 1)

            def logits(t):
                _, n = TT[t]
                pe.wait_ge(hn_ready, t + 1)
                if t == 0:
                    pe.wait_ge(u_out_ready, 2)
                    pe.wait_ge(router_in, 48)
                else:
                    pe.wait_ge(hnT_ready, t)
                if t == NT - 1:
                    pe.wait_ge(sel_ready, 1)
                for k in range(KT):
                    last = nc.tensor.transpose(turned_h(t)[:, k, :], hn[0:n, t, k * P:(k + 1) * P], ident[0:n, 0:n])
                last.then_inc(hn_turned, 1)
                pe.wait_ge(hnT_ready, t + 1)
                for k in range(KT):
                    last = mm(LG[0:n, t, :], hnT[:, k, 0:n], w_rt[:, k, :], start=(k == 0), stop=(k == KT - 1))
                last.then_inc(logits_done, 1)

            def ranks(out, counted, t0, nt):
                mm(out[:, :, :], ones[:, :], sel_sum[:, t0:t0 + counted, :], start=True, stop=False,
                   skip_group_check=True)
                mm(out[:, 0:nt, :], before[:, :], sel[:, t0:t0 + nt, :], start=False, stop=True,
                   skip_group_check=True).then_inc(ranked, 1)

            def gather_first(tiles):
                for k in range(KT):
                    for t in tiles:
                        m = TT[t][1]
                        last = mm(XE[:, k, :], hn[0:m, t, k * P:(k + 1) * P], oh[0:m, t, :, 0, :],
                                  start=(t == 0 and k % (KT // 2) == 0), stop=(t == NT - 1),
                                  skip_group_check=True)
                return last

            project_out(0)
            project_out(1)
            logits(0)
            project_out(2, (0,))
            logits(1)
            project_out(2, (1,), range(MIX // 2))
            pe.wait_ge(sel_ready, 2)
            ranks(RK, 2, 0, 2)
            project_out(2, (1,), range(MIX // 2, MIX))
            pe.wait_ge(hnT_ready, 2)
            pe.wait_ge(first_marked, 1)
            gather_first((0, 1))
            logits(2)
            pe.wait_ge(sel_ready, NT)
            ranks(RK_LAST, 2, 2, 1)

            def gather(i, tiles=range(KT)):
                if 0 in tiles:
                    pe.wait_ge(oh_ready, i + 1)
                for k in tiles:
                    for t, (_, m) in enumerate(TT):
                        last = mm(XE[:, k, :], hn[0:m, t, k * P:(k + 1) * P], oh[0:m, t, :, 0, :],
                                  start=(t == 0), stop=(t == NT - 1))
                if KT - 1 in tiles:
                    last.then_inc(gathered, 1)

            def gate_up(chunks, s, between=None):
                for k, ch in enumerate(chunks):
                    pe.wait_ge(split_done, ch.nth + 1)
                    for w in (w_hi, w_lo):
                        for n in range(FLAT // 512):
                            last = mm(GU[:, n, :], xhl[:, s, k, :], w[:, ch.split, n * 512:(n + 1) * 512],
                                      start=(k == 0 and w is w_hi), stop=(k == KT - 1 and w is w_lo),
                                      skip_group_check=True)
                    last.then_inc(chunk_used, 1)
                    if between:
                        between(k)

            def down(n, chunks, between=None, he=he, out=Y):
                pe.wait_ge(he_ready, n + 1)
                for m, ch in enumerate(chunks):
                    pe.wait_ge(split_done, ch.nth + 1)
                    for a in range(FPC):
                        for half in range(2):
                            cols = slice(half * HALF, (half + 1) * HALF)
                            w_cols = slice(a * D + half * HALF, a * D + (half + 1) * HALF)
                            for w in (w_hi, w_lo):
                                last = mm(out[:, cols], he[:, FPC * m + a, :], w[:, ch.split, w_cols],
                                          start=(m == 0 and a == 0 and w is w_hi),
                                          stop=(m == DNC - 1 and a == FPC - 1 and w is w_lo),
                                          skip_group_check=True)
                    last.then_inc(chunk_used, 1)
                    if between:
                        between(m)

            def fold_gu(n, tiles=range(2 * FT)):
                if 0 in tiles:
                    pe.wait_ge(gu_copied, n + 1)
                for f in tiles:
                    last = mm(TU[:, f // FT, f % FT, :], gu_sb[:, f * P:(f + 1) * P], fold[:, :],
                              start=True, stop=True)
                if 2 * FT - 1 in tiles:
                    last.then_inc(folded, 1)

            def turn_oh(i, experts=(0, 1)):
                pe.wait_ge(oh_ready, i + 1)
                for s in experts:
                    for t in range(NT):
                        nc.tensor.transpose(OT[:, s, t * P:(t + 1) * P],
                                            oh[:, t, s, :, :].rearrange("p a c -> p (a c)"), ident[:, :])
                    for t in range(NT):
                        last = mm(OT[:, s, NT * P:NT * P + 1], oh[:, t, s, :, :].rearrange("p a c -> p (a c)"),
                                  gate_col[:, t, s:s + 1], start=(t == 0), stop=(t == NT - 1))
                last.then_inc(oh_turned, 1)

            def scatter(i, u, experts=(0, 1), last_pair=False):
                t, half = u // 2, u % 2
                if u == 0:
                    pe.wait_ge(ohT_ready, i + 1)
                if u >= 2 and not last_pair:
                    pe.wait_ge(added, 2 * NT * i + u - 1)
                for s in experts:
                    for y in (y_hi, y_lo):
                        last = mm(ps[:, LAST_BANK[u] if last_pair else 6 + half, :],
                                  ohT[:, s, t * P:(t + 1) * P], y[:, s, half * HALF:(half + 1) * HALF],
                                  start=(s == 0 and y is y_hi),
                                  stop=(s == (1 if last_pair else experts[-1]) and y is y_lo),
                                  skip_group_check=last_pair)
                if not last_pair or 1 in experts:
                    last.then_inc(scattered, 1)

            def chunks_of(e, which):
                return [Chunk(e, c) for c in which]

            def spread_b_down(k):
                u = k - 1
                if u == 0:
                    pe.wait_ge(gatesT_ready, 1)
                    pe.wait_ge(b_down_in, 16)
                if 0 <= u < 2 * NT:
                    t, half = u // 2, u % 2
                    t0, m = t * P, TT[t][1]
                    if u >= 2:
                        pe.wait_ge(b_added, u - 1)
                    mm(ps[0:m, 6 + half, :], gatesT[:, t0:t0 + m], b_dn[:, half * HALF:(half + 1) * HALF],
                       start=True, stop=True).then_inc(b_spread, 1)

            def even(i, e, step):
                def fold_last(k):
                    if k == 0:
                        pe.wait_ge(ohT_ready, i)
                    if k < 4:
                        fold_gu(e - 1, range(4 * k, 4 * k + 4))

                def fold_this(m):
                    if m == 1:
                        pe.wait_ge(u_biased, e)
                        fold_gu(e, range(FT))
                    if m == 2:
                        fold_gu(e, range(FT, 2 * FT))

                first = isinstance(i, int) and i == 0
                if not first:
                    pe.wait_ge(gu_copied, e)
                pe.wait_ge(xl_ready, i + 1)
                gate_up(chunks_of(step, range(GUC)), 0, None if first else fold_last)
                if not first:
                    pe.wait_ge(yl_ready, e - 1)
                    down(e - 1, chunks_of(step, range(GUC, CH)), fold_this)

            def odd(i, e, step, last=False):
                def scatter_and_turn(k):
                    if not isinstance(i, int) or i > 0:
                        if k == 1:
                            pe.wait_ge(yl_ready, e - 1)
                        if 1 <= k <= 2 * NT:
                            scatter(i - 1, k - 1)
                    else:
                        spread_b_down(k)
                    if k == GUC - 1:
                        pe.wait_ge(u_biased, e)
                        turn_oh(i)

                def gather_next(m):
                    if last:
                        if m == 1:
                            pe.wait_ge(gu_copied, e + 1)
                            pe.wait_ge(ohT_ready, i + 1)
                            fold_gu(e)
                        return
                    if m == 1:
                        pe.wait_ge(gu_copied, e + 1)
                        gather(i + 1, range(KT // 2))
                    if m == 2:
                        gather(i + 1, range(KT // 2, KT))

                pe.wait_ge(gu_copied, e)
                gate_up(chunks_of(step, range(GUC)), 1, scatter_and_turn)
                if not isinstance(i, int) or i > 0:
                    pe.wait_ge(added, 2 * NT * i)
                else:
                    pe.wait_ge(b_added, 2 * NT)
                down(e - 1, chunks_of(step, range(GUC, CH)), gather_next)

            pe.wait_ge(oh_ready, 1)
            gather_first((NT - 1,)).then_inc(gathered, 1)
            pe.wait_ge(rank_ready, 1)
            for t in range(NT):
                last = nc.tensor.transpose(ps[0:NE, 7, t * P:(t + 1) * P], gates[:, t, :], ident[:, :])
            last.then_inc(gates_turned, 1)
            even(0, 0, 0)
            fold_gu(0)
            odd(0, 1, 1)
            with pe.Fori(1, PAIRS - 1) as i:
                even(i, 2 * i, (i, 0))
                odd(i, 2 * i + 1, (i, 1))
            even(PAIRS - 1, NE - 2, NE - 2)
            odd(PAIRS - 1, NE - 1, NE - 1, last=True)
            down(NE - 1, chunks_of(NE, range(GUC, CH)), he=he_last, out=Y_LAST)
            pe.wait_ge(yl_ready, NE - 1)
            pe.wait_ge(u_biased, NE)
            for u in range(2 * NT):
                scatter(PAIRS - 1, u, (0,), last_pair=True)
            pe.wait_ge(yl_ready, NE)
            for u in range(2 * NT):
                scatter(PAIRS - 1, u, (1,), last_pair=True)

            def again(n, e):
                i = n - NE + PAIRS
                pe.wait_ge(added, 2 * NT * i)
                gather(i)
                turn_oh(i, (0,))
                pe.wait_ge(xl_ready, i + 1)
                gate_up([LateChunk(n, e, c) for c in range(GUC)], 0)
                pe.wait_ge(ohT_ready, i + 1)
                fold_gu(n)
                down(n, [LateChunk(n, e, c) for c in range(GUC, CH)])
                pe.wait_ge(yl_ready, n + 1)
                for u in range(2 * NT):
                    scatter(i, u, (0,))

            further_rounds(pe, again)

        @block.scalar
        def _(act):
            A = nc.scalar.activation
            rows = vec_rows
            act.dma_start(rows[V_G1:V_G1 + KT, :], norm1_g.rearrange("l (k p) -> (l k) p", p=P)).then_inc(vec_in, 16)
            act.dma_start(rows[V_CONV:V_CONV + CW * CT, :],
                           conv_w.rearrange("l w (c p) -> (l w c) p", p=P)).then_inc(vec_in, 16)
            for g in range(2):
                half = slice(g * HEAD_DIM, (g + 1) * HEAD_DIM)
                act.dma_start(rows[V_QG:V_QG + 1, half], q_norm_g).then_inc(vec_in, 16)
                act.dma_start(rows[V_KG:V_KG + 1, half], k_norm_g).then_inc(vec_in, 16)
            act.dma_start(rows[V_STATE:NV, :],
                           state_conv.rearrange("l b r (c p) -> (l b r c) p", p=P)).then_inc(vec_in, 16)
            act.dma_start(ck_nat[:, :], cache_k[0, 0].rearrange("t h d -> t (h d)")).then_inc(ck_in, 16)
            act.dma_start(cv_nat[:, :], cache_v[0, 0].rearrange("t h d -> t (h d)")).then_inc(cv_in, 16)
            act.dma_start(sink_row[:, :], sinks.to_broadcast([P, NH])).then_inc(sink_in, 16)
            act.wait_ge(eps_set, 1)
            for t, (_, n) in enumerate(TT):
                act.wait_ge(x_in[t // 2], 16)
                if t:
                    act.wait_ge(x_sumsq, t)
                A(junk[0:n, :], x[0:n, t, :], ACT.Square, accum_out=st[0:n, 0, t:t + 1]).then_inc(x_sumsq, 1)
                act.wait_ge(x_sumsq, t + 1)
                A(st[0:n, 1, t:t + 1], st[0:n, 0, t:t + 1], ACT.Sqrt, bias=eps[0:n, :], scale=1.0 / D
                  ).then_inc(x_std, 1)

            def square_head(i):
                act.wait_ge(qk_done, i + 1)
                A(qk_sq[:, i, :], ps[:, QK_BANK[i], 0:TOK], ACT.Square).then_inc(qk_squared, 1)

            def root_head(i):
                act.wait_ge(head_ss, i + 1)
                A(qk_sq[:, i, :], ps[:, SS_BANK[i % 2], 0:TOK], ACT.Sqrt, bias=eps[:, :], scale=1.0 / HEAD_DIM
                  ).then_inc(head_std, 1)

            for i in range(1 + QT):
                square_head(i)
                if i == 0:
                    act.wait_ge(bias_turned, 1)
                    nc.scalar.copy(b_guT[:, :, :].rearrange("p f e -> p (f e)"), ps[:, 6, :]).then_inc(bias_ready, 1)
                if i:
                    root_head(i - 1)
            act.wait_ge(v_done, 1)
            nc.scalar.copy(v_nat[:, 0:2, :].rearrange("p t n -> p (t n)"), ps[:, V_BANK, 0:2 * P]).then_inc(v_ready, 1)
            nc.scalar.copy(v_nat[0:DEC, 2, :], ps[0:DEC, V_BANK, 2 * P:3 * P]).then_inc(v_ready, 1)
            root_head(QT)

            def exps(c):
                off, n = key_window(c)
                act.wait_ge(smx_neg, 2 * (c + 1))
                for b in range(4):
                    A(probs[:, b, off:off + n], SC[:, b, off:off + n], ACT.Exp, bias=smx[:, 2, b:b + 1],
                      scale=HEAD_DIM ** -0.5, accum_out=smx[:, 4, b:b + 1]).then_inc(exp_done, 1)
                A(smx[:, 5, :], smx[:, 3, :], ACT.Exp).then_inc(exp_done, 1)

            def copy_probsT(c):
                off, n = key_window(c)
                act.wait_ge(probs_turned, c + 1)
                if c >= 1:
                    act.wait_ge(att_done, c)
                lo = min(P, off + n)
                last = nc.scalar.copy(probsT[0:lo, 0, :], PT[0:lo, 0, :])
                if off + n > P:
                    last = nc.scalar.copy(probsT[0:off + n - P, 1, :], PT[0:off + n - P, 1, :])
                last.then_inc(probsT_ready, 1)

            for n in range(3 * CT):
                if n % 3 == 0:
                    act.wait_ge(bch_done, n + 1)
                    if n:
                        act.wait_ge(u_ready, n // 3)
                    nc.scalar.copy(c_sb[:, :], ps[:, BCH_BANK[0], 0:TOK]).then_inc(c_copied, 1)
                if n % 2 == 0:
                    if n // 2 >= 1:
                        copy_probsT(n // 2 - 1)
                    if n // 2 < NCH:
                        exps(n // 2)
                elif n == 1:
                    act.wait_ge(k_turned, 1)
                    nc.scalar.copy(k_out[:, 0, :], KO[:, 0, :]).then_inc(k_out_ready, 1)
                    nc.scalar.copy(k_out[0:DEC, 1, :], KO[0:DEC, 1, :]).then_inc(k_out_ready, 1)
            act.wait_ge(u_turned, 1)
            for s in range(2):
                nc.scalar.copy(u_out[:, s, :], ps[0:CW - 1, s, :]).then_inc(u_out_ready, 1)

            def rms_h(t):
                _, n = TT[t]
                act.wait_ge(h_ready, 2 * (t + 1))
                if t:
                    act.wait_ge(h_sumsq, t)
                A(junk_h[0:n, :], x[0:n, t, :], ACT.Square, accum_out=st[0:n, 0, t:t + 1]).then_inc(h_sumsq, 1)
                act.wait_ge(h_sumsq, t + 1)
                A(st[0:n, 1, t:t + 1], st[0:n, 0, t:t + 1], ACT.Sqrt, bias=eps[0:n, :], scale=1.0 / D
                  ).then_inc(h_std, 1)

            def split_hi(ch):
                act.wait_ge(raw_in[ch.raw], 16 * ch.arrivals)
                if ch.resplit:
                    act.wait_ge(chunk_used, ch.free_split)
                nc.scalar.copy(w_hi[:, ch.split, :], slot(raw, ch.raw)).then_inc(hi_done, 1)

            def copy_hnT(t):
                _, n = TT[t]
                act.wait_ge(hn_turned, t + 1)
                if t:
                    act.wait_ge(logits_done, t)
                nc.scalar.copy(hnT[:, :, 0:n], turned_h(t)).then_inc(hnT_ready, 1)

            rms_h(0)
            rms_h(1)
            copy_hnT(0)
            act.wait_ge(kv_stored, 8 * 16)
            act.wait_ge(conv_mixed, CT)
            act.wait_ge(att_mixed, NCH)
            for c in range(EARLY):
                split_hi(Chunk(0, c))
            copy_hnT(1)
            rms_h(2)
            copy_hnT(2)
            act.wait_ge(top_ready, NT)
            for t in range(NT):
                A(gates[:, t, :], lg[:, t, :], ACT.Exp, bias=neg_top[:, t:t + 1]).then_inc(gexp_done, 1)

            def split_xh(i, experts=(0, 1)):
                act.wait_ge(gathered, i + 1)
                for s in experts:
                    last = nc.scalar.copy(xhl[:, s, :, 0:CAP], XE[:, :, s * CAP:(s + 1) * CAP])
                last.then_inc(xh_ready, 1)

            def copy_gu(n, last_chunk):
                act.wait_ge(chunk_used, last_chunk.nth + 1)
                nc.scalar.copy(gu_sb[:, :], GU.rearrange("p a n -> p (a n)")).then_inc(gu_copied, 1)

            def sigmoid(n, ge=ge, sg=sg):
                act.wait_ge(g_ready, n + 1)
                A(sg[:, :, :], ge[:, :, :], ACT.Sigmoid, scale=ALPHA).then_inc(sig_ready, 1)

            def split_hh(n, he=he):
                act.wait_ge(hidden_ready, n + 1)
                nc.scalar.copy(he[:, :, 0:CAP], ue[:, :, :]).then_inc(hh_ready, 1)

            def copy_ohT(i, experts=(0, 1)):
                act.wait_ge(oh_turned, i + 1)
                for s in experts:
                    nc.scalar.copy(ohT[:, s, :], OT[:, s, 0:NT * P])
                nc.scalar.copy(gate_row[:, 0:len(experts)], OT[:, 0:len(experts), NT * P]).then_inc(ohT_ready, 1)

            def split_yh(n, s, last_chunk, rows=Y):
                act.wait_ge(chunk_used, last_chunk.nth + 1)
                A(y_hi[:, s, :], rows, ACT.Copy, scale=gate_row[:, s:s + 1]).then_inc(yh_ready, 1)

            def step(e, at, par, nxt, i=None, last=False):
                first = isinstance(e, int) and e == 0
                for c in range(AHEAD[1 - par], CH if not first else GUC):
                    split_hi(Chunk(at, c))
                    if not first and c == (4 if par else 6):
                        sigmoid(e - 1)
                    if not first and c == (5 if par else 7):
                        split_hh(e - 1)
                    if c == 9:
                        copy_gu(e, Chunk(at, GUC - 1))
                        if par:
                            copy_ohT(i)
                for c in ahead(par, nxt):
                    split_hi(Chunk(nxt, c))
                    if par and c == 1:
                        split_xh(i + 1)
                    if last and c == GUC + 1:
                        sigmoid(e, ge_last, sg_last)
                    if last and c == GUC + 2:
                        split_hh(e, he_last)
                if first:
                    copy_gu(0, Chunk(at, GUC - 1))
                else:
                    split_yh(e - 1, 1 - par, Chunk(at, CH - 1))

            act.wait_ge(rank_ready, 1)
            split_hi(Chunk(0, EARLY))
            split_xh(0)
            act.wait_ge(gates_turned, 1)
            nc.scalar.copy(gatesT[:, :], ps[0:NE, 7, 0:NT * P]).then_inc(gatesT_ready, 1)
            step(0, 0, 0, 1)
            step(1, 1, 1, 2, i=0)
            with act.Fori(1, PAIRS - 1) as i:
                step(2 * i, (i, 0), 0, (i, 1))
                step(2 * i + 1, (i, 1), 1, (i + 1, 0), i=i)
            step(NE - 2, NE - 2, 0, NE - 1)
            step(NE - 1, NE - 1, 1, NE, i=PAIRS - 1, last=True)
            split_yh(NE - 1, 1, Chunk(NE, CH - 1), Y_LAST)

            def again(n, e):
                i = n - NE + PAIRS
                act.wait_ge(scattered, 2 * NT * i)
                split_xh(i, (0,))
                copy_ohT(i, (0,))
                for c in range(CH):
                    if c == GUC:
                        copy_gu(n, LateChunk(n, e, GUC - 1))
                        sigmoid(n)
                        split_hh(n)
                    split_hi(LateChunk(n, e, c))
                split_yh(n, 0, LateChunk(n, e, CH - 1))

            further_rounds(act, again)

        @block.vector
        def _(dve):
            V = nc.vector
            V.memset(eps[:, :], EPS).then_inc(eps_set, 1)
            dve.wait_ge(consts, 3)
            for g in range(2):
                half = slice(g * CAP, (g + 1) * CAP)
                V.tensor_copy(fold[half, :], ident[half, half]).then_inc(heads_set, 1)
            V.memset(head_ones[:, :], 0.0).then_inc(heads_set, 1)
            dve.wait_ge(heads_set, 3)
            for g in range(2):
                half = slice(g * HEAD_DIM, (g + 1) * HEAD_DIM)
                V.memset(head_ones[half, half], 1.0).then_inc(heads_set, 1)
            V.memset(lg[:, :, :], 0.0).then_inc(router_set, 1)
            V.memset(top4[:, :, :], NO_LOGIT).then_inc(router_set, 1)
            V.memset(uT[:, :, 0:CW - 1], 0.0).then_inc(conv_pad, 1)
            for t, (_, n) in enumerate(TT):
                dve.wait_ge(x_std, t + 1)
                V.reciprocal(st[0:n, 2, t:t + 1], st[0:n, 1, t:t + 1]).then_inc(x_rstd, 1)
                dve.wait_ge(x_rstd, t + 1)
                V.tensor_scalar(hn[0:n, t, :], x[0:n, t, :], st[0:n, 2, t:t + 1], None, ALU.mult
                                ).then_inc(x_scaled, 1)
            dve.wait_ge(vec_turned, 2)
            V.tensor_copy(vec[:, :], ps[:, B_VEC, 0:NV]).then_inc(vec_ready, 1)
            V.tensor_copy(ckT[:, :], ps[:, B_VEC, P:2 * P]).then_inc(vec_ready, 1)
            dve.wait_ge(vec_ready, 1)
            for t, (t0, n) in enumerate(TT):
                dve.wait_ge(x_turned, t + 1)
                per = KT // len(XT_BANK[t])
                for i, bank in enumerate(XT_BANK[t]):
                    g = vec[:, V_G1 + i * per:V_G1 + (i + 1) * per].unsqueeze(2).to_broadcast([P, per, n])
                    V.tensor_tensor(xnT[:, i * per:(i + 1) * per, t0:t0 + n],
                                    ps[:, bank, 0:per * n].rearrange("p (k t) -> p k t", t=n), g, ALU.mult
                                    ).then_inc(xnT_ready, 1)
            V.tensor_copy(uT[:, :, SEQ + CW - 1:SEQ + 2 * (CW - 1)],
                          vec[:, V_STATE:NV].rearrange("p (r c) -> p c r", r=CW - 1)).then_inc(conv_pad, 1)
            for i in range(1 + QT):
                dve.wait_ge(head_std, i + 1)
                V.reciprocal(qk_sq[:, i, :], qk_sq[:, i, :]).then_inc(head_rstd, 1)
                dve.wait_ge(head_rstd, i + 1)
                if i == 0:
                    V.scalar_tensor_tensor(out=kT[:, :], in0=ps[:, QK_BANK[i], 0:TOK], scalar=vec[:, V_KG:V_KG + 1],
                                           in1=qk_sq[:, i, :], op0=ALU.mult, op1=ALU.mult).then_inc(qk_ready, 1)
                    continue
                for a in range(2):
                    head = 2 * (i - 1) + a
                    g, j = head // (NH // NKV), head % (NH // NKV)
                    src = slice(a * HEAD_DIM, (a + 1) * HEAD_DIM)
                    by_chunk = lambda ap: ap.rearrange("p (c t) -> p c t", t=CHUNK)
                    last = V.scalar_tensor_tensor(
                        out=qT[g * HEAD_DIM:(g + 1) * HEAD_DIM, :, j, :], in0=by_chunk(ps[src, QK_BANK[i], 0:TOK]),
                        scalar=vec[src, V_QG:V_QG + 1], in1=by_chunk(qk_sq[src, i, :]), op0=ALU.mult, op1=ALU.mult)
                last.then_inc(qk_ready, 1)

            dve.wait_ge(sink_in, 16)
            for a in range(2):
                half = slice(a * CHUNK, (a + 1) * CHUNK)
                V.tensor_copy(sink[half, :], sink_row[half, :].rearrange("p (b a) -> p a b", a=2)[:, a, :]
                              ).then_inc(sink_set, 1)

            def softmax(c):
                off, n = key_window(c)
                S = 4 * c
                dve.wait_ge(scores_done, c + 1)
                if c == 0:
                    dve.wait_ge(sink_set, 2)
                V.tensor_reduce(smx[:, 0, :], SC[:, :, off:off + n], AX.X, ALU.max).then_inc(smx_step, 1)
                dve.wait_ge(smx_step, S + 1)
                V.scalar_tensor_tensor(out=smx[:, 1, :], in0=smx[:, 0, :], scalar=HEAD_DIM ** -0.5, in1=sink[:, :],
                                       op0=ALU.mult, op1=ALU.max).then_inc(smx_step, 1)
                dve.wait_ge(smx_step, S + 2)
                V.tensor_scalar(smx[:, 2, :], smx[:, 1, :], -1.0, None, ALU.mult).then_inc(smx_neg, 1)
                V.tensor_tensor(smx[:, 3, :], sink[:, :], smx[:, 1, :], ALU.subtract).then_inc(smx_neg, 1)
                dve.wait_ge(exp_done, 5 * (c + 1))
                V.tensor_tensor(smx[:, 6, :], smx[:, 4, :], smx[:, 5, :], ALU.add).then_inc(smx_step, 1)
                dve.wait_ge(smx_step, S + 3)
                V.reciprocal(smx[:, 7, :], smx[:, 6, :]).then_inc(smx_step, 1)
                dve.wait_ge(smx_step, S + 4)
                V.tensor_tensor(probs[:, :, off:off + n], probs[:, :, off:off + n],
                                smx[:, 7, :].unsqueeze(2).to_broadcast([P, 4, n]), ALU.mult).then_inc(probs_ready, 1)

            def convolve(j):
                dve.wait_ge(c_copied, j + 1)
                dve.wait_ge(bch_done, 3 * j + 2)
                hc = ps[:, BCH_BANK[1], 0:TOK]
                V.tensor_tensor(uT[:, j, CW - 1:CW - 1 + SEQ], c_sb[:, 0:SEQ], hc[:, 0:SEQ], ALU.mult
                                ).then_inc(cv_step, 1)
                V.tensor_tensor(uT[:, j, UW - DEC:UW], c_sb[:, SEQ:TOK], hc[:, SEQ:TOK], ALU.mult
                                ).then_inc(u_ready, 1)
                dve.wait_ge(cv_step, 3 * j + 1)
                dve.wait_ge(u_ready, j + 1)
                if j == 0:
                    dve.wait_ge(conv_pad, 2)
                else:
                    dve.wait_ge(conv_mixed, j)
                W = UW - (CW - 1)
                tap = lambda w: vec[:, V_CONV + w * CT + j:V_CONV + w * CT + j + 1]
                V.tensor_scalar(cv[:, :], uT[:, j, 0:W], tap(0), None, ALU.mult).then_inc(cv_step, 1)
                dve.wait_ge(cv_step, 3 * j + 2)
                V.scalar_tensor_tensor(out=cv[:, :], in0=uT[:, j, 1:1 + W], scalar=tap(1), in1=cv[:, :],
                                       op0=ALU.mult, op1=ALU.add).then_inc(cv_step, 1)
                dve.wait_ge(cv_step, 3 * j + 3)
                V.scalar_tensor_tensor(out=cv[:, :], in0=uT[:, j, 2:2 + W], scalar=tap(2), in1=cv[:, :],
                                       op0=ALU.mult, op1=ALU.add).then_inc(rows_moved, 1)

            def gate_conv(j):
                dve.wait_ge(bch_done, 3 * j + 3)
                dve.wait_ge(rows_moved, j + 1)
                B = ps[:, BCH_BANK[2], 0:TOK]
                V.tensor_tensor(mixT[:, QT + j, 0:SEQ], B[:, 0:SEQ], cv[:, 0:SEQ], ALU.mult)
                V.tensor_tensor(mixT[:, QT + j, SEQ:TOK], B[:, SEQ:TOK], cv[:, SEQ + CW - 1:], ALU.mult
                                ).then_inc(conv_mixed, 1)

            for n in range(3 * CT):
                if n % 3 == 1:
                    convolve(n // 3)
                if n % 3 == 2:
                    gate_conv(n // 3)
                if n % 2 == 0 and n // 2 < NCH:
                    softmax(n // 2)
                if n % 2 == 1 and n >= 3:
                    c = (n - 3) // 2
                    dve.wait_ge(att_done, c + 1)
                    V.tensor_copy(mixT[:, 0:QT, c * CHUNK:(c + 1) * CHUNK],
                                  AO.rearrange("p (j t) -> p j t", t=CHUNK)).then_inc(att_mixed, 1)

            def norm_h(t):
                _, n = TT[t]
                for half in range(2):
                    cols = slice(half * HALF, (half + 1) * HALF)
                    dve.wait_ge(out_done, 2 * t + half + 1)
                    V.tensor_tensor(x[0:n, t, cols], ps[0:n, OUT_BANK[t][half], :], x[0:n, t, cols], ALU.add
                                    ).then_inc(h_ready, 1)
                dve.wait_ge(h_std, t + 1)
                V.reciprocal(st[0:n, 2, t:t + 1], st[0:n, 1, t:t + 1]).then_inc(h_rstd, 1)
                dve.wait_ge(h_rstd, t + 1)
                V.scalar_tensor_tensor(out=hn[0:n, t, :], in0=x[0:n, t, :], scalar=st[0:n, 2, t:t + 1],
                                       in1=g2[0:n, :], op0=ALU.mult, op1=ALU.mult).then_inc(hn_ready, 1)

            n_route = [0]

            def then(ins):
                n_route[0] += 1
                ins.then_inc(route, 1)
                dve.wait_ge(route, n_route[0])

            def choose(t):
                _, n = TT[t]
                dve.wait_ge(logits_done, t + 1)
                then(V.tensor_tensor(lg[0:n, t, :], LG[0:n, t, :], b_rt[0:n, :], ALU.add))
                then(V.max(top8[:, t, :], lg[:, t, :]))
                then(V.tensor_copy(top4[:, t, 0:TOP_K], top8[:, t, 0:TOP_K]))
                V.tensor_scalar(neg_top[:, t:t + 1], top8[:, t, 0:1], -1.0, None, ALU.mult).then_inc(top_ready, 1)
                then(V.match_replace(left[:, t, :], top4[:, t, :], lg[:, t, :], -NO_LOGIT))
                then(V.tensor_tensor(sel[:, t, :], left[:, t, :], lg[:, t, :], ALU.not_equal))
                if n < P:
                    then(V.memset(sel[n:P, t, :], 0.0))
                V.tensor_tensor(sel_sum[:, t + 1, :], sel_sum[:, t, :], sel[:, t, :], ALU.add).then_inc(sel_ready, 1)
                dve.wait_ge(sel_ready, t + 1)

            def split_lo(ch):
                dve.wait_ge(hi_done, ch.nth + 1)
                V.tensor_tensor(w_lo[:, ch.split, :], slot(raw, ch.raw), w_hi[:, ch.split, :], ALU.subtract
                                ).then_inc(split_done, 1)

            def mark_rows(i, e, experts=(0, 1)):
                for s in experts:
                    V.tensor_tensor(oh[:, :, s, :, :], row_ids[:, :].unsqueeze(1).unsqueeze(1).to_broadcast([P, NT, 2, CAP]),
                                    rank[:, :, bass.ds(e + s, 1)].unsqueeze(3).to_broadcast([P, NT, 2, CAP]),
                                    ALU.is_equal)
                V.tensor_copy(gate_col[:, :, 0:len(experts)], gates[:, :, bass.ds(e, len(experts))]).then_inc(oh_ready, 1)

            def rank_tiles(tiles, told):
                dve.wait_ge(ranked, told)
                src = RK[:, :, :] if told == 1 else RK_LAST[:, 0:1, :]
                then(V.scalar_tensor_tensor(out=rank[:, tiles, :], in0=src, scalar=1.0, in1=sel[:, tiles, :],
                                            op0=ALU.add, op1=ALU.mult))
                then(V.tensor_scalar(rank[:, tiles, :], rank[:, tiles, :], -1.0, None, ALU.add))
                n = tiles.stop - tiles.start
                for s in range(2):
                    last = V.tensor_tensor(oh[:, tiles, s, :, :],
                                           row_ids[:, :].unsqueeze(1).unsqueeze(1).to_broadcast([P, n, 2, CAP]),
                                           rank[:, tiles, s:s + 1].unsqueeze(3).to_broadcast([P, n, 2, CAP]),
                                           ALU.is_equal)
                return last

            dve.wait_ge(router_set, 2)
            dve.wait_ge(router_in, 48)
            norm_h(0)
            norm_h(1)
            then(V.memset(sel_sum[:, 0, :], 0.0))
            for c in range(EARLY):
                split_lo(Chunk(0, c))
            choose(0)
            choose(1)
            rank_tiles(slice(0, 2), 1).then_inc(first_marked, 1)
            norm_h(2)
            choose(2)
            dve.wait_ge(gexp_done, NT)
            then(V.tensor_tensor(gates[:, :, :], gates[:, :, :], sel[:, :, :], ALU.mult))
            then(V.tensor_reduce(gsum[:, :], gates[:, :, :], AX.X, ALU.add))
            then(V.memset(gsum[DEC:P, 2:3], 1.0))
            then(V.reciprocal(gsum[:, :], gsum[:, :]))
            then(V.tensor_tensor(gates[:, :, :], gates[:, :, :],
                                 gsum[:, :].unsqueeze(2).to_broadcast([P, NT, NE]), ALU.mult))
            rank_tiles(slice(2, NT), 2)
            V.tensor_copy(gate_col[:, :, :], gates[:, :, 0:2]).then_inc(oh_ready, 1)
            V.tensor_copy(counts[:, :], RK_LAST[:, 1, :]).then_inc(counts_ready, 1)
            then(V.tensor_reduce(most[:, :], RK_LAST[:, 1, :], AX.X, ALU.max))
            V.tensor_copy(most_i[:, :], most[:, :]).then_inc(counts_ready, 1)
            dve.wait_ge(counts_ready, 2)
            V.memset(smx[:, 0, 0:1], 0.0).then_inc(rank_ready, 1)

            def split_xl(i, experts=(0, 1)):
                dve.wait_ge(xh_ready, i + 1)
                for s in experts:
                    last = V.tensor_tensor(xhl[:, s, :, CAP:], XE[:, :, s * CAP:(s + 1) * CAP], xhl[:, s, :, 0:CAP],
                                           ALU.subtract)
                last.then_inc(xl_ready, 1)

            def gate_and_up(n, e, ge=ge):
                bias = lambda f0: b_guT[:, f0:f0 + FT, bass.ds(e, 1)].to_broadcast([P, FT, CAP])
                dve.wait_ge(folded, n + 1)
                V.tensor_tensor(ge[:, :, :], TU[:, 0], bias(0), ALU.add).then_inc(g_biased, 1)
                V.tensor_tensor(ue[:, :, :], TU[:, 1], bias(FT), ALU.add).then_inc(u_biased, 1)
                dve.wait_ge(g_biased, n + 1)
                V.tensor_scalar(ge[:, :, :], ge[:, :, :], LIMIT, None, ALU.min).then_inc(g_ready, 1)
                dve.wait_ge(u_biased, n + 1)
                V.tensor_scalar(ue[:, :, :], ue[:, :, :], LIMIT, -LIMIT, ALU.min, ALU.max).then_inc(u_clipped, 1)

            def hidden(n, ge=ge, sg=sg):
                dve.wait_ge(sig_ready, n + 1)
                V.tensor_tensor(ge[:, :, :], ge[:, :, :], sg[:, :, :], ALU.mult).then_inc(gs_ready, 1)
                dve.wait_ge(u_clipped, n + 1)
                dve.wait_ge(gs_ready, n + 1)
                V.scalar_tensor_tensor(out=ue[:, :, :], in0=ue[:, :, :], scalar=1.0, in1=ge[:, :, :],
                                       op0=ALU.add, op1=ALU.mult).then_inc(hidden_ready, 1)

            def split_hl(n, he=he):
                dve.wait_ge(hh_ready, n + 1)
                V.tensor_tensor(he[:, :, CAP:], ue[:, :, :], he[:, :, 0:CAP], ALU.subtract).then_inc(he_ready, 1)

            def split_yl(n, s, rows=Y):
                dve.wait_ge(yh_ready, n + 1)
                V.scalar_tensor_tensor(out=y_lo[:, s, :], in0=rows, scalar=gate_row[:, s:s + 1], in1=y_hi[:, s, :],
                                       op0=ALU.mult, op1=ALU.subtract).then_inc(yl_ready, 1)

            def add_rows(done, told, base, units=range(2 * NT), banks=(6, 7) * NT):
                for u in units:
                    t, half = u // 2, u % 2
                    _, m = TT[t]
                    cols = slice(half * HALF, (half + 1) * HALF)
                    dve.wait_ge(done, base + u + 1)
                    V.tensor_tensor(x[0:m, t, cols], ps[0:m, banks[u], :], x[0:m, t, cols], ALU.add
                                    ).then_inc(told, 1)

            def step(e, at, par, nxt, i=None, last=False):
                first = isinstance(e, int) and e == 0
                adds = par and not (isinstance(e, int) and e == 1)
                for c in range(AHEAD[1 - par], CH if not first else GUC):
                    split_lo(Chunk(at, c))
                    if adds and c - 3 in range(2 * NT):
                        add_rows(scattered, added, 2 * NT * (i - 1), [c - 3])
                    if par and not adds and c - 3 in range(2 * NT):
                        add_rows(b_spread, b_added, 0, [c - 3])
                    if not first and c == (3 if par else 5):
                        gate_and_up(e - 1, e - 1)
                    if not first and c == (4 if par else 6):
                        hidden(e - 1)
                    if not first and c == (5 if par else 7):
                        split_hl(e - 1)
                    if par and not last and c == 9:
                        dve.wait_ge(oh_turned, i + 1)
                        mark_rows(i + 1, 2 * i + 2)
                for c in ahead(par, nxt):
                    split_lo(Chunk(nxt, c))
                    if par and c == 1:
                        split_xl(i + 1)
                    if last and c == GUC:
                        gate_and_up(e, e, ge_last)
                    if last and c == GUC + 1:
                        hidden(e, ge_last, sg_last)
                    if last and c == GUC + 2:
                        split_hl(e, he_last)
                if not first:
                    split_yl(e - 1, 1 - par)

            split_lo(Chunk(0, EARLY))
            split_xl(0)
            step(0, 0, 0, 1)
            step(1, 1, 1, 2, i=0)
            with dve.Fori(1, PAIRS - 1) as i:
                step(2 * i, (i, 0), 0, (i, 1))
                step(2 * i + 1, (i, 1), 1, (i + 1, 0), i=i)
            step(NE - 2, NE - 2, 0, NE - 1)
            step(NE - 1, NE - 1, 1, NE, i=PAIRS - 1, last=True)
            split_yl(NE - 1, 1, Y_LAST)
            add_rows(scattered, added, 2 * NT * (PAIRS - 1), banks=LAST_BANK)

            def next_round(q):
                V.tensor_scalar(row_ids[:, :], row_ids[:, :], float(CAP), None, ALU.add).then_inc(round_set, 1)
                dve.wait_ge(round_set, q)
                V.memset(smx[:, 0, 2:3], 0.0)

            def again(n, e):
                i = n - NE + PAIRS
                dve.wait_ge(added, 2 * NT * i)
                mark_rows(i, e, (0,))
                split_xl(i, (0,))
                for c in range(CH):
                    if c == GUC:
                        gate_and_up(n, e)
                        hidden(n)
                        split_hl(n)
                    split_lo(LateChunk(n, e, c))
                split_yl(n, 0)
                add_rows(scattered, added, 2 * NT * i)

            further_rounds(dve, again, next_round, at_start=lambda: dve.wait_ge(y_stored, 16 * NT),
                           at_end=lambda: V.memset(smx[:, 0, 1:2], 0.0).then_inc(y_ready, 2 * NT))


_INS = ['x_prompt', 'x_sample', 'cache_k', 'cache_v', 'state_conv', 'norm1_g', 'w_in', 'q_norm_g', 'k_norm_g',
        'sinks', 'conv_w', 'w_out', 'norm2_g', 'w_router', 'b_router', 'w_gu', 'b_gu', 'w_down', 'b_down']
_OUTS = [(1, 256, 1024), (1, 64, 1024), (1, 1, 128, 2, 64), (1, 1, 128, 2, 64), (1, 1, 2, 512),
         (1, 1, 128, 2, 64), (1, 1, 128, 2, 64), (1, 1, 2, 512)]


def kernel(**inputs):
    import numpy as _np
    import concourse.bacc as _bacc
    from concourse import mybir as _mybir
    from concourse.bass_utils import run_bass_kernel_spmd as _run

    nc = _bacc.Bacc("TRN2", target_bir_lowering=False, num_devices=1)
    arrays, args = {}, []
    for name in _INS:
        a = _np.ascontiguousarray(inputs[name])
        arrays[f"in_{name}_dram"] = a
        args.append(nc.dram_tensor(f"in_{name}_dram", a.shape, _mybir.dt.from_np(a.dtype), kind="ExternalInput").ap())
    for i, shape in enumerate(_OUTS):
        dt = _mybir.dt.from_np(_np.dtype("float32"))
        args.append(nc.dram_tensor(f"out_{i}_dram", shape, dt, kind="ExternalOutput").ap())
    hybrid_layer_kernel(nc, *args)
    r = _run(nc, [arrays], core_ids=[0])
    return tuple(r.results[0][f"out_{i}_dram"] for i in range(len(_OUTS)))
```
